# Optimizing a Trainium2 kernel written in Bass

```python
import math
import jax, jax.numpy as jnp
from jax import lax
import numpy as np

D_MODEL = 2048
BATCH = 1
SEQ = 256
DEPTH = 1

ML_HEADS = 8
ML_QK_DIM = D_MODEL // 2 // ML_HEADS
ML_V_DIM = D_MODEL // ML_HEADS
ML_QK_WIDTH = ML_HEADS * ML_QK_DIM
ML_WIDTH = ML_HEADS * ML_V_DIM
GATE_SOFTCAP = 15.0
DN_HEADS = 16
DN_HEAD_DIM = D_MODEL // DN_HEADS
DN_WIDTH = DN_HEADS * DN_HEAD_DIM
CONV_WIDTH = 4
CHUNK = 64
NORM_EPS = 1e-6

IN_SIZES = (ML_QK_WIDTH, ML_QK_WIDTH, ML_WIDTH, ML_WIDTH, ML_WIDTH, ML_HEADS, ML_HEADS,
            3 * DN_WIDTH, DN_WIDTH, DN_HEADS, DN_HEADS,
            D_MODEL, D_MODEL)
IN_DIM = sum(IN_SIZES)
OUT_DIM = ML_WIDTH + DN_WIDTH


def _rmsnorm(x, w=None):
    xf = x.astype(jnp.float32)
    y = xf * lax.rsqrt(jnp.mean(xf * xf, axis=-1, keepdims=True) + NORM_EPS)
    return y if w is None else y * w.astype(jnp.float32)

def _l2norm(x):
    return x * lax.rsqrt(jnp.sum(x * x, axis=-1, keepdims=True) + NORM_EPS)

def _heads(t, n):
    b, s, _ = t.shape
    return t.reshape(b, s, n, -1).transpose(0, 2, 1, 3)

def _merge_heads(t):
    b, h, s, d = t.shape
    return t.transpose(0, 2, 1, 3).reshape(b, s, h * d)

def _chunks(t):
    b, h, s = t.shape[:3]
    t = t.reshape(b, h, s // CHUNK, CHUNK, *t.shape[3:])
    return jnp.moveaxis(t, 2, 0)

def _unchunk(t):
    nc, b, h, l, d = t.shape
    return jnp.moveaxis(t, 0, 2).reshape(b, h, nc * l, d)

def _softcap(t):
    return GATE_SOFTCAP * jnp.tanh(t / GATE_SOFTCAP)

def _mlstm_chunkwise(q, k, v, i_pre, logf):
    b_, h_, s_, dk = q.shape
    dv = v.shape[-1]
    q = q * (dk ** -0.5)
    qc, kc, vc = _chunks(q), _chunks(k), _chunks(v)
    ic, fc = _chunks(i_pre), _chunks(logf)
    bcum = jnp.cumsum(fc, axis=-1)
    causal = jnp.tril(jnp.ones((CHUNK, CHUNK), dtype=bool))
    dmat = bcum[..., :, None] - bcum[..., None, :] + ic[..., None, :]
    dmat = jnp.where(causal, dmat, -jnp.inf)
    dmax = jnp.max(dmat, axis=-1)
    scores = jnp.einsum('cbhtd,cbhsd->cbhts', qc, kc)
    w_end = bcum[..., -1:] - bcum + ic
    w_end_max = jnp.max(w_end, axis=-1)

    def step(carry, inp):
        C, n, m = carry
        q_c, k_c, v_c, b_c, dm_c, dmax_c, sc_c, we_c, wem_c = inp
        inter_log = b_c + m[..., None]
        m_t = jnp.maximum(inter_log, dmax_c)
        inter_w = jnp.exp(inter_log - m_t)
        intra_w = jnp.exp(dm_c - m_t[..., None]) * sc_c
        num = (inter_w[..., None] * jnp.einsum('bhtd,bhde->bhte', q_c, C)
               + jnp.einsum('bhts,bhse->bhte', intra_w, v_c))
        den = inter_w * jnp.einsum('bhtd,bhd->bht', q_c, n) + jnp.sum(intra_w, axis=-1)
        h = num / jnp.maximum(jnp.abs(den), jnp.exp(-m_t))[..., None]
        m_new = jnp.maximum(b_c[..., -1] + m, wem_c)
        decay = jnp.exp(b_c[..., -1] + m - m_new)
        kw = k_c * jnp.exp(we_c - m_new[..., None])[..., None]
        C_new = decay[..., None, None] * C + jnp.einsum('bhsd,bhse->bhde', kw, v_c)
        n_new = decay[..., None] * n + jnp.sum(kw, axis=-2)
        return (C_new, n_new, m_new), h

    init = (jnp.zeros((b_, h_, dk, dv), jnp.float32),
            jnp.zeros((b_, h_, dk), jnp.float32),
            jnp.zeros((b_, h_), jnp.float32))
    _, hs = lax.scan(step, init, (qc, kc, vc, bcum, dmat, dmax, scores, w_end, w_end_max))
    return _unchunk(hs)

def _gated_delta_chunkwise(q, k, v, beta, g):
    b_, h_, s_, dk = q.shape
    dv = v.shape[-1]
    q = q * (dk ** -0.5)
    qc, kc, vc = _chunks(q), _chunks(k), _chunks(v)
    bc, gc = _chunks(beta), _chunks(g)
    gam = jnp.cumsum(gc, axis=-1)
    incl = jnp.tril(jnp.ones((CHUNK, CHUNK), dtype=bool))
    strict = jnp.tril(jnp.ones((CHUNK, CHUNK), dtype=bool), k=-1)
    rel = gam[..., :, None] - gam[..., None, :]
    decay_mat = jnp.where(incl, jnp.exp(jnp.where(incl, rel, 0.0)), 0.0)
    kk = jnp.einsum('cbhtd,cbhsd->cbhts', kc, kc)
    a_mat = jnp.where(strict, bc[..., :, None] * kk * decay_mat, 0.0)
    lhs = a_mat + jnp.eye(CHUNK, dtype=a_mat.dtype)
    rhs = jnp.concatenate([vc * bc[..., None], kc * (bc * jnp.exp(gam))[..., None]], axis=-1)
    sol = lax.linalg.triangular_solve(lhs, rhs, left_side=True, lower=True, unit_diagonal=True)
    w_val, w_k = sol[..., :dv], sol[..., dv:]
    qk = jnp.einsum('cbhtd,cbhsd->cbhts', qc, kc) * decay_mat
    q_dec = qc * jnp.exp(gam)[..., None]
    k_end = kc * jnp.exp(gam[..., -1:] - gam)[..., None]
    g_end = jnp.exp(gam[..., -1])

    def step(S, inp):
        wv, wk, qk_c, qd, ke, ge = inp
        u = wv - jnp.einsum('bhtd,bhde->bhte', wk, S)
        o = jnp.einsum('bhtd,bhde->bhte', qd, S) + jnp.einsum('bhts,bhse->bhte', qk_c, u)
        S_new = ge[..., None, None] * S + jnp.einsum('bhsd,bhse->bhde', ke, u)
        return S_new, o

    S0 = jnp.zeros((b_, h_, dk, dv), jnp.float32)
    _, os_ = lax.scan(step, S0, (w_val, w_k, qk, q_dec, k_end, g_end))
    return _unchunk(os_)

def _causal_conv_silu(x, w):
    kw = w.shape[0]
    s = x.shape[1]
    xp = jnp.pad(x, ((0, 0), (kw - 1, 0), (0, 0)))
    y = sum(w[j].astype(jnp.float32) * xp[:, j:j + s] for j in range(kw))
    return jax.nn.silu(y)

def _hybrid_layer(h, norm_w, w_in, ml_i_bias, ml_f_bias, ml_norm_w,
                  dn_conv_w, dn_a_log, dn_dt_bias, dn_norm_w, w_out):
    u = _rmsnorm(h, norm_w)
    proj = jnp.matmul(u, w_in.astype(jnp.float32))
    idx = np.cumsum(IN_SIZES)[:-1].tolist()
    (ml_q, ml_k, ml_v, ml_o, ml_z, ml_i, ml_f,
     dn_qkv, dn_z, dn_b, dn_a, gate_a, gate_b) = jnp.split(proj, idx, axis=-1)

    i_pre = _softcap(ml_i + ml_i_bias).transpose(0, 2, 1)
    logf = jax.nn.log_sigmoid(_softcap(ml_f + ml_f_bias)).transpose(0, 2, 1)
    h_a = _mlstm_chunkwise(_heads(ml_q, ML_HEADS), _heads(ml_k, ML_HEADS),
                           _heads(ml_v, ML_HEADS), i_pre, logf)
    h_a = _merge_heads(_rmsnorm(h_a)) * ml_norm_w.astype(jnp.float32)
    h_a = h_a * jax.nn.sigmoid(ml_o) * jax.nn.silu(ml_z)

    qkv = _causal_conv_silu(dn_qkv, dn_conv_w)
    dq, dk_, dv_ = jnp.split(qkv, 3, axis=-1)
    dq = _l2norm(_heads(dq, DN_HEADS))
    dk_ = _l2norm(_heads(dk_, DN_HEADS))
    dv_ = _heads(dv_, DN_HEADS)
    beta = jax.nn.sigmoid(dn_b).transpose(0, 2, 1)
    g = (-jnp.exp(dn_a_log.astype(jnp.float32))
         * jax.nn.softplus(dn_a + dn_dt_bias)).transpose(0, 2, 1)
    h_b = _gated_delta_chunkwise(dq, dk_, dv_, beta, g)
    h_b = _rmsnorm(h_b, dn_norm_w)
    h_b = _merge_heads(h_b) * jax.nn.silu(dn_z)

    w_out = w_out.astype(jnp.float32)
    y_a = jnp.matmul(h_a, w_out[:ML_WIDTH])
    y_b = jnp.matmul(h_b, w_out[ML_WIDTH:])
    return jax.nn.sigmoid(gate_a) * y_a + jax.nn.sigmoid(gate_b) * y_b

def first_inputs(seed: int = 0) -> dict:
    key = jax.random.key(seed)
    ks = jax.random.split(key, 13)
    x = jax.random.normal(ks[0], (BATCH, SEQ, D_MODEL), jnp.float32)
    norm_w = 1.0 + 0.05 * jax.random.normal(ks[1], (DEPTH, D_MODEL), jnp.float32)
    w_in = jax.random.normal(ks[2], (DEPTH, D_MODEL, IN_DIM), jnp.float32) * D_MODEL ** -0.5
    ml_i_bias = 0.1 * jax.random.normal(ks[3], (DEPTH, ML_HEADS), jnp.float32)
    ml_f_bias = 3.0 + 0.5 * jax.random.normal(ks[4], (DEPTH, ML_HEADS), jnp.float32)
    ml_norm_w = 1.0 + 0.05 * jax.random.normal(ks[5], (DEPTH, ML_WIDTH), jnp.float32)
    dn_conv_w = jax.random.normal(ks[6], (DEPTH, CONV_WIDTH, 3 * DN_WIDTH), jnp.float32) * CONV_WIDTH ** -0.5
    dn_a_log = jnp.log(jax.random.uniform(ks[7], (DEPTH, DN_HEADS), jnp.float32, 1.0, 16.0))
    dt = jnp.exp(jax.random.uniform(ks[8], (DEPTH, DN_HEADS), jnp.float32,
                                    math.log(1e-3), math.log(1e-1)))
    dn_dt_bias = dt + jnp.log(-jnp.expm1(-dt))
    dn_norm_w = 1.0 + 0.05 * jax.random.normal(ks[9], (DEPTH, DN_HEAD_DIM), jnp.float32)
    w_out = jax.random.normal(ks[10], (DEPTH, OUT_DIM, D_MODEL), jnp.float32) * OUT_DIM ** -0.5
    final_norm_w = 1.0 + 0.05 * jax.random.normal(ks[11], (D_MODEL,), jnp.float32)
    return {"x": x, "norm_w": norm_w, "w_in": w_in, "ml_i_bias": ml_i_bias,
            "ml_f_bias": ml_f_bias, "ml_norm_w": ml_norm_w, "dn_conv_w": dn_conv_w,
            "dn_a_log": dn_a_log, "dn_dt_bias": dn_dt_bias, "dn_norm_w": dn_norm_w,
            "w_out": w_out, "final_norm_w": final_norm_w}

def first_block(x, norm_w, w_in, ml_i_bias, ml_f_bias, ml_norm_w, dn_conv_w,
              dn_a_log, dn_dt_bias, dn_norm_w, w_out, final_norm_w):
    h = x
    for l in range(DEPTH):
        y = _hybrid_layer(h, norm_w[l], w_in[l], ml_i_bias[l], ml_f_bias[l], ml_norm_w[l],
                          dn_conv_w[l], dn_a_log[l], dn_dt_bias[l], dn_norm_w[l], w_out[l])
        h = h + y.astype(h.dtype)
    return _rmsnorm(h, final_norm_w).astype(x.dtype)


MIX_WIDTH = D_MODEL
ATTN_HEAD_DIM = 64
ATTN_WIDTH = MIX_WIDTH // 2
ATTN_HEADS = ATTN_WIDTH // ATTN_HEAD_DIM
DILATION_PATTERNS = ((128, 1), (512, 4), (2048, 16))
QBLK = 128
GLA_WIDTH = MIX_WIDTH - ATTN_WIDTH
GLA_HEADS = 4
GLA_KEY_WIDTH = GLA_WIDTH // 2
GLA_HEAD_DK = GLA_KEY_WIDTH // GLA_HEADS
GLA_HEAD_DV = GLA_WIDTH // GLA_HEADS
GLA_GATE_RANK = 16
GLA_GATE_TAU = 16.0
GLA_CHUNK = 64
FFN_HIDDEN = -(-(8 * D_MODEL) // (3 * 256)) * 256
REL_BUCKETS = 32
REL_MAX_DISTANCE = 1024
IN_SIZES_2 = (ATTN_WIDTH, ATTN_WIDTH, ATTN_WIDTH,
            GLA_KEY_WIDTH, GLA_KEY_WIDTH, GLA_WIDTH, GLA_WIDTH, 2 * GLA_GATE_RANK)
IN_WIDTH = 3 * ATTN_WIDTH + 2 * GLA_KEY_WIDTH + 2 * GLA_WIDTH + 2 * GLA_GATE_RANK


def rmsnorm(x, w):
    x32 = x.astype(jnp.float32)
    y = x32 * lax.rsqrt(jnp.mean(x32 * x32, axis=-1, keepdims=True) + NORM_EPS)
    return y.astype(x.dtype) * w

def _t5_bucket(rel):
    nb = REL_BUCKETS // 2
    ret = np.where(rel > 0, nb, 0)
    n = np.abs(rel)
    max_exact = nb // 2
    large = max_exact + (np.log(np.maximum(n, 1) / max_exact)
                         / math.log(REL_MAX_DISTANCE / max_exact)
                         * (nb - max_exact)).astype(np.int64)
    large = np.minimum(large, nb - 1)
    return (ret + np.where(n < max_exact, n, large)).astype(np.int32)

def _band_layout(L, radius, dilation):
    nb = -(-L // QBLK)
    span = QBLK + 2 * radius
    key_idx = np.arange(nb)[:, None] * QBLK + np.arange(span)[None, :]
    kpos = key_idx - radius
    qpos = np.arange(nb)[:, None] * QBLK + np.arange(QBLK)[None, :]
    off = kpos[:, None, :] - qpos[:, :, None]
    valid = (np.abs(off) <= radius) & (kpos[:, None, :] >= 0) & (kpos[:, None, :] < L)
    bucket = _t5_bucket(off[0] * dilation)
    return nb, key_idx, valid, bucket

def _from_sub(t, L, S):
    B, H, r = t.shape[:3]
    rest = t.shape[5:]
    t = t.reshape((B, H, r, -1) + rest)[:, :, :, :L]
    t = jnp.swapaxes(t, 2, 3)
    return t.reshape((B, H, S) + rest)

def dilated_window_attention(q, k, v, rel_table, window, dilation):
    B, H, S, Dh = q.shape
    L = S // dilation
    R = (window // 2) // dilation
    nb, key_idx, valid, bucket = _band_layout(L, R, dilation)
    Lp = nb * QBLK

    def to_sub(t):
        return t.reshape(B, H, L, dilation, Dh).transpose(0, 1, 3, 2, 4)

    zpad = ((0, 0), (0, 0), (0, 0))
    qs = jnp.pad(to_sub(q), zpad + ((0, Lp - L), (0, 0)))
    ks = jnp.pad(to_sub(k), zpad + ((R, Lp - L + R), (0, 0)))
    vs = jnp.pad(to_sub(v), zpad + ((R, Lp - L + R), (0, 0)))
    qb = qs.reshape(B, H, dilation, nb, QBLK, Dh)
    kb = ks[:, :, :, key_idx]
    vb = vs[:, :, :, key_idx]

    bias = jnp.transpose(rel_table[bucket].astype(jnp.float32), (2, 0, 1))
    logits = (jnp.einsum('bhrnqd,bhrnkd->bhrnqk', qb, kb).astype(jnp.float32)
              * (Dh ** -0.5) + bias[None, :, None, None])
    logits = jnp.where(valid[None, None, None], logits, -1e30)
    m = jnp.max(logits, axis=-1, keepdims=True)
    p = jnp.exp(logits - m)
    s = jnp.sum(p, axis=-1, keepdims=True)
    o = jnp.einsum('bhrnqk,bhrnkd->bhrnqd', p, vb.astype(jnp.float32)) / s
    lse = (m + jnp.log(s))[..., 0]
    return _from_sub(o, L, S), _from_sub(lse, L, S)

def mixture_of_dilations(q, k, v, rel_table):
    outs, lses = [], []
    for window, dilation in DILATION_PATTERNS:
        o, l = dilated_window_attention(q, k, v, rel_table, window, dilation)
        outs.append(o)
        lses.append(l)
    w = jax.nn.softmax(jnp.stack(lses, axis=0), axis=0)
    out = sum(w[i][..., None] * outs[i] for i in range(len(outs)))
    return out

def gla_causal(q, k, v, log_a):
    B, H, S, Dk = q.shape
    Dv = v.shape[-1]
    n = S // GLA_CHUNK
    qc = q.astype(jnp.float32).reshape(B, H, n, GLA_CHUNK, Dk)
    kc = k.astype(jnp.float32).reshape(B, H, n, GLA_CHUNK, Dk)
    vc = v.astype(jnp.float32).reshape(B, H, n, GLA_CHUNK, Dv)
    G = jnp.cumsum(log_a.astype(jnp.float32).reshape(B, H, n, GLA_CHUNK, Dk), axis=-2)
    q_in = qc * jnp.exp(G)
    k_in = kc * jnp.exp(-G)
    tril = jnp.tril(jnp.ones((GLA_CHUNK, GLA_CHUNK), jnp.float32))
    A = jnp.einsum('bhncd,bhnjd->bhncj', q_in, k_in) * tril
    intra = jnp.einsum('bhncj,bhnjv->bhncv', A, vc)
    G_last = G[..., -1:, :]
    k_end = kc * jnp.exp(G_last - G)
    U = jnp.einsum('bhnjd,bhnjv->bhndv', k_end, vc)
    decay = jnp.exp(G_last[..., 0, :])

    def step(state, inp):
        dec, u = inp
        return state * dec[..., None] + u, state

    _, S_prev = lax.scan(step, jnp.zeros((B, H, Dk, Dv), jnp.float32),
                         (jnp.moveaxis(decay, 2, 0), jnp.moveaxis(U, 2, 0)))
    S_prev = jnp.moveaxis(S_prev, 0, 2)
    inter = jnp.einsum('bhncd,bhndv->bhncv', q_in, S_prev)
    return (intra + inter).reshape(B, H, S, Dv)

def _heads_2(t, n_heads):
    B, S, W = t.shape
    return t.reshape(B, S, n_heads, W // n_heads).transpose(0, 2, 1, 3)

def _merge_heads_2(t):
    B, H, S, Dh = t.shape
    return t.transpose(0, 2, 1, 3).reshape(B, S, H * Dh)

def second_inputs(seed: int = 0) -> dict:
    key = jax.random.key(seed)
    ks = jax.random.split(key, 16)
    f32 = jnp.float32
    nrm = lambda k, shape, scale: jax.random.normal(k, shape, f32) * scale
    return {
        "x": nrm(ks[0], (BATCH, SEQ, D_MODEL), 1.0),
        "attn_norm_w": 1.0 + nrm(ks[1], (DEPTH, D_MODEL), 0.02),
        "w_in": nrm(ks[2], (DEPTH, D_MODEL, IN_WIDTH), D_MODEL ** -0.5),
        "rel_bias_table": nrm(ks[3], (REL_BUCKETS, ATTN_HEADS), 0.3),
        "gla_gate_w_fwd": nrm(ks[4], (DEPTH, GLA_GATE_RANK, GLA_KEY_WIDTH), GLA_GATE_RANK ** -0.5),
        "gla_gate_b_fwd": nrm(ks[5], (DEPTH, GLA_KEY_WIDTH), 0.1),
        "gla_gate_w_bwd": nrm(ks[6], (DEPTH, GLA_GATE_RANK, GLA_KEY_WIDTH), GLA_GATE_RANK ** -0.5),
        "gla_gate_b_bwd": nrm(ks[7], (DEPTH, GLA_KEY_WIDTH), 0.1),
        "gla_norm_w": 1.0 + nrm(ks[8], (DEPTH, GLA_WIDTH), 0.02),
        "w_out": nrm(ks[9], (DEPTH, MIX_WIDTH, D_MODEL), MIX_WIDTH ** -0.5),
        "ffn_norm_w": 1.0 + nrm(ks[10], (DEPTH, D_MODEL), 0.02),
        "w_gate": nrm(ks[11], (DEPTH, D_MODEL, FFN_HIDDEN), D_MODEL ** -0.5),
        "w_up": nrm(ks[12], (DEPTH, D_MODEL, FFN_HIDDEN), D_MODEL ** -0.5),
        "w_down": nrm(ks[13], (DEPTH, FFN_HIDDEN, D_MODEL), FFN_HIDDEN ** -0.5),
        "final_norm_w": 1.0 + nrm(ks[14], (D_MODEL,), 0.02),
    }

def second_block(x, attn_norm_w, w_in, rel_bias_table, gla_gate_w_fwd, gla_gate_b_fwd,
              gla_gate_w_bwd, gla_gate_b_bwd, gla_norm_w, w_out, ffn_norm_w,
              w_gate, w_up, w_down, final_norm_w):
    split_idx = []
    acc = 0
    for size in IN_SIZES_2[:-1]:
        acc += size
        split_idx.append(acc)

    for l in range(DEPTH):
        h = rmsnorm(x, attn_norm_w[l])
        proj = h @ w_in[l]
        aq, ak, av, gq, gk, gv, gr, glr = jnp.split(proj, split_idx, axis=-1)

        attn = mixture_of_dilations(_heads_2(aq, ATTN_HEADS), _heads_2(ak, ATTN_HEADS),
                                    _heads_2(av, ATTN_HEADS), rel_bias_table)
        attn_out = _merge_heads_2(attn).astype(x.dtype)

        lr_f, lr_b = glr[..., :GLA_GATE_RANK], glr[..., GLA_GATE_RANK:]
        log_a_f = jax.nn.log_sigmoid((lr_f @ gla_gate_w_fwd[l] + gla_gate_b_fwd[l])
                                     .astype(jnp.float32)) / GLA_GATE_TAU
        log_a_b = jax.nn.log_sigmoid((lr_b @ gla_gate_w_bwd[l] + gla_gate_b_bwd[l])
                                     .astype(jnp.float32)) / GLA_GATE_TAU
        qh = _heads_2(gq, GLA_HEADS) * (GLA_HEAD_DK ** -0.5)
        kh = _heads_2(gk, GLA_HEADS)
        vh = _heads_2(gv, GLA_HEADS)
        fwd = gla_causal(qh, kh, vh, _heads_2(log_a_f, GLA_HEADS))
        flip = lambda t: jnp.flip(t, axis=2)
        bwd = flip(gla_causal(flip(qh), flip(kh), flip(vh), flip(_heads_2(log_a_b, GLA_HEADS))))
        o = fwd + bwd
        o = o * lax.rsqrt(jnp.mean(o * o, axis=-1, keepdims=True) + NORM_EPS)
        gla_out = (_merge_heads_2(o).astype(x.dtype) * gla_norm_w[l]) * jax.nn.silu(gr)

        mixed = jnp.concatenate([attn_out, gla_out], axis=-1) @ w_out[l]
        x = x + mixed

        h = rmsnorm(x, ffn_norm_w[l])
        x = x + (jax.nn.silu(h @ w_gate[l]) * (h @ w_up[l])) @ w_down[l]

    return rmsnorm(x, final_norm_w)


def setup_inputs(seed=0):
    out = dict(first_inputs(seed))
    for name, value in second_inputs(seed + 1).items():
        if name != "x":
            out[name + "_2"] = value
    return out


def reference(
    x, norm_w, w_in, ml_i_bias, ml_f_bias, ml_norm_w, dn_conv_w, dn_a_log, dn_dt_bias,
    dn_norm_w, w_out, final_norm_w, attn_norm_w_2, w_in_2, rel_bias_table_2, gla_gate_w_fwd_2,
    gla_gate_b_fwd_2, gla_gate_w_bwd_2, gla_gate_b_bwd_2, gla_norm_w_2, w_out_2, ffn_norm_w_2,
    w_gate_2, w_up_2, w_down_2, final_norm_w_2,
):
    x = first_block(
        x, norm_w, w_in, ml_i_bias, ml_f_bias, ml_norm_w, dn_conv_w, dn_a_log, dn_dt_bias,
        dn_norm_w, w_out, final_norm_w,
    )
    return second_block(
        x, attn_norm_w_2, w_in_2, rel_bias_table_2, gla_gate_w_fwd_2, gla_gate_b_fwd_2,
        gla_gate_w_bwd_2, gla_gate_b_bwd_2, gla_norm_w_2, w_out_2, ffn_norm_w_2, w_gate_2,
        w_up_2, w_down_2, final_norm_w_2,
    )


_drawn_inputs = setup_inputs


def setup_inputs(seed=0):
    import zlib

    import numpy as np

    out = dict(_drawn_inputs(seed))
    spreads = {}
    factors = {'ml_i_bias': 46.945,
     'ml_norm_w': 6.756,
     'dn_norm_w': 3.417,
     'attn_norm_w_2': 3.099,
     'gla_gate_b_fwd_2': 4.585,
     'gla_gate_b_bwd_2': 4.789,
     'gla_norm_w_2': 6.306,
     'ffn_norm_w_2': 4.014,
     'final_norm_w_2': 7.942,
     'rel_bias_table_2': 2.883}
    for name, (base, spread) in spreads.items():
        noise = np.random.default_rng([zlib.crc32(name.encode()), seed]).standard_normal(out[name].shape)
        drawn = base * np.exp(spread * noise) if base else spread * noise
        out[name] = __import__('jax').numpy.asarray(drawn.astype(out[name].dtype))
    for name, factor in factors.items():
        out[name] = (out[name] * factor).astype(out[name].dtype)
    return out
```

```python
from contextlib import ExitStack

import numpy as np
import concourse.bass as bass
from concourse import mybir

F32 = mybir.dt.float32
F32R = mybir.dt.float32r
ACT = mybir.ActivationFunctionType
ALU = mybir.AluOpType
AX = mybir.AxisListType.X

P = 128
T = 256
NT = T // P
D = 2048
KD = D // P
NC = 512
EPS = 1e-6

ML_H, ML_DK, ML_DV = 8, 128, 256
DN_H, DN_D = 16, 128
DN_W = DN_H * DN_D
CONV = 4
CAP = 15.0
C_MQ = 0
C_MK = C_MQ + ML_H * ML_DK
C_MV = C_MK + ML_H * ML_DK
C_MO = C_MV + ML_H * ML_DV
C_MZ = C_MO + ML_H * ML_DV
C_MI = C_MZ + ML_H * ML_DV
C_DQ = C_MI + 2 * ML_H
C_DK = C_DQ + DN_W
C_DV = C_DK + DN_W
C_DZ = C_DV + DN_W
C_DB = C_DZ + DN_W
C_GA = C_DB + 2 * DN_H
C_GB = C_GA + D

AT_H, AT_D = 16, 64
GL_H, GL_DK, GL_DV, GL_R, GL_C = 4, 128, 256, 16, 64
GL_TAU = 16.0
C_AQ = 0
C_AK = C_AQ + AT_H * AT_D
C_AV = C_AK + AT_H * AT_D
C_GQ = C_AV + AT_H * AT_D
C_GK = C_GQ + GL_H * GL_DK
C_GV = C_GK + GL_H * GL_DK
C_GR = C_GV + GL_H * GL_DV
C_GL = C_GR + GL_H * GL_DV
FFN = 5632
KF = FFN // P

CH = 4
RAW = 3
RING = 4
AHEAD = 3
LAHEAD = 2
LRING = LAHEAD + 1
NBLK = 15
BLK = 1024
NEG = -1e30
LEVELS = 7
BAND = 3 * P


def host_constants():
    r = np.arange(P)[:, None]
    c = np.arange(P)[None, :]
    f = np.float32
    base = [(r == c), (r > c), (r <= c), np.ones((P, P))]
    levels = []
    for l in range(LEVELS):
        w = 2 << l
        levels.append((r // w == c // w) & (r % w < w // 2) & (c % w >= w // 2))
    first = base + levels + [np.where(c > r, NEG, 0.0)]
    same = r // GL_C == c // GL_C
    h = np.arange(GL_C)[None, :]
    second = [same & (r <= c), same & (r >= c), r + c == P - 1,
              np.concatenate([r % GL_C <= h, r % GL_C >= h], axis=1)]
    rel = np.arange(2 * T) - (T - 1)
    half, exact, far = 16, 8, 1024
    n = np.abs(rel)
    large = exact + (np.log(np.maximum(n, 1) / exact) / np.log(far / exact) * (half - exact)).astype(np.int64)
    bucket = np.where(rel > 0, half, 0) + np.where(n < exact, n, np.minimum(large, half - 1))
    times = (n <= 64).astype(np.int64) + (n % 4 == 0) + (n % 16 == 0)
    hot = np.zeros((33, 2 * T), f)
    hot[bucket, np.arange(2 * T)] = 1.0
    hot[32] = np.where(times > 0, np.log(np.maximum(times, 1)), NEG)
    return {"const_first": np.concatenate([np.asarray(m, f) for m in first], axis=1),
            "const_second": np.concatenate([np.asarray(m, f) for m in second], axis=1),
            "const_rel": hot}


class Token:

    def __init__(self, sem, value):
        self.sem, self.value = sem, value


def flat(tokens):
    for t in tokens:
        if isinstance(t, (list, tuple)):
            yield from flat(t)
        elif t is not None:
            yield t


class Queue:

    def __init__(self, nc, ctx, name):
        self.nc, self.ctx, self.name = nc, ctx, name
        self.items, self.sems, self.seen = [], {}, {}

    def do(self, stage, fn, *after, inc=1):
        waits = []
        for t in flat(after):
            if self.seen.get(id(t.sem), 0) < t.value:
                self.seen[id(t.sem)] = t.value
                waits.append((t.sem, t.value))
        if stage is None:
            self.items.append((waits, fn, None, 0))
            return None
        if inc == 1:
            stage = stage.split("_")[0]
        if stage not in self.sems:
            self.sems[stage] = [self.ctx.enter_context(self.nc.semaphore(f"{self.name}_{stage}")), 0]
        s = self.sems[stage]
        s[1] += inc
        self.items.append((waits, fn, s[0], inc))
        return Token(s[0], s[1])

    def play(self, eng):
        for waits, fn, sem, inc in self.items:
            for s, v in waits:
                eng.wait_ge(s, v)
            ins = fn(eng)
            if sem is not None:
                ins.then_inc(sem, inc)


class Place:

    def __init__(self, t):
        self.t, self.free = t, []


def over(ap, axis, n):
    ap = ap.unsqueeze(axis)
    shape = list(ap.shape)
    shape[axis] = n
    return ap.broadcast_to(shape)


class Job:

    def __init__(self, load, chunks, n, done, lhs=None, split=None, ready=lambda k: []):
        self.load, self.chunks, self.n, self.done = load, chunks, n, done
        self.lhs, self.split, self.ready = lhs, split, ready


def build(nc, a, out):
    with ExitStack() as ctx:
        _build(nc, ctx, a, out)


def _build(nc, ctx, a, out):
    def sb(name, shape, dt=F32):
        return ctx.enter_context(nc.sbuf_tensor(name, shape, dt))

    pe, act, dve, pool, sp = (Queue(nc, ctx, n) for n in ("pe", "act", "dve", "pool", "sp"))

    raw = sb("weight_raw", [P, RAW, CH * NC])
    whi = sb("weight_hi", [P, RING, 2 * NC], F32R)
    wlo = sb("weight_lo", [P, RING, 2 * NC], F32R)
    lhi = sb("lhs_hi", [P, LRING, 2, T], F32R)
    llo = sb("lhs_lo", [P, LRING, 2, T], F32R)
    xhi = sb("x_hi", [P, KD, T], F32R)
    xlo = sb("x_lo", [P, KD, T], F32R)
    arena = sb("arena", [P, 2 * KD * T + NBLK * BLK])
    cst = sb("constants", [P, 4 * P])
    cst2 = sb("phase_constants", [P, (LEVELS + 1) * P])
    wcol = sb("norm_columns", [P, 80])
    cwcol = sb("conv_columns", [P, 2 * 96])
    gt = sb("gate_work", [P, 10, 2, 48])
    sm = sb("stats", [P, 900])

    acts = arena[:, 0:2 * KD * T].rearrange("p (k t) -> p k t", t=T)
    acts_all = arena[:, 0:KF * T].rearrange("p (k t) -> p k t", t=T)
    blocks = [Place(arena[:, 2 * KD * T + i * BLK:2 * KD * T + (i + 1) * BLK]) for i in range(NBLK)]
    tail = blocks[:3]
    free_blocks = list(blocks)
    acts_free = []

    IDN, STR, INC, ONE = (cst[:, i * P:(i + 1) * P] for i in range(4))
    LVL = [cst2[:, i * P:(i + 1) * P] for i in range(LEVELS)]
    NEGM = cst2[:, LEVELS * P:(LEVELS + 1) * P]
    CUMF, CUMB, FLIP = (cst2[:, i * P:(i + 1) * P] for i in range(3))
    MASKF, MASKB = cst2[:, 3 * P:3 * P + GL_C], cst2[:, 3 * P + GL_C:4 * P]

    pairs = [Place([ctx.enter_context(nc.psum_tensor(f"gemm_{i}_{j}", [P, NC], F32)) for j in range(NT)])
             for i in range(2)]
    banks = [Place(ctx.enter_context(nc.psum_tensor(f"side_{i}", [P, NC], F32))) for i in range(4)]
    free_banks = list(banks)

    def take():
        while not free_blocks:
            yield False
        return free_blocks.pop(0)

    def take_some(n):
        r = []
        for _ in range(n):
            r.append((yield from take()))
        return r

    def give(b, *readers):
        b.free = [readers]
        free_blocks.append(b)

    def bank():
        while not free_banks:
            yield False
        return free_banks.pop(0)

    def done_with(b, *readers):
        b.free = [readers]
        free_banks.append(b)

    stat = [0]

    def small(n):
        assert stat[0] + n <= 900, stat
        stat[0] += n
        return sm[:, stat[0] - n:stat[0]]

    def copy(q, stage, o, i, *after, scale=None):
        if q is act:
            return act.do(stage, lambda e: e.activation(o, i, ACT.Copy, scale=1.0 if scale is None else scale), *after)
        return q.do(stage, lambda e: e.tensor_copy(o, i), *after)

    def func(stage, f, o, i, *after, **kw):
        return act.do(stage, lambda e: e.activation(o, i, f, **kw), *after)

    def tt(q, stage, o, x, y, op, *after):
        return q.do(stage, lambda e: e.tensor_tensor(o, x, y, op), *after)

    def ts(stage, o, x, s1, op0, s2, op1, *after):
        if op1 is None:
            return dve.do(stage, lambda e: e.tensor_scalar(o, x, s1, None, op0), *after)
        return dve.do(stage, lambda e: e.tensor_scalar(o, x, s1, s2, op0, op1), *after)

    def stt(stage, o, x, s, y, op0, op1, *after):
        return dve.do(stage, lambda e: e.scalar_tensor_tensor(out=o, in0=x, scalar=s, in1=y, op0=op0, op1=op1), *after)

    def reduce(stage, o, i, op, *after):
        return dve.do(stage, lambda e: e.tensor_reduce(o, i, AX, op), *after)

    def mm(stage, o, l, r, *after, start=True, stop=True):
        return pe.do(stage, lambda e: e.matmul(o, l, r, start=start, stop=stop), *after)

    def turn(stage, o, i, *after):
        n = i.shape[0]
        return pe.do(stage, lambda e: e.transpose(o, i, IDN[0:n, 0:n]), *after)

    def rsqrt(stage, o, i, mul, *after):
        n = list(i.shape)
        half = over(minus_half[:, 0:1], 2, n[2])[:, 0:1, :].broadcast_to(n) if len(n) == 3 else minus_half[:, 0:1].broadcast_to(n)
        t = ts(stage + "_mean", i, i, mul, ALU.mult, EPS, ALU.add, *after)
        return tt(pool, stage, o, i, half, ALU.pow, t, t_half)

    def load(stage, o, i, *after, q=None):
        return (q or act).do(stage, lambda e: e.dma_start(o, i), *after, inc=16)

    xblk = [free_blocks.pop(0) for _ in range(D // NC)]
    t_x = []
    for n in range(D // NC):
        t_x.append(load(f"x{n}", xblk[n].t.rearrange("p (t n) -> p t n", t=NT),
                        a["x"][0, :, n * NC:(n + 1) * NC].rearrange("(t p) n -> p t n", p=P)))
    t_c = load("constants", cst[:, :], a["const_first"][:, 0:4 * P])
    rows = free_blocks.pop(0)
    vrows, crows = rows.t[:, 0:P], [rows.t[0:96, (1 + i) * P:(2 + i) * P] for i in range(2)]
    at = 0
    W_NORM, W_ATT, W_FFN, W_ML, W_DN, W_GLA = 0, 16, 32, 48, 64, 65
    for name in ("norm_w", "attn_norm_w_2", "ffn_norm_w_2", "ml_norm_w", "dn_norm_w", "gla_norm_w_2"):
        n = a[name].shape[1] // P
        t_v = (load("norm_rows", vrows[at:at + n, :], a[name].rearrange("a (r p) -> (a r) p", p=P)))
        at += n
    NV = at
    cw = a["dn_conv_w"].rearrange("a j (r p) -> (a j r) p", p=P)
    for i in range(2):
        t_v = load("norm_rows", crows[i], cw[i * 96:(i + 1) * 96, :])
    gb = sb("gate_bias", [P, 48])
    for lo, n, name in ((0, 8, "ml_i_bias"), (8, 8, "ml_f_bias"), (16, 16, "dn_a_log"), (32, 16, "dn_dt_bias")):
        t_b = load("gate_bias", gb[:, lo:lo + n], a[name].broadcast_to([P, n]))
    t_c2 = load("phase_constants", cst2[:, :], a["const_first"][:, 4 * P:])
    minus_half = sb("minus_half", [P, 1])
    t_half = dve.do("minus_half", lambda e: e.memset(minus_half[:, :], -0.5))

    pvec = free_banks.pop(0)
    turn("norm_columns", pvec.t[:, 0:NV], vrows[0:NV, :], t_c, t_v)
    for i in range(2):
        t = turn("norm_columns", pvec.t[:, P + i * 96:P + (i + 1) * 96], crows[i])
    t_w = [copy(dve, "norm_columns", wcol[:, 0:NV], pvec.t[:, 0:NV], t),
           copy(dve, "norm_columns", cwcol[:, :], pvec.t[:, P:P + 192], t)]
    done_with(pvec, t_w)
    give(rows, t)

    x_ready = {}

    def square_sums(n, b, acc, *after):
        scratch = yield from bank()
        for i in range(NT):
            s = func("square_sum", ACT.Square, scratch.t[:, :], b.t[:, i * NC:(i + 1) * NC], after, scratch.free,
                     accum_out=acc[:, i, n:n + 1])
            scratch.free = [s]
        done_with(scratch, s)
        return s

    def norm_scale(acc, *after):
        total, r = small(NT), small(NT)
        t = reduce("norm_total", total, acc, ALU.add, *after)
        return r, rsqrt("norm_rsqrt", r, total, 1.0 / D, t)

    def norm_turn(key, blks, r, wc, free, *after):
        got = []
        for n, b in enumerate(blks):
            s = yield from take()
            for i in range(NT):
                tsc = func("norm_scaled", ACT.Copy, s.t[:, i * NC:(i + 1) * NC], b.t[:, i * NC:(i + 1) * NC],
                           after, s.free, scale=r[:, i:i + 1])
            for c in range(0, NC // P, 2):
                p = yield from bank()
                for cc in range(2):
                    for i in range(NT):
                        t = turn("norm_turned", p.t[:, cc * T + i * P:cc * T + (i + 1) * P],
                                 s.t[:, i * NC + (c + cc) * P:i * NC + (c + cc + 1) * P], tsc, p.free)
                k0 = n * (NC // P) + c
                part = [(k, p.t[:, (k - k0) * T:(k - k0 + 1) * T], wcol[:, wc + k:wc + k + 1]) for k in (k0, k0 + 1)]
                for k, src, w in part:
                    hi = func("x_hi", ACT.Copy, xhi[:, k, :], src, t, t_w, free, scale=w)
                for k, src, w in part:
                    lo = stt("x_lo", xlo[:, k, :], src, w, xhi[:, k, :].bitcast(F32), ALU.mult, ALU.subtract,
                             t, hi, free)
                    got.append([hi, lo])
                done_with(p, hi, lo)
            give(s, t)
            yield True
        x_ready[key] = got

    state = {"pair": 0}
    gens = []
    urgent = []

    def step_all(limit=3):
        moved = False
        for lst, lim in ((urgent, 99), (gens, limit)):
            for g in list(lst[:lim]):
                try:
                    moved |= next(g) is not False
                except StopIteration:
                    lst.remove(g)
                    moved = True
        return moved

    def settle(until):
        idle = 0
        while not until():
            idle = 0 if step_all(4) else idle + 1
            assert idle < 8, ("nothing moves", len(free_blocks), len(free_banks), sorted(got))

    def run_jobs(jobs):
        halves = [(j, c, h) for j in jobs for c in range(len(j.chunks)) for h in range(2)]
        state_w = {}
        state_l = {}
        chunk_of = []
        for idx, (j, c, h) in enumerate(halves):
            chunk_of.append(idx // 2)
        loaded = {}

        def load_chunk(ci):
            j, c, _ = halves[2 * ci]
            slot = ci % RAW
            view = raw[:, slot, 0:CH * j.n].rearrange("p (k n) -> p k n", k=CH)
            prev = [state_w[2 * (ci - RAW) + h][0:2] for h in range(2)] if ci >= RAW else []
            for dst, src in j.load(view, j.chunks[c]):
                t = sp.do(f"weight{slot}", lambda e, dst=dst, src=src: e.dma_start(dst, src), prev, inc=16)
            loaded[ci] = t

        def split(idx):
            j, c, h = halves[idx]
            ci = idx // 2
            if ci not in loaded:
                load_chunk(ci)
            r = idx % RING
            src = raw[:, ci % RAW, h * 2 * j.n:(h + 1) * 2 * j.n]
            hi_t, lo_t = whi[:, r, 0:2 * j.n], wlo[:, r, 0:2 * j.n]
            used = state_w[idx - RING][2] if idx >= RING else []
            hi = copy(act, "weight_hi", hi_t, src, loaded[ci], used)
            lo = tt(dve, "weight_lo", lo_t, src, hi_t.bitcast(F32), ALU.subtract, hi, used)
            state_w[idx] = [hi, lo, None]
            if h == 1 and 2 * (ci + RAW) < len(halves):
                load_chunk(ci + RAW)

        def split_lhs(idx):
            j, c, h = halves[idx]
            k = j.chunks[c] * CH + 2 * h
            r = idx % LRING
            src = j.split(k)
            used = state_w[idx - LRING][2] if idx >= LRING else []
            hi = copy(act, "lhs_hi", lhi[:, r], src, j.ready(k), used)
            lo = tt(dve, "lhs_lo", llo[:, r], src, lhi[:, r].bitcast(F32), ALU.subtract, hi, used)
            state_l[idx] = [hi, lo]

        for ci in range(min(RAW, len(halves) // 2)):
            load_chunk(ci)
        for idx in range(min(AHEAD, len(halves))):
            split(idx)
        pair = None
        for idx, (j, c, h) in enumerate(halves):
            if idx + AHEAD < len(halves):
                split(idx + AHEAD)
            k0 = j.chunks[c] * CH + 2 * h
            if j.split is None:
                settle(lambda: j.ready(k0) is not None)
                parts, made = j.lhs, j.ready(k0)
            else:
                for look in range(idx, min(idx + LAHEAD + 1, len(halves))):
                    jj, cc, hh = halves[look]
                    if jj.split is None or look in state_l:
                        continue
                    kk = jj.chunks[cc] * CH + 2 * hh
                    if look == idx:
                        settle(lambda: jj.ready(kk) is not None)
                    if jj.ready(kk) is None:
                        break
                    split_lhs(look)
                r = idx % LRING
                parts = lambda k: (lhi[:, r, k - k0], llo[:, r, k - k0])
                made = state_l[idx]
            if c == 0 and h == 0:
                state["pair"] += 1
                pair = pairs[state["pair"] % 2]
                settle(lambda: pair.free is not None)
                opening = pair.free
                pair.free = None
            r4 = idx % RING
            last = c == len(j.chunks) - 1 and h == 1
            for kk in range(2):
                xh, xl = parts(k0 + kk)
                wh = whi[:, r4, kk * j.n:(kk + 1) * j.n]
                wl = wlo[:, r4, kk * j.n:(kk + 1) * j.n]
                for i in range(NT):
                    for n3, (l, w) in enumerate(((xh, wh), (xh, wl), (xl, wh))):
                        end = kk == 1 and i == NT - 1 and n3 == 2
                        t = mm("product" if end else None, pair.t[i][:, 0:j.n], l[:, i * P:(i + 1) * P], w,
                               state_w[idx][0:2], made, opening if c == 0 and h == 0 else None,
                               start=(c == 0 and h == 0 and kk == 0 and n3 == 0), stop=(last and kk == 1 and n3 == 2))
            state_w[idx][2] = t
            state["last"] = t
            if last:
                urgent.append(j.done(pair, t))
            step_all()

    def columns(w, c0, n=NC):
        def f(view, c):
            return [(view, w[c * CH * P:(c + 1) * CH * P, c0:c0 + n].rearrange("(k p) n -> p k n", p=P))]
        return f

    def product(w, c0, done, key, n=NC):
        return Job(columns(w, c0, n), list(range(KD // CH)), n, done,
                   lhs=lambda k: (xhi[:, k], xlo[:, k]),
                   ready=lambda k: x_ready[key][k:k + 2] if key in x_ready else None)

    got = {}

    def keep(key, q=None, then=None):
        def done(pair, t):
            b = yield from take()
            for i in range(NT):
                e = copy((act, dve)[i] if q is None else q, "kept_" + ("ad"[i] if q is None else "x"),
                         b.t[:, i * NC:(i + 1) * NC], pair.t[i][:, :], t, b.free)
                if i == 0:
                    e0 = e
            pair.free = [e0, e]
            got[key] = (b, [e0, e])
            if then is not None:
                gens.append(then())
            yield True
        return done

    def keep_silu2(key, then=None):
        def done(pair, t):
            b = yield from take()
            for i in range(NT):
                e = func("half_tanh", ACT.Tanh, b.t[:, i * NC:(i + 1) * NC], pair.t[i][:, :], t, b.free, scale=0.5)
            yield True
            for i in range(NT):
                bb = b.t[:, i * NC:(i + 1) * NC]
                e2 = stt("silu2", bb, bb, 1.0, pair.t[i][:, :], ALU.add, ALU.mult, e)
            pair.free = [e2]
            got[key] = (b, [e2])
            if then is not None:
                gens.append(then())
            yield True
        return done

    def need(*keys):
        while not all(k in got for k in keys):
            yield False
        return [got.pop(k) for k in keys]

    def to_channels(b, t_b, scale=None):
        o = yield from take()
        view = o.t.rearrange("p (c t) -> p c t", t=T)
        ts_ = []
        for c in range(0, 4, 2):
            p = yield from bank()
            for cc in range(2):
                for i in range(NT):
                    t = turn("to_channels", p.t[:, cc * T + i * P:cc * T + (i + 1) * P],
                             b.t[:, i * NC + (c + cc) * P:i * NC + (c + cc + 1) * P], t_b, p.free)
            e = copy(act, "to_channels", view[:, c:c + 2, :], p.t[:, :].rearrange("p (c t) -> p c t", t=T), t, o.free, scale=scale)
            done_with(p, e)
            ts_.append(e)
            yield True
        give(b, t)
        return o, ts_

    w_in = a["w_in"][0]
    w_out = a["w_out"][0]

    def first_norm():
        acc = small(NT * (D // NC)).rearrange("p (t n) -> p t n", t=NT)
        for n in range(D // NC):
            s = yield from square_sums(n, xblk[n], acc, t_x[n])
        r, t = norm_scale(acc, s)
        yield True
        yield from norm_turn("u1", xblk, r, W_NORM, [], t)
        for b in xblk:
            give(b, x_ready["u1"])

    gens.append(first_norm())

    gates = {}

    def load_gates(view, c):
        rows_ = slice(c * CH * P, (c + 1) * CH * P)
        return [(view[:, :, 0:16], w_in[rows_, C_MI:C_MI + 16].rearrange("(k p) n -> p k n", p=P)),
                (view[:, :, 16:48], w_in[rows_, C_DB:C_DB + 32].rearrange("(k p) n -> p k n", p=P))]

    def gates_done(pair, t):
        g = [gt[:, i] for i in range(10)]
        v = g[0]
        for i in range(NT):
            e = copy(dve, "gate_raw", v[:, i, :], pair.t[i][:, 0:48], t)
        pair.free = [e]
        th, arg, ex, u, ln, inv, z, res = g[1:9]
        b2 = lambda lo, n: over(gb[:, lo:lo + n], 1, NT)
        t1 = tt(dve, "gate_biased", th[:, :, 0:16], v[:, :, 0:16], b2(0, 16), ALU.add, e, t_b)
        t2 = tt(dve, "gate_z", z[:, :, 0:16], v[:, :, 32:48], b2(32, 16), ALU.add, e, t_b)
        t3 = func("gate_tanh", ACT.Tanh, th[:, :, 0:16], th[:, :, 0:16], t1, scale=1.0 / CAP)
        t4 = ts("gate_arg", arg[:, :, 0:8], th[:, :, 8:16], -CAP, ALU.mult, None, None, t3)
        t5 = ts("gate_arg", arg[:, :, 8:24], v[:, :, 16:32], -1.0, ALU.mult, None, None, e)
        t6 = stt("gate_arg", arg[:, :, 24:40], z[:, :, 0:16], -1.0, z[:, :, 0:16], ALU.mult, ALU.min, t2)
        t7 = func("gate_exp", ACT.Exp, ex[:, :, 0:40], arg[:, :, 0:40], t4, t5, t6)
        ta = func("gate_exp", ACT.Exp, gb[:, 16:32], gb[:, 16:32], t_b)
        t8 = ts("gate_u", u[:, :, 0:40], ex[:, :, 0:40], 1.0, ALU.add, None, None, t7)
        t9 = dve.do("gate_inv", lambda e: e.reciprocal(inv[:, :, 0:40], u[:, :, 0:40]), t8)
        func("gate_ln", ACT.Ln, ln[:, :, 0:8], u[:, :, 0:8], t8)
        tl = func("gate_ln", ACT.Ln, ln[:, :, 24:40], u[:, :, 24:40], t8)
        yield True
        for lo, n in ((0, 8), (24, 16)):
            s = (slice(None), slice(None), slice(lo, lo + n))
            x1 = ts("gate_log1p", arg[s], u[s], -1.0, ALU.add, None, None, t8)
            x2 = tt(dve, "gate_log1p", arg[s], ex[s], arg[s], ALU.subtract, x1)
            x3 = tt(dve, "gate_log1p", arg[s], arg[s], inv[s], ALU.mult, x2, t9)
            x4 = tt(dve, "gate_log1p", arg[s], arg[s], ln[s], ALU.add, x3, tl)
        r1 = ts("gate_i", res[:, :, 0:8], th[:, :, 0:8], CAP, ALU.mult, None, None, t3)
        r2 = ts("gate_f", res[:, :, 8:16], arg[:, :, 0:8], -1.0, ALU.mult, None, None, x4)
        y1 = stt("gate_g", res[:, :, 16:32], z[:, :, 0:16], 0.0, arg[:, :, 24:40], ALU.max, ALU.add, x4)
        y2 = stt("gate_g", res[:, :, 16:32], res[:, :, 16:32], -1.0, over(gb[:, 16:32], 1, NT), ALU.mult, ALU.mult, y1, ta)
        gates.update(i=res[:, :, 0:8], f=res[:, :, 8:16], g=res[:, :, 16:32], beta=inv[:, :, 8:24],
                     t=[r1, r2, y2, t9])
        yield True
        p = yield from bank()
        ft = g[9]
        mm("forget_sum", p.t[:, 0:8], INC, res[:, 0, 8:16], gates["t"], p.free)
        mm("forget_sum", p.t[:, 8:16], ONE, res[:, 0, 8:16], stop=False)
        m = mm("forget_sum", p.t[:, 8:16], INC, res[:, 1, 8:16], start=False)
        c = copy(dve, "forget_sum", ft[:, :, 0:8], p.t[:, 0:16].rearrange("p (t h) -> p t h", t=NT), m)
        done_with(p, c)
        gates.update(F=ft[:, :, 0:8], tF=[c])
        yield True

    def conv(key, ct):
        (b, tb), = yield from need(key)
        y = yield from take()
        yv = y.t.rearrange("p (c t) -> p c t", t=T)
        fin = []
        for c in range(0, 4, 2):
            p = yield from bank()
            for cc in range(2):
                for i in range(NT):
                    t = turn("conv_turned", p.t[:, cc * T + i * P:cc * T + (i + 1) * P],
                             b.t[:, i * NC + (c + cc) * P:i * NC + (c + cc + 1) * P], tb, p.free)
            yield True
            w = lambda cc, j: cwcol[:, j * 48 + ct + c + cc:j * 48 + ct + c + cc + 1]
            for cc in range(2):
                s0 = func("conv_last_tap", ACT.Copy, yv[:, c + cc, :], p.t[:, cc * T:(cc + 1) * T], t, y.free, t_w,
                          scale=w(cc, CONV - 1))
            for cc in range(2):
                s = s0
                for j in range(1, CONV):
                    s = stt("conv_tap", yv[:, c + cc, j:T], p.t[:, cc * T:(cc + 1) * T - j], w(cc, CONV - 1 - j),
                            yv[:, c + cc, j:T], ALU.mult, ALU.add, s)
                fin.append(s)
            done_with(p, fin)
            yield True
        give(b, t)
        th = yield from take()
        e = func("conv_tanh", ACT.Tanh, th.t, y.t, fin, th.free, scale=0.5)
        e = stt("conv_silu2", y.t, th.t, 1.0, y.t, ALU.add, ALU.mult, e)
        give(th, e)
        got[key + "c"] = (y, [e])
        yield True

    HB = 4
    hb_ready = {}

    def delta(g):
        h0 = g * HB
        (yk, tk), (yq, tq) = yield from need(f"dk{g}c", f"dq{g}c")
        beta, gg = gates["beta"], gates["g"]
        hs = slice(h0, h0 + HB)
        ss = small(4 * HB).rearrange("p (q t h) -> p q t h", q=2, t=NT)
        p = yield from bank()
        sq_free = []
        for n, (y, t_y) in enumerate(((yq, tq), (yk, tk))):
            sq = yield from take()
            e = func("delta_square", ACT.Square, sq.t, y.t, t_y, sq.free)
            for i in range(NT):
                for h in range(HB):
                    m = mm("delta_square_sum", p.t[:, (n * NT + i) * HB + h:(n * NT + i) * HB + h + 1],
                           sq.t[:, h * T + i * P:h * T + (i + 1) * P], ONE[:, 0:1], e, p.free)
            give(sq, m)
            yield True
        e = ts("delta_ss", ss.rearrange("p q t h -> p (q t h)"), p.t[:, 0:4 * HB], 0.25, ALU.mult, EPS, ALU.add, m)
        done_with(p, e)
        r = small(4 * HB).rearrange("p (q t h) -> p q t h", q=2, t=NT)
        e = tt(pool, "delta_rsqrt", r.rearrange("p q t h -> p (q t h)"), ss.rearrange("p q t h -> p (q t h)"),
               minus_half[:, 0:1].broadcast_to([P, 4 * HB]), ALU.pow, e, t_half)
        rq, rk, ck, hb_ = (small(NT * HB).rearrange("p (t h) -> p t h", t=NT) for _ in range(4))
        t_rq = ts("delta_factor", rq, r[:, 0], 0.5 * DN_D ** -0.5, ALU.mult, None, None, e)
        t_rk = ts("delta_factor", rk, r[:, 1], 0.5, ALU.mult, None, None, e)
        t_ck = tt(dve, "delta_factor", ck, rk, beta[:, :, hs], ALU.mult, t_rk, gates["t"])
        t_hb = ts("delta_factor", hb_, beta[:, :, hs], 0.5, ALU.mult, None, None, gates["t"])
        yield True
        kc = yield from take()
        for i in range(NT):
            p = yield from bank()
            for h in range(HB):
                m = turn("delta_k", p.t[:, h * P:(h + 1) * P], yk.t[:, h * T + i * P:h * T + (i + 1) * P], tk, p.free)
            e = tt(dve, "delta_k_scaled", kc.t[:, i * NC:(i + 1) * NC].rearrange("p (h d) -> p h d", h=HB),
                   p.t[:, :].rearrange("p (h d) -> p h d", h=HB), over(ck[:, i], 2, P), ALU.mult, m, t_ck, kc.free)
            done_with(p, e)
            yield True
        kt = yield from take()
        ktv = kt.t.rearrange("p (h t) -> p h t", h=HB)
        t_kc = []
        for i in range(NT):
            p = yield from bank()
            for h in range(HB):
                m = turn("delta_kc", p.t[:, h * P:(h + 1) * P], kc.t[:, i * NC + h * P:i * NC + (h + 1) * P], e, p.free)
            t_kc.append(copy(act, "delta_kc", ktv[:, :, i * P:(i + 1) * P],
                             p.t[:, :].rearrange("p (h d) -> p h d", h=HB), m, kt.free))
            done_with(p, t_kc)
            yield True
        give(kc, m)
        R0, R1 = (yield from take()), (yield from take())
        R0v, R1v = R0.t.rearrange("p (h t) -> p h t", h=HB), R1.t[:, 0:NC].rearrange("p (h t) -> p h t", h=HB)
        ra = tt(pool, "delta_decay_rhs", R0v[:, :, 0:P], over(INC, 1, HB), over(gg[:, 0, hs], 2, P), ALU.mult,
                R0.free, t_c, gates["t"])
        rb = tt(pool, "delta_decay_rhs", R0v[:, :, P:T], over(ONE, 1, HB), over(gg[:, 0, hs], 2, P), ALU.mult)
        rc = tt(pool, "delta_decay_rhs", R1v, over(INC, 1, HB), over(gg[:, 1, hs], 2, P), ALU.mult, R1.free)
        E0, E1 = (yield from take()), (yield from take())
        E0v, E1v = E0.t.rearrange("p (h t) -> p h t", h=HB), E1.t[:, 0:NC].rearrange("p (h t) -> p h t", h=HB)
        es = []
        yield True
        for n in range(2):
            p = yield from bank()
            mm("delta_decay", p.t[:, :], STR, R0v[:, 2 * n:2 * n + 2, :], rb, p.free, stop=False)
            m = mm("delta_decay", p.t[:, :].rearrange("p (h t) -> p h t", h=2)[:, :, P:T], ONE,
                   R1v[:, 2 * n:2 * n + 2, :], rc, start=False)
            es.append(func("delta_decay", ACT.Exp, E0v[:, 2 * n:2 * n + 2, :],
                           p.t[:, :].rearrange("p (h t) -> p h t", h=2), m, E0.free))
            done_with(p, es)
        p = yield from bank()
        m = mm("delta_decay", p.t[:, :], STR, R1v, rc, p.free)
        es.append(func("delta_decay", ACT.Exp, E1v, p.t[:, :].rearrange("p (h t) -> p h t", h=HB), m, E1.free))
        done_with(p, es)
        give(R0, m)
        give(R1, m)
        yield True
        e = tt(pool, "delta_masked", E0v[:, :, 0:P], E0v[:, :, 0:P], over(INC, 1, HB), ALU.mult, es)
        e = tt(pool, "delta_masked", E1v, E1v, over(INC, 1, HB), ALU.mult, es)
        e = tt(pool, "delta_masked", E0v, E0v, over(rk[:, 0], 2, T), ALU.mult, e, t_rk)
        t_E = tt(pool, "delta_masked", E1v, E1v, over(rk[:, 1], 2, P), ALU.mult, e)
        P0, B0 = (yield from take()), (yield from take())
        PB1 = yield from take()
        P0v, B0v = (b.t.rearrange("p (h t) -> p h t", h=HB) for b in (P0, B0))
        P1v, B1v = (PB1.t[:, i * NC:(i + 1) * NC].rearrange("p (h t) -> p h t", h=HB) for i in range(2))
        t_P, t_B = [], []
        yield True
        for dst, y, lst in ((B0v, kt, t_B), (P0v, yq, t_P)):
            for n in range(2):
                p = yield from bank()
                for h in range(2 * n, 2 * n + 2):
                    m = mm("delta_scores", p.t[:, (h - 2 * n) * T:(h - 2 * n + 1) * T], yk.t[:, h * T:h * T + P],
                           y.t[:, h * T:(h + 1) * T], tk, tq, t_kc, p.free)
                lst.append(tt(dve, "delta_weights", dst[:, 2 * n:2 * n + 2, :],
                              p.t[:, :].rearrange("p (h t) -> p h t", h=2), E0v[:, 2 * n:2 * n + 2, :], ALU.mult,
                              m, t_E, P0.free, B0.free))
                done_with(p, lst)
                yield True
        for dst, y, lst in ((B1v, kt, t_B), (P1v, yq, t_P)):
            p = yield from bank()
            for h in range(HB):
                m = mm("delta_scores", p.t[:, h * P:(h + 1) * P], yk.t[:, h * T + P:(h + 1) * T],
                       y.t[:, h * T + P:(h + 1) * T], p.free)
            lst.append(tt(dve, "delta_weights", dst, p.t[:, :].rearrange("p (h t) -> p h t", h=HB), E1v, ALU.mult,
                          m, t_E, PB1.free))
            done_with(p, lst)
            yield True
        give(yk, m)
        give(yq, m)
        give(kt, m)
        give(E0, t_P, t_B)
        give(E1, t_P, t_B)
        U, Tt = (yield from take()), (yield from take())
        BM = yield from take()
        X = yield from take()
        half = lambda b, i: b.t[:, i * NC:(i + 1) * NC]
        hv = lambda b, i: half(b, i).rearrange("p (h t) -> p h t", h=HB)
        Bv = [B0v[:, :, 0:P], B1v]
        t_U, t_T, t_X = [None] * 2, [None] * 2, [None] * 2
        for i in range(NT):
            e = tt(pool, "delta_level", hv(BM, i), Bv[i], over(LVL[0], 1, HB), ALU.mult, t_B, BM.free, t_c2)
            t_U[i] = tt(dve, "delta_U", hv(U, i), over(IDN, 1, HB), hv(BM, i), ALU.subtract, e, U.free)
        yield True
        for i in range(NT):
            p = yield from bank()
            for h in range(HB):
                m = turn("delta_T", p.t[:, h * P:(h + 1) * P], hv(U, i)[:, h, :], t_U[i], p.free)
            t_T[i] = copy(act, "delta_T", half(Tt, i), p.t[:, :], m, Tt.free)
            done_with(p, t_T[i])
        for l in range(1, LEVELS):
            last = l == LEVELS - 1
            t_BM = [None] * 2
            for i in range(NT):
                t_BM[i] = tt(pool, "delta_level", hv(BM, i), Bv[i], over(LVL[l], 1, HB), ALU.mult, t_X[i], t_U[i])
            yield True
            for i in range(NT):
                p = yield from bank()
                for h in range(HB):
                    m = mm("delta_X", p.t[:, h * P:(h + 1) * P], hv(BM, i)[:, h, :], hv(Tt, i)[:, h, :],
                           t_BM[i], t_T[i], p.free)
                t_X[i] = copy(act, "delta_X", half(X, i), p.t[:, :], m, X.free, t_U[i], t_T[i])
                done_with(p, t_X[i])
            X.free = []
            yield True
            for i in range(NT):
                p = yield from bank()
                for h in range(HB):
                    m = mm("delta_Y", p.t[:, h * P:(h + 1) * P], hv(X, i)[:, h, :], hv(U, i)[:, h, :],
                           t_X[i], t_U[i], p.free)
                if not last:
                    p2 = yield from bank()
                    for h in range(HB):
                        m2 = mm("delta_YT", p2.t[:, h * P:(h + 1) * P], hv(U, i)[:, h, :], hv(X, i)[:, h, :], p2.free)
                    t_T[i] = tt(dve, "delta_T", half(Tt, i), half(Tt, i), p2.t[:, :], ALU.subtract, m2)
                    done_with(p2, t_T[i])
                    m = m2
                t_U[i] = tt(dve, "delta_U", half(U, i), half(U, i), p.t[:, :], ALU.subtract, m)
                done_with(p, t_U[i])
        give(Tt, t_X, t_T)
        give(BM, t_X)
        give(X, t_U, t_T)
        yield True
        (yv, tv), = yield from need(f"dv{g}c")
        bv, u = (yield from take()), (yield from take())
        bvv = lambda i: bv.t[:, i * NC:(i + 1) * NC].rearrange("p (h d) -> p h d", h=HB)
        t_bv = []
        for i in range(NT):
            p = yield from bank()
            for h in range(HB):
                m = turn("delta_v", p.t[:, h * P:(h + 1) * P], yv.t[:, h * T + i * P:h * T + (i + 1) * P], tv, p.free)
            t_bv.append(tt(dve, "delta_bv", bvv(i), p.t[:, :].rearrange("p (h d) -> p h d", h=HB),
                           over(hb_[:, i], 2, P), ALU.mult, m, t_hb, bv.free))
            done_with(p, t_bv)
        give(yv, m)
        yield True
        p = yield from bank()
        for h in range(HB):
            m = mm("delta_u", p.t[:, h * P:(h + 1) * P], hv(U, 0)[:, h, :], bvv(0)[:, h, :], t_U, t_bv, p.free)
        t_u0 = copy(act, "delta_u", half(u, 0), p.t[:, :], m, u.free)
        done_with(p, t_u0)
        yield True
        p = yield from bank()
        for h in range(HB):
            m = mm("delta_bu", p.t[:, h * P:(h + 1) * P], B0v[:, h, P:T], hv(u, 0)[:, h, :], t_u0, p.free)
        e = tt(dve, "delta_bv", half(bv, 1), half(bv, 1), p.t[:, :], ALU.subtract, m)
        done_with(p, e)
        yield True
        p = yield from bank()
        for h in range(HB):
            m = mm("delta_u", p.t[:, h * P:(h + 1) * P], hv(U, 1)[:, h, :], bvv(1)[:, h, :], e, p.free)
        t_u1 = copy(act, "delta_u", half(u, 1), p.t[:, :], m)
        done_with(p, t_u1)
        give(bv, m)
        give(U, m)
        give(B0, m)
        o = yield from take()
        t_o = []
        yield True
        for i in range(NT):
            p = yield from bank()
            for h in range(HB):
                if i == 0:
                    m = mm("delta_o", p.t[:, h * P:(h + 1) * P], P0v[:, h, 0:P], hv(u, 0)[:, h, :], t_u0, t_P, p.free)
                else:
                    mm("delta_o", p.t[:, h * P:(h + 1) * P], P0v[:, h, P:T], hv(u, 0)[:, h, :], p.free, stop=False)
                    m = mm("delta_o", p.t[:, h * P:(h + 1) * P], P1v[:, h, :], hv(u, 1)[:, h, :], t_u1, start=False)
            t_o.append(tt(dve, "delta_o", hv(o, i), p.t[:, :].rearrange("p (h d) -> p h d", h=HB),
                          over(rq[:, i], 2, P), ALU.mult, m, t_rq, o.free))
            done_with(p, t_o)
            yield True
        give(P0, m)
        give(PB1, m)
        give(u, m)
        sq = yield from take()
        e = func("delta_o_square", ACT.Square, sq.t, o.t, t_o, sq.free)
        s2, ro = small(NT * HB), small(NT * HB)
        e = reduce("delta_o_sum", s2, sq.t.rearrange("p (g d) -> p g d", d=P), ALU.add, e)
        give(sq, e)
        e = rsqrt("delta_o_rsqrt", ro, s2, 1.0 / DN_D, e)
        yield True
        (wz, tz), = yield from need(f"dz{g}")
        e = tt(pool, "delta_o_normed", o.t.rearrange("p (g d) -> p g d", d=P), o.t.rearrange("p (g d) -> p g d", d=P),
               over(ro, 2, P), ALU.mult, e)
        e = stt("delta_o_gated", o.t, wz.t, 0.5, o.t, ALU.mult, ALU.mult, e, tz)
        give(wz, e)
        yield True
        t_h = []
        for i in range(NT):
            p = yield from bank()
            for h in range(HB):
                m = turn("delta_out", p.t[:, h * P:(h + 1) * P], hv(o, i)[:, h, :], e, p.free)
            t_h.append(copy(act, "delta_out", acts[:, KD + h0:KD + h0 + HB, i * P:(i + 1) * P],
                            p.t[:, :].rearrange("p (h t) -> p h t", h=HB), m, acts_free, scale=wcol[:, W_DN:W_DN + 1]))
            done_with(p, t_h)
        give(o, m)
        hb_ready[g] = t_h
        yield True

    ml = {}

    def mlstm_scores(G):
        (qr, tq), = yield from need(f"mq{G}")
        (kr, tk), = yield from need(f"mk{G}")
        qT, tq = yield from to_channels(qr, tq)
        kT, tk = yield from to_channels(kr, tk)
        hs = slice(G * HB, (G + 1) * HB)
        ig, fg, Fs = gates["i"], gates["f"], gates["F"]
        FS, II = (yield from take()), (yield from take())
        hv = lambda b, i: b.t[:, i * NC:(i + 1) * NC].rearrange("p (h t) -> p h t", h=HB)
        hf = lambda b, i: b.t[:, i * NC:(i + 1) * NC]
        for i in range(NT):
            tt(pool, "ml_decay_rhs", hv(FS, i), over(STR, 1, HB), over(fg[:, i, hs], 2, P), ALU.mult, FS.free, gates["t"])
            r = tt(pool, "ml_decay_rhs", hv(II, i), over(IDN, 1, HB), over(ig[:, i, hs], 2, P), ALU.mult, II.free)
        yield True
        Dd, Dx = (yield from take()), (yield from take())
        mx = small(3 * HB).rearrange("p (n h) -> p n h", h=HB)
        tm = []
        for n, (i, s) in enumerate(((0, 0), (1, 1), (1, 0))):
            p = yield from bank()
            pv = p.t[:, :].rearrange("p (h t) -> p h t", h=HB)
            mm("ml_decay", p.t[:, :], INC if i == s else ONE, hf(FS, s), r, p.free, stop=False)
            if i != s:
                mm("ml_decay", pv, INC, over(fg[:, 1, hs], 2, P), start=False, stop=False)
            m = mm("ml_decay", p.t[:, :], ONE, hf(II, s), start=False)
            if i == s:
                e = tt(dve, "ml_masked", hv(Dd, n), pv, over(NEGM, 1, HB), ALU.add, m, Dd.free, t_c2)
                tm.append(reduce("ml_max", mx[:, n], hv(Dd, n), ALU.max, e))
            else:
                e = copy(act, "ml_decay", hf(Dx, 0), p.t[:, :], m, Dx.free)
                tm.append(reduce("ml_max", mx[:, n], hv(Dx, 0), ALU.max, e))
            done_with(p, e)
            yield True
        give(FS, m)
        give(II, m)
        M, nM, em = (small(NT * HB).rearrange("p (t h) -> p t h", t=NT) for _ in range(3))
        e1 = tt(dve, "ml_m", M[:, 0], mx[:, 0], Fs[:, 0, hs], ALU.max, tm, gates["tF"])
        e2 = tt(dve, "ml_m", M[:, 1], mx[:, 1], mx[:, 2], ALU.max, tm)
        e2 = tt(dve, "ml_m", M[:, 1], M[:, 1], Fs[:, 1, hs], ALU.max, e2)
        e3 = ts("ml_m", nM, M, -1.0, ALU.mult, None, None, e1, e2)
        t_em = func("ml_em", ACT.Exp, em, nM, e3)
        tiles = ((0, 0, hv(Dd, 0), hf(Dd, 0)), (1, 1, hv(Dd, 1), hf(Dd, 1)), (1, 0, hv(Dx, 0), hf(Dx, 0)))
        es = []
        for n, (i, s, v, f) in enumerate(tiles):
            for h in range(HB):
                e = func("ml_exp", ACT.Exp, v[:, h], v[:, h], e3, bias=nM[:, i, h:h + 1])
            es.append(e)
            yield True
        dn = small(3 * HB).rearrange("p (n h) -> p n h", h=HB)
        WT = yield from take_some(2)
        wtv = [hv(WT[0], 0), hv(WT[0], 1), hv(WT[1], 0)]
        t_W, t_d = [], []
        for n, (i, s, v, f) in enumerate(tiles):
            p = yield from bank()
            for h in range(HB):
                m = mm("ml_scores", p.t[:, h * P:(h + 1) * P], qT.t[:, h * T + i * P:h * T + (i + 1) * P],
                       kT.t[:, h * T + s * P:h * T + (s + 1) * P], tq, tk, p.free)
            e = stt("ml_weights", f, p.t[:, :], ML_DK ** -0.5, f, ALU.mult, ALU.mult, m, es[n])
            t_d.append(reduce("ml_den", dn[:, n], v, ALU.add, e))
            done_with(p, e)
            yield True
            p = yield from bank()
            for h in range(HB):
                m2 = turn("ml_turned", p.t[:, h * P:(h + 1) * P], v[:, h], e, p.free)
            t_W.append(copy(act, "ml_turned", wtv[n], p.t[:, :].rearrange("p (h t) -> p h t", h=HB), m2, WT[n // 2].free))
            done_with(p, t_W)
            yield True
        give(qT, m)
        give(kT, m)
        give(Dd, m2, t_d)
        give(Dx, m2, t_d)
        den, inv = (small(NT * HB).rearrange("p (t h) -> p t h", t=NT) for _ in range(2))
        e = tt(dve, "ml_den2", dn[:, 1], dn[:, 1], dn[:, 2], ALU.add, t_d)
        e = stt("ml_den2", den, dn[:, 0:2], -1.0, dn[:, 0:2], ALU.mult, ALU.max, e)
        e = tt(dve, "ml_den2", den, den, em, ALU.max, e, t_em)
        e = dve.do("ml_inv", lambda q: q.reciprocal(inv, den), e)
        ml[G] = dict(W=wtv, WT=WT, tW=t_W, inv=inv, tinv=e, users=[], left=2)
        yield True

    ha_ready = {}

    def mlstm_out(pr):
        G, h0 = pr // 2, 2 * (pr % 2)
        while G not in ml:
            yield False
        s = ml[G]
        (v, tv), = yield from need(f"mv{pr}")
        ssq, rr, fac = (small(NT * 2).rearrange("p (t h) -> p t h", t=NT) for _ in range(3))
        ps = []
        for i in range(NT):
            p = yield from bank()
            for hh in range(2):
                h = h0 + hh
                o = p.t[:, hh * ML_DV:(hh + 1) * ML_DV]
                vv = lambda k: v.t[:, k * NC + hh * ML_DV:k * NC + (hh + 1) * ML_DV]
                if i == 0:
                    m = mm("ml_num", o, s["W"][0][:, h], vv(0), s["tW"], tv, p.free)
                else:
                    mm("ml_num", o, s["W"][2][:, h], vv(0), p.free, stop=False)
                    m = mm("ml_num", o, s["W"][1][:, h], vv(1), start=False)
            ps.append(p)
        s["users"].append(m)
        s["left"] -= 1
        if s["left"] == 0:
            for b in s["WT"]:
                give(b, s["users"])
        give(v, m)
        yield True
        hA = yield from take()
        for i in range(NT):
            for hh in range(2):
                q = func("ml_square", ACT.Square, hA.t[:, 0:ML_DV], ps[i].t[:, hh * ML_DV:(hh + 1) * ML_DV], m,
                         s["tinv"], hA.free, scale=s["inv"][:, i, h0 + hh:h0 + hh + 1], accum_out=ssq[:, i, hh:hh + 1])
                hA.free = [q]
        e = rsqrt("ml_rsqrt", rr.rearrange("p t h -> p (t h)"), ssq.rearrange("p t h -> p (t h)"), 1.0 / ML_DV, q)
        e = stt("ml_factor", fac, rr, 0.25, s["inv"][:, :, h0:h0 + 2], ALU.mult, ALU.mult, e)
        yield True
        (g, tg), = yield from need(f"mg{pr}")
        for i in range(NT):
            for hh in range(2):
                sl = slice(i * NC + hh * ML_DV, i * NC + (hh + 1) * ML_DV)
                e2 = stt("ml_gated", hA.t[:, sl], ps[i].t[:, hh * ML_DV:(hh + 1) * ML_DV], fac[:, i, hh:hh + 1],
                         g.t[:, sl], ALU.mult, ALU.mult, e, tg, q)
            done_with(ps[i], e2)
        give(g, e2)
        yield True
        th = []
        for c in range(0, 4, 2):
            p = yield from bank()
            for cc in range(2):
                for i in range(NT):
                    m = turn("ml_out", p.t[:, cc * T + i * P:cc * T + (i + 1) * P],
                             hA.t[:, i * NC + (c + cc) * P:i * NC + (c + cc + 1) * P], e2, p.free)
            for cc in range(2):
                k = pr * 4 + c + cc
                th.append(copy(act, "ml_out", acts[:, k, :], p.t[:, cc * T:(cc + 1) * T], m, acts_free,
                               scale=wcol[:, W_ML + k:W_ML + k + 1]))
            done_with(p, th)
            yield True
        give(hA, m)
        ha_ready[pr] = th

    def keep_tanh(key):
        def done(pair, t):
            b = yield from take()
            for i in range(NT):
                e = func("half_tanh", ACT.Tanh, b.t[:, i * NC:(i + 1) * NC], pair.t[i][:, :], t, b.free, scale=0.5)
            pair.free = [e]
            got[key] = (b, [e])
            yield True
        return done

    def mlstm_gate(pr):
        def done(pair, t):
            yield from keep_silu2(f"mzz{pr}")(pair, t)
            (z, tz), (o, to) = yield from need(f"mzz{pr}", f"mo{pr}")
            e = stt("ml_gate", z.t, o.t, 1.0, z.t, ALU.add, ALU.mult, tz, to)
            give(o, e)
            got[f"mg{pr}"] = (z, [e])
            gens.append(mlstm_out(pr))
            yield True
        return done

    jobs = [Job(load_gates, list(range(KD // CH)), 48, gates_done, lhs=lambda k: (xhi[:, k], xlo[:, k]),
                ready=lambda k: x_ready["u1"][k:k + 2] if "u1" in x_ready else None)]

    def j1(c0, done):
        jobs.append(product(w_in, c0, done, "u1"))

    def dn_jobs(g):
        j1(C_DK + g * NC, keep(f"dk{g}", then=lambda: conv(f"dk{g}", DN_W // P + 4 * g)))
        j1(C_DQ + g * NC, keep(f"dq{g}", then=lambda: conv(f"dq{g}", 4 * g)))
        j1(C_DV + g * NC, keep(f"dv{g}", then=lambda: conv(f"dv{g}", 2 * DN_W // P + 4 * g)))
        j1(C_DZ + g * NC, keep_silu2(f"dz{g}", then=lambda: delta(g)))

    def ml_qk(G):
        j1(C_MQ + G * NC, keep(f"mq{G}"))
        j1(C_MK + G * NC, keep(f"mk{G}", then=lambda: mlstm_scores(G)))

    def ml_pair(pr):
        j1(C_MV + pr * NC, keep(f"mv{pr}"))
        j1(C_MO + pr * NC, keep_tanh(f"mo{pr}"))
        j1(C_MZ + pr * NC, mlstm_gate(pr))

    dn_jobs(0)
    ml_qk(0)
    ml_pair(0)
    dn_jobs(1)
    ml_pair(1)
    dn_jobs(2)
    ml_qk(1)
    ml_pair(2)
    dn_jobs(3)
    ml_pair(3)

    resid = {}
    acc1 = small(NT * (D // NC)).rearrange("p (t n) -> p t n", t=NT)
    sums1 = []

    def gated(n, which):
        def done(pair, t):
            (g, tg), = yield from need(f"g{which}{n}")
            for i in range(NT):
                s = slice(i * NC, (i + 1) * NC)
                e = stt("out_gated", g.t[:, s], g.t[:, s], 1.0, pair.t[i][:, :], ALU.add, ALU.mult, tg, t)
            pair.free = [e]
            if which == "b":
                got[f"yb{n}"] = (g, [e])
                yield True
                return
            (b, tb), = yield from need(f"yb{n}")
            x = yield from take()
            tx = load(f"x{n}", x.t.rearrange("p (t n) -> p t n", t=NT),
                      a["x"][0, :, n * NC:(n + 1) * NC].rearrange("(t p) n -> p t n", p=P), x.free, q=act)
            e = tt(pool, "out_sum", b.t, b.t, g.t, ALU.add, e, tb)
            give(g, e)
            yield True
            e = stt("out_resid", x.t, b.t, 0.5, x.t, ALU.mult, ALU.add, e, tx)
            give(b, e)
            resid[n] = (x, [e])
            sums1.append((yield from square_sums(n, x, acc1, e)))
            yield True
        return done

    def out_job(n, k0, ready, done):
        return Job(columns(w_out, n * NC), list(range(k0 // CH, (k0 + KD) // CH)), NC, done,
                   split=lambda k: acts[:, k:k + 2, :],
                   ready=ready)

    for n in range(D // NC):
        j1(C_GB + n * NC, keep_tanh(f"gb{n}"))
        jobs.append(out_job(n, KD, lambda k: hb_ready.get((k - KD) // 4), gated(n, "b")))
        j1(C_GA + n * NC, keep_tanh(f"ga{n}"))
        jobs.append(out_job(n, 0, lambda k: ha_ready.get(k // 4), gated(n, "a")))

    w2 = a["w_in_2"][0]
    x2_dram = nc.dram_tensor("x2", (P, NT, D), F32, kind="Internal").ap()
    kept = {}

    def second_norm():
        while len(resid) < D // NC or len(sums1) < D // NC:
            yield False
        last_use = state["last"]
        acts_free[:] = [last_use]
        r, t = norm_scale(acc1, sums1)
        wb = (yield from take_some(2))
        tw = [load(f"final_norm{i}", wb[i].t, a["final_norm_w"][i * BLK:(i + 1) * BLK].unsqueeze(0).broadcast_to([P, BLK]), wb[i].free)
              for i in range(2)]
        acc = small(NT * (D // NC)).rearrange("p (t n) -> p t n", t=NT)
        ss = []
        for n in range(D // NC):
            b, tb = resid[n]
            for i in range(NT):
                s = slice(i * NC, (i + 1) * NC)
                e = stt("x2", b.t[:, s], b.t[:, s], r[:, i:i + 1], wb[n // 2].t[:, (n % 2) * NC:(n % 2 + 1) * NC],
                        ALU.mult, ALU.mult, tb, t, tw[n // 2])
            resid[n] = (b, [e])
            ss.append((yield from square_sums(n, b, acc, e)))
        for b in wb:
            give(b, e)
        for n in range(D // NC):
            b, tb = resid[n]
            kept[n] = load(f"x2_store{n}", x2_dram[:, :, n * NC:(n + 1) * NC], b.t.rearrange("p (t n) -> p t n", t=NT), tb, q=sp)
        r, t = norm_scale(acc, ss)
        yield from norm_turn("u2", [resid[n][0] for n in range(D // NC)], r, W_ATT, [last_use], t)
        for n in range(D // NC):
            give(resid[n][0], x_ready["u2"], kept[n])
        resid.clear()

    H = acts[:, KD:2 * KD, :].rearrange("p k t -> p (k t)")
    line_dram = nc.dram_tensor("rel_line", (AT_H, 2 * T), F32, kind="Internal").ap()
    Hv = H[:, 0:8 * BAND].rearrange("p (h j) -> p h j", h=8)
    hband = {}

    def rel_line():
        b = yield from take()
        o = yield from take()
        tab, hot = b.t[0:33, 0:AT_H], o.t[0:33, 0:2 * T]
        t0 = dve.do("rel_ones", lambda e: e.memset(b.t[32:33, 0:AT_H], 1.0), b.free)
        t1 = load("rel_table", b.t[0:32, 0:AT_H], a["rel_bias_table_2"][:, :], b.free)
        t2 = load("rel_hot", hot, a["const_rel"][:, :], o.free)
        p = yield from bank()
        m = mm("rel_line", p.t[0:AT_H, :], tab, hot, t0, t1, t2, p.free)
        e = copy(dve, "rel_line", b.t[0:AT_H, NC:2 * NC], p.t[0:AT_H, :], m)
        done_with(p, e)
        give(o, m)
        e = load("rel_store", line_dram[:, :], b.t[0:AT_H, NC:2 * NC], e)
        give(b, e)
        hband["stored"] = e
        yield True

    def load_band(half, *after):
        src = bass.AP(tensor=line_dram.tensor, offset=half * 8 * 2 * T, ap=[[1, P], [2 * T, 8], [1, BAND]])
        hband[half] = load(f"rel_band{half}", Hv, src, hband["stored"], after)

    gens.append(rel_line())

    def second_constants():
        while "u2" not in x_ready:
            yield False
        t = load("second_constants", cst2[:, 0:4 * P], a["const_second"][:, :], state["last_first"])
        hband["c2"] = t
        while "stored" not in hband:
            yield False
        load_band(0, acts_free)
        yield True

    at_ready = {}

    def attention(half):
        (qr, tq), (kr, tk), (v, tv) = yield from need(f"aq{half}", f"ak{half}", f"av{half}")
        qT, tq = yield from to_channels(qr, tq, scale=AT_D ** -0.5)
        kT, tk = yield from to_channels(kr, tk)
        while half not in hband:
            yield False
        o = yield from take()
        ov = o.t.rearrange("p (t h d) -> p t h d", t=NT, h=8)
        t_o = []
        po = None
        sums = small(NT * 8).rearrange("p (h t) -> p h t", t=NT)
        for h in range(8):
            c, base = h // 2, (h % 2) * AT_D
            rows_ = slice(base, base + AT_D)
            p = yield from bank()
            for i in range(NT):
                mm("at_logits", p.t[:, i * T:(i + 1) * T], qT.t[rows_, c * T + i * P:c * T + (i + 1) * P],
                   kT.t[rows_, c * T:(c + 1) * T], tq, tk, p.free, stop=False)
                m = mm("at_logits", p.t[:, i * T:(i + 1) * T], FLIP, Hv[:, h, P - i * P:P - i * P + T], hband[half],
                       hband["c2"], start=False)
            E = yield from take()
            mx, nm = small(NT), small(NT)
            e = reduce("at_max", mx, p.t[:, :].rearrange("p (i k) -> p i k", i=NT), ALU.max, m)
            e = ts("at_negmax", nm, mx, -1.0, ALU.mult, None, None, e)
            for i in range(NT):
                x = func("at_exp", ACT.Exp, E.t[:, i * T:(i + 1) * T], p.t[:, i * T:(i + 1) * T], e, E.free,
                         bias=nm[:, i:i + 1], accum_out=sums[:, h, i:i + 1])
            done_with(p, x)
            m_band = m
            yield True
            p = yield from bank()
            for kt_ in range(NT):
                for i in range(NT):
                    m = turn("at_turned", p.t[:, kt_ * T + i * P:kt_ * T + (i + 1) * P],
                             E.t[:, i * T + kt_ * P:i * T + (kt_ + 1) * P], x, p.free)
            e = copy(dve, "at_turned", E.t[:, NC:2 * NC], p.t[:, :], m)
            done_with(p, e)
            yield True
            if h % 4 == 0:
                po = yield from bank()
            for i in range(NT):
                for kt_ in range(NT):
                    m = mm("at_pv", po.t[:, ((h % 4) * NT + i) * AT_D:((h % 4) * NT + i + 1) * AT_D],
                           E.t[:, NC + kt_ * T + i * P:NC + kt_ * T + (i + 1) * P],
                           v.t[:, kt_ * NC + h * AT_D:kt_ * NC + (h + 1) * AT_D], e, tv, po.free,
                           start=kt_ == 0, stop=kt_ == 1)
            give(E, m)
            if h % 4 == 3:
                inv = small(NT * 4).rearrange("p (h t) -> p h t", t=NT)
                e = dve.do("at_inv", lambda q, inv=inv, s=sums[:, h - 3:h + 1]: q.reciprocal(inv, s), x)
                for i in range(NT):
                    pv = po.t[:, :].rearrange("p (h t d) -> p h t d", h=4, t=NT)[:, :, i]
                    t_o.append(tt(dve, "at_out", ov[:, i, h - 3:h + 1], pv, over(inv[:, :, i], 2, AT_D), ALU.mult,
                                  m, e, o.free))
                done_with(po, t_o)
            yield True
        give(qT, m)
        give(kT, m)
        give(v, m)
        if half == 0:
            load_band(1, m_band)
        th = []
        for c in range(0, 4, 2):
            p = yield from bank()
            for cc in range(2):
                for i in range(NT):
                    m = turn("at_out", p.t[:, cc * T + i * P:cc * T + (i + 1) * P],
                             o.t[:, i * NC + (c + cc) * P:i * NC + (c + cc + 1) * P], t_o, p.free)
            th.append(copy(act, "at_out", acts[:, 4 * half + c:4 * half + c + 2, :],
                           p.t[:, :].rearrange("p (c t) -> p c t", c=2), m, acts_free))
            done_with(p, th)
            yield True
        give(o, m)
        at_ready[half] = th

    gl = {}
    NCH = T // GL_C

    def gla_gates(pair, t):
        b = yield from take()
        bv = b.t[:, 0:64].rearrange("p (t n) -> p t n", t=NT)
        for i in range(NT):
            e = copy(dve, "gla_rank", bv[:, i], pair.t[i][:, 0:32], t, b.free)
        pair.free = [e]
        w = yield from take()
        wv = w.t[0:GL_R, :].rearrange("p (d n) -> p d n", d=2)
        bi = yield from take()
        biv = bi.t[0:1, :].rearrange("p (d n) -> p d n", d=2)
        for d_, s in enumerate(("fwd", "bwd")):
            tl = (load("gla_gate_w", wv[:, d_], a[f"gla_gate_w_{s}_2"][0], w.free))
            tl = load("gla_gate_w", biv[:, d_], a[f"gla_gate_b_{s}_2"], bi.free)
        p = yield from bank()
        for d_ in range(2):
            for i in range(NT):
                m = turn("gla_rank", p.t[0:GL_R, d_ * T + i * P:d_ * T + (i + 1) * P],
                         bv[:, i, d_ * GL_R:(d_ + 1) * GL_R], e, p.free)
        lr = b.t[0:GL_R, NC:2 * NC]
        e = copy(dve, "gla_rank", lr, p.t[0:GL_R, :], m)
        done_with(p, e)
        yield True
        la = (yield from take_some(2))
        tla = []
        for d_ in range(2):
            for i in range(NT):
                p = yield from bank()
                mm("gla_gate", p.t[:, :], lr[:, d_ * T + i * P:d_ * T + (i + 1) * P], wv[:, d_], e, tl, p.free, stop=False)
                m = mm("gla_gate", p.t[:, :], ONE[0:1, :], biv[:, d_], start=False)
                o = la[d_].t[:, i * NC:(i + 1) * NC]
                x = func("gla_abs", ACT.Abs, o, p.t[:, :], m, la[d_].free)
                x = func("gla_exp", ACT.Exp, o, o, x, scale=-1.0)
                x = func("gla_ln", ACT.Ln, o, o, x, bias=1.0)
                x = stt("gla_log", o, p.t[:, :], 0.0, o, ALU.min, ALU.subtract, x)
                done_with(p, x)
                tla.append(x)
                yield True
        give(b, m)
        give(w, m)
        give(bi, m)
        gl["la"] = (la, tla)

    def gla(hp):
        if hp == 0:
            (qr, tq), (kr, tk) = yield from need("gq", "gk")
            qT, tq = yield from to_channels(qr, tq, scale=GL_DK ** -0.5)
            kT, tk = yield from to_channels(kr, tk)
            gl["qk"] = (qT, kT, tq, tk)
        while "qk" not in gl or "la" not in gl or "c2" not in hband:
            yield False
        qT, kT, tq, tk = gl["qk"]
        la, tla = gl["la"]
        (v, tv), = yield from need(f"gv{hp}")
        cols = slice(2 * hp * T, (2 * hp + 2) * T)
        q_in, k_in, kend = (yield from take()), (yield from take()), (yield from take())
        dec = small(2 * 2 * NCH).rearrange("p (d h c) -> p d h c", d=2, h=2)
        t_in, t_ke, t_dec = [], [], []
        for d_ in range(2):
            p = yield from bank()
            for hh in range(2):
                for i in range(NT):
                    h = 2 * hp + hh
                    m = mm("gla_sum", p.t[:, hh * T + i * P:hh * T + (i + 1) * P],
                           la[d_].t[:, i * NC + h * P:i * NC + (h + 1) * P], (CUMF, CUMB)[d_], tla, hband["c2"], p.free)
            pc = p.t[:, :].rearrange("p (h c t) -> p h c t", h=2, c=NCH)
            end = GL_C - 1 if d_ == 0 else 0
            gend = small(2 * NCH)
            e = copy(dve, "gla_end", gend, p.t[:, end::GL_C], m)
            t_dec.append(func("gla_dec", ACT.Exp, dec[:, d_].rearrange("p h c -> p (h c)"), gend, e, scale=1.0 / GL_TAU))
            s = slice(d_ * NC, (d_ + 1) * NC)
            x1 = func("gla_eq", ACT.Exp, q_in.t[:, s], p.t[:, :], e, q_in.free, scale=1.0 / GL_TAU)
            x2 = func("gla_eq", ACT.Exp, k_in.t[:, s], p.t[:, :], e, k_in.free, scale=-1.0 / GL_TAU)
            x3 = tt(dve, "gla_rest", kend.t[:, s].rearrange("p (g t) -> p g t", t=GL_C), over(gend, 2, GL_C),
                    p.t[:, :].rearrange("p (g t) -> p g t", t=GL_C), ALU.subtract, x2, kend.free)
            done_with(p, x1, x2, x3)
            x3 = func("gla_eq", ACT.Exp, kend.t[:, s], kend.t[:, s], x3, scale=1.0 / GL_TAU)
            t_in.append(tt(dve, "gla_q_in", q_in.t[:, s], q_in.t[:, s], qT.t[:, cols], ALU.mult, x1, tq))
            t_in.append(tt(dve, "gla_k_in", k_in.t[:, s], k_in.t[:, s], kT.t[:, cols], ALU.mult, x2, tk))
            t_ke.append(tt(dve, "gla_k_end", kend.t[:, s], kend.t[:, s], kT.t[:, cols], ALU.mult, x3, tk))
            yield True
        if hp == 1:
            give(qT, t_in, t_ke)
            give(kT, t_in, t_ke)
            for b in la:
                give(b, m)
        p = yield from bank()
        pa = p.t[:, :].rearrange("p (d h t c) -> p d h t c", d=2, h=2, t=NT)
        for d_ in range(2):
            for hh in range(2):
                for n in range(NCH):
                    b0 = (n % 2) * GL_C
                    at_ = slice(d_ * NC + hh * T + n * GL_C, d_ * NC + hh * T + (n + 1) * GL_C)
                    m = mm("gla_scores", pa[b0:b0 + GL_C, d_, hh, n // 2], k_in.t[:, at_], q_in.t[:, at_], t_in, p.free)
        give(k_in, m)
        S = yield from take_some(2)
        Sv = [b.t[:, 0:3 * GL_DV].rearrange("p (n v) -> p n v", n=3) for b in S]
        Av = [b.t[:, 3 * GL_DV:BLK].rearrange("p (g c) -> p g c", c=GL_C) for b in S]
        x = [tt(dve, "gla_masked", Av[d_], p.t[:, d_ * 256:(d_ + 1) * 256].rearrange("p (g c) -> p g c", c=GL_C),
                over((MASKF, MASKB)[d_], 1, 2 * NT), ALU.mult, m, S[d_].free) for d_ in range(2)]
        done_with(p, x)
        t_A = tt(dve, "gla_masked", Av[0], Av[0], Av[1], ALU.add, x)
        yield True
        ke = yield from take()
        kev = ke.t.rearrange("p (d h t k) -> p d h t k", d=2, h=2, t=NT)
        t_k = []
        for d_ in range(2):
            p = yield from bank()
            for hh in range(2):
                for i in range(NT):
                    m = turn("gla_k_end", p.t[:, (hh * NT + i) * P:(hh * NT + i + 1) * P],
                             kend.t[:, d_ * NC + hh * T + i * P:d_ * NC + hh * T + (i + 1) * P], t_ke, p.free)
            t_k.append(copy(act, "gla_k_end", ke.t[:, d_ * NC:(d_ + 1) * NC], p.t[:, :], m, ke.free))
            done_with(p, t_k)
            yield True
        give(kend, m)
        pos = []
        ssq = small(2 * NT).rearrange("p (h t) -> p h t", t=NT)
        go = yield from take()
        for i in range(NT):
            pos.append((yield from bank()))
        m_o = None
        for hh in range(2):
            t_S = [[None] * 3, [None] * 3]
            for d_ in range(2):
                order = range(3) if d_ == 0 else range(3, 0, -1)
                for z, n in enumerate(order):
                    b0 = (n % 2) * GL_C
                    p = yield from bank()
                    m = mm("gla_state", p.t[:, 0:GL_DV], kev[b0:b0 + GL_C, d_, hh, n // 2],
                           v.t[b0:b0 + GL_C, (n // 2) * NC + hh * GL_DV:(n // 2) * NC + (hh + 1) * GL_DV], t_k, tv, p.free)
                    if z == 0:
                        e = copy(dve, "gla_state", Sv[d_][:, 0], p.t[:, 0:GL_DV], m, S[d_].free)
                    else:
                        e = stt("gla_state", Sv[d_][:, z], Sv[d_][:, z - 1], dec[:, d_, hh, n:n + 1], p.t[:, 0:GL_DV],
                                ALU.mult, ALU.add, m, e, t_dec, S[d_].free)
                    done_with(p, e)
                    t_S[d_][z] = e
                    yield True
            for n in range(NCH):
                b0 = (n % 2) * GL_C
                o = pos[n // 2].t[b0:b0 + GL_C, hh * GL_DV:(hh + 1) * GL_DV]
                fr = pos[n // 2].free
                terms = [(Av[0][b0:b0 + GL_C, hh * NT + n // 2, :],
                          v.t[b0:b0 + GL_C, (n // 2) * NC + hh * GL_DV:(n // 2) * NC + (hh + 1) * GL_DV])]
                at_ = lambda d_: slice(d_ * NC + hh * T + n * GL_C, d_ * NC + hh * T + (n + 1) * GL_C)
                if n > 0:
                    terms.append((q_in.t[:, at_(0)], Sv[0][:, n - 1]))
                if n < NCH - 1:
                    terms.append((q_in.t[:, at_(1)], Sv[1][:, NCH - 2 - n]))
                for z, (l, r) in enumerate(terms):
                    m_o = mm("gla_o", o, l, r, t_A, t_S, fr, start=z == 0, stop=z == len(terms) - 1)
            S[0].free, S[1].free = [m_o], [m_o]
            yield True
        for b in (ke, q_in, v, *S):
            give(b, m_o)
        for i in range(NT):
            for hh in range(2):
                x = func("gla_square", ACT.Square, go.t[:, 0:GL_DV], pos[i].t[:, hh * GL_DV:(hh + 1) * GL_DV], m_o,
                         go.free, accum_out=ssq[:, hh, i:i + 1])
                go.free = [x]
        rr = small(2 * NT).rearrange("p (h t) -> p h t", t=NT)
        e = rsqrt("gla_rsqrt", rr.rearrange("p h t -> p (h t)"), ssq.rearrange("p h t -> p (h t)"), 1.0 / GL_DV, x)
        e = ts("gla_factor", rr, rr, 0.5, ALU.mult, None, None, e)
        yield True
        (g, tg), = yield from need(f"gr{hp}")
        for i in range(NT):
            for hh in range(2):
                s = slice(i * NC + hh * GL_DV, i * NC + (hh + 1) * GL_DV)
                e2 = stt("gla_gated", go.t[:, s], pos[i].t[:, hh * GL_DV:(hh + 1) * GL_DV], rr[:, hh, i:i + 1],
                         g.t[:, s], ALU.mult, ALU.mult, e, tg, x)
            done_with(pos[i], e2)
        give(g, e2)
        yield True
        th = []
        for c in range(0, 4, 2):
            p = yield from bank()
            for cc in range(2):
                for i in range(NT):
                    m = turn("gla_out", p.t[:, cc * T + i * P:cc * T + (i + 1) * P],
                             go.t[:, i * NC + (c + cc) * P:i * NC + (c + cc + 1) * P], e2, p.free)
            for cc in range(2):
                k = hp * 4 + c + cc
                th.append(copy(act, "gla_out", acts[:, 8 + k, :], p.t[:, cc * T:(cc + 1) * T], m, acts_free,
                               scale=wcol[:, W_GLA + k:W_GLA + k + 1]))
            done_with(p, th)
            yield True
        give(go, m)
        at_ready[2 + hp] = th

    def j2(c0, done, n=NC):
        jobs.append(product(w2, c0, done, "u2", n))

    j2(C_GL, gla_gates, 2 * GL_R)
    j2(C_GQ, keep("gq"))
    j2(C_GK, keep("gk"))
    j2(C_GV, keep("gv0", then=lambda: gla(0)))
    j2(C_GR, keep_silu2("gr0"))
    j2(C_AQ, keep("aq0"))
    j2(C_AK, keep("ak0"))
    j2(C_AV, keep("av0", then=lambda: attention(0)))
    j2(C_AQ + NC, keep("aq1"))
    j2(C_AK + NC, keep("ak1"))
    j2(C_AV + NC, keep("av1", then=lambda: attention(1)))
    j2(C_GV + NC, keep("gv1", then=lambda: gla(1)))
    j2(C_GR + NC, keep_silu2("gr1"))

    acc3 = small(NT * (D // NC)).rearrange("p (t n) -> p t n", t=NT)
    acc4 = small(NT * (D // NC)).rearrange("p (t n) -> p t n", t=NT)
    sums3, sums4 = [], []

    def add_resid(n, acc, sums):
        def done(pair, t):
            if n not in resid:
                b = yield from take()
                resid[n] = (b, [load(f"x2_load{n}", b.t.rearrange("p (t n) -> p t n", t=NT),
                                     x2_dram[:, :, n * NC:(n + 1) * NC], b.free, kept[n])])
            b, tb = resid[n]
            for i in range(NT):
                s = slice(i * NC, (i + 1) * NC)
                e = tt(dve, "resid", b.t[:, s], b.t[:, s], pair.t[i][:, :], ALU.add, t, tb)
            pair.free = [e]
            resid[n] = (b, [e])
            yield True
            sums.append((yield from square_sums(n, b, acc, e)))
        return done

    for n in range(D // NC):
        jobs.append(Job(columns(a["w_out_2"][0], n * NC), [0, 2, 1, 3], NC, add_resid(n, acc3, sums3),
                        split=lambda k: acts[:, k:k + 2, :], ready=lambda k: at_ready.get(k // 4)))

    def third_norm():
        while len(sums3) < D // NC:
            yield False
        last_use = state["last"]
        acts_free[:] = [last_use]
        r, t = norm_scale(acc3, sums3)
        yield from norm_turn("u3", [resid[n][0] for n in range(D // NC)], r, W_FFN, [last_use], t)
        got_tail = []
        for b in tail:
            while b not in free_blocks:
                yield False
            free_blocks.remove(b)
            got_tail.append(b.free)
        acts_free.append(got_tail)
        state["tail"] = True

    ffn_ready = {}

    def ffn_up(n):
        def done(pair, t):
            (g, tg), = yield from need(f"fg{n}")
            for i in range(NT):
                s = slice(i * NC, (i + 1) * NC)
                e = stt("ffn_act", g.t[:, s], g.t[:, s], 0.5, pair.t[i][:, :], ALU.mult, ALU.mult, t, tg)
            pair.free = [e]
            yield True
            while "tail" not in state:
                yield False
            th = []
            for c in range(0, 4, 2):
                p = yield from bank()
                for cc in range(2):
                    for i in range(NT):
                        m = turn("ffn_act", p.t[:, cc * T + i * P:cc * T + (i + 1) * P],
                                 g.t[:, i * NC + (c + cc) * P:i * NC + (c + cc + 1) * P], e, p.free)
                k = 4 * n + c
                th.append(copy((act, dve)[c // 2], "ffn_act", acts_all[:, k:k + 2, :],
                               p.t[:, :].rearrange("p (c t) -> p c t", c=2), m, acts_free))
                done_with(p, th[-1])
                yield True
            give(g, m)
            ffn_ready[n] = th
        return done

    for n in range(FFN // NC):
        jobs.append(product(a["w_gate_2"][0], n * NC, keep_silu2(f"fg{n}"), "u3"))
        jobs.append(product(a["w_up_2"][0], n * NC, ffn_up(n), "u3"))
    for n in range(D // NC):
        jobs.append(Job(columns(a["w_down_2"][0], n * NC), list(range(KF // CH)), NC, add_resid(n, acc4, sums4),
                        split=lambda k: acts_all[:, k:k + 2, :], ready=lambda k: ffn_ready.get(k // 4)))

    def last_norm():
        while "tail" not in state:
            yield False
        wb = (yield from take_some(2))
        tw = [load(f"final_norm2_{i}", wb[i].t, a["final_norm_w_2"][i * BLK:(i + 1) * BLK].unsqueeze(0).broadcast_to([P, BLK]), wb[i].free)
              for i in range(2)]
        while len(sums4) < D // NC:
            yield False
        r, t = norm_scale(acc4, sums4)
        for n in range(D // NC):
            b, tb = resid[n]
            for i in range(NT):
                s = slice(i * NC, (i + 1) * NC)
                e = stt("final", b.t[:, s], b.t[:, s], r[:, i:i + 1], wb[n // 2].t[:, (n % 2) * NC:(n % 2 + 1) * NC],
                        ALU.mult, ALU.mult, tb, t, tw[n // 2])
            stored.append(load(f"store{n}", out[0, :, n * NC:(n + 1) * NC].rearrange("(t p) n -> p t n", p=P),
                               b.t.rearrange("p (t n) -> p t n", t=NT), e, q=sp))

    stored = []

    def background():
        yield from second_norm()
        state["last_first"] = state["last"]
        yield from second_constants()
        yield from third_norm()
        yield from last_norm()

    def beside():
        g = background()
        while True:
            try:
                r = next(g)
            except StopIteration:
                return
            yield r

    urgent.append(beside())
    run_jobs(jobs)
    settle(lambda: len(stored) == D // NC and not gens)

    block = ctx.enter_context(nc.Block())

    @block.sync
    def _(e):
        sp.play(e)
        for t in stored:
            e.wait_ge(t.sem, t.value)

    @block.tensor
    def _(e):
        pe.play(e)

    @block.scalar
    def _(e):
        act.play(e)

    @block.vector
    def _(e):
        dve.play(e)

    @block.gpsimd
    def _(e):
        pool.play(e)


_INS = ["x", "norm_w", "w_in", "ml_i_bias", "ml_f_bias", "ml_norm_w", "dn_conv_w", "dn_a_log", "dn_dt_bias",
        "dn_norm_w", "w_out", "final_norm_w", "attn_norm_w_2", "w_in_2", "rel_bias_table_2", "gla_gate_w_fwd_2",
        "gla_gate_b_fwd_2", "gla_gate_w_bwd_2", "gla_gate_b_bwd_2", "gla_norm_w_2", "w_out_2", "ffn_norm_w_2",
        "w_gate_2", "w_up_2", "w_down_2", "final_norm_w_2"]


def kernel(**inputs):
    import numpy as _np
    import concourse.bacc as _bacc
    from concourse import mybir as _mybir
    from concourse.bass_utils import run_bass_kernel_spmd as _run

    nc = _bacc.Bacc("TRN2", target_bir_lowering=False, num_devices=1)
    given = {n: inputs[n] for n in _INS}
    given.update(host_constants())
    arrays, args = {}, {}
    for name, value in given.items():
        v = _np.ascontiguousarray(value)
        arrays[f"in_{name}_dram"] = v
        args[name] = nc.dram_tensor(f"in_{name}_dram", v.shape, _mybir.dt.from_np(v.dtype), kind="ExternalInput").ap()
    out = nc.dram_tensor("out_0_dram", (1, T, D), _mybir.dt.float32, kind="ExternalOutput").ap()
    build(nc, args, out)
    r = _run(nc, [arrays], core_ids=[0])
    return r.results[0]["out_0_dram"]
```

```python
from contextlib import ExitStack

import numpy as np
import concourse.bass as bass
from concourse import mybir

F32 = mybir.dt.float32
F32R = mybir.dt.float32r
ACT = mybir.ActivationFunctionType
ALU = mybir.AluOpType
AX = mybir.AxisListType.X

P = 128
T = 256
NT = T // P
D = 2048
KD = D // P
NC = 512
EPS = 1e-6

ML_H, ML_DK, ML_DV = 8, 128, 256
DN_H, DN_D = 16, 128
DN_W = DN_H * DN_D
CONV = 4
CAP = 15.0
C_MQ = 0
C_MK = C_MQ + ML_H * ML_DK
C_MV = C_MK + ML_H * ML_DK
C_MO = C_MV + ML_H * ML_DV
C_MZ = C_MO + ML_H * ML_DV
C_MI = C_MZ + ML_H * ML_DV
C_DQ = C_MI + 2 * ML_H
C_DK = C_DQ + DN_W
C_DV = C_DK + DN_W
C_DZ = C_DV + DN_W
C_DB = C_DZ + DN_W
C_GA = C_DB + 2 * DN_H
C_GB = C_GA + D

AT_H, AT_D = 16, 64
GL_H, GL_DK, GL_DV, GL_R, GL_C = 4, 128, 256, 16, 64
GL_TAU = 16.0
C_AQ = 0
C_AK = C_AQ + AT_H * AT_D
C_AV = C_AK + AT_H * AT_D
C_GQ = C_AV + AT_H * AT_D
C_GK = C_GQ + GL_H * GL_DK
C_GV = C_GK + GL_H * GL_DK
C_GR = C_GV + GL_H * GL_DV
C_GL = C_GR + GL_H * GL_DV
FFN = 5632
KF = FFN // P

CH = 4
RAW = 3
RING = 4
AHEAD = 3
LAHEAD = 2
LRING = LAHEAD + 1
NBLK = 15
BLK = 1024
NEG = -1e30
LEVELS = 7
BAND = 3 * P


def host_constants():
    r = np.arange(P)[:, None]
    c = np.arange(P)[None, :]
    f = np.float32
    base = [(r == c), (r > c), (r <= c), np.ones((P, P))]
    levels = []
    for l in range(LEVELS):
        w = 2 << l
        levels.append((r // w == c // w) & (r % w < w // 2) & (c % w >= w // 2))
    first = base + levels + [np.where(c > r, NEG, 0.0)]
    same = r // GL_C == c // GL_C
    h = np.arange(GL_C)[None, :]
    second = [same & (r <= c), same & (r >= c), r + c == P - 1,
              np.concatenate([r % GL_C <= h, r % GL_C >= h], axis=1)]
    rel = np.arange(2 * T) - (T - 1)
    half, exact, far = 16, 8, 1024
    n = np.abs(rel)
    large = exact + (np.log(np.maximum(n, 1) / exact) / np.log(far / exact) * (half - exact)).astype(np.int64)
    bucket = np.where(rel > 0, half, 0) + np.where(n < exact, n, np.minimum(large, half - 1))
    times = (n <= 64).astype(np.int64) + (n % 4 == 0) + (n % 16 == 0)
    hot = np.zeros((33, 2 * T), f)
    hot[bucket, np.arange(2 * T)] = 1.0
    hot[32] = np.where(times > 0, np.log(np.maximum(times, 1)), NEG)
    return {"const_first": np.concatenate([np.asarray(m, f) for m in first], axis=1),
            "const_second": np.concatenate([np.asarray(m, f) for m in second], axis=1),
            "const_rel": hot}


class Token:

    def __init__(self, sem, value):
        self.sem, self.value = sem, value


def flat(tokens):
    for t in tokens:
        if isinstance(t, (list, tuple)):
            yield from flat(t)
        elif t is not None:
            yield t


class Queue:

    def __init__(self, nc, ctx, name):
        self.nc, self.ctx, self.name = nc, ctx, name
        self.items, self.sems, self.seen = [], {}, {}

    def do(self, stage, fn, *after, inc=1):
        waits = []
        for t in flat(after):
            if self.seen.get(id(t.sem), 0) < t.value:
                self.seen[id(t.sem)] = t.value
                waits.append((t.sem, t.value))
        if stage is None:
            self.items.append((waits, fn, None, 0))
            return None
        if inc == 1:
            stage = stage.split("_")[0]
        if stage not in self.sems:
            self.sems[stage] = [self.ctx.enter_context(self.nc.semaphore(f"{self.name}_{stage}")), 0]
        s = self.sems[stage]
        s[1] += inc
        self.items.append((waits, fn, s[0], inc))
        return Token(s[0], s[1])

    def play(self, eng):
        for waits, fn, sem, inc in self.items:
            for s, v in waits:
                eng.wait_ge(s, v)
            ins = fn(eng)
            if sem is not None:
                ins.then_inc(sem, inc)


class Place:

    def __init__(self, t):
        self.t, self.free = t, []


def over(ap, axis, n):
    ap = ap.unsqueeze(axis)
    shape = list(ap.shape)
    shape[axis] = n
    return ap.broadcast_to(shape)


class Job:

    def __init__(self, load, chunks, n, done, lhs=None, split=None, ready=lambda k: [], key=None):
        self.load, self.chunks, self.n, self.done, self.key = load, chunks, n, done, key
        self.lhs, self.split, self.ready = lhs, split, ready


def build(nc, a, out):
    with ExitStack() as ctx:
        _build(nc, ctx, a, out)


def _build(nc, ctx, a, out):
    def sb(name, shape, dt=F32):
        return ctx.enter_context(nc.sbuf_tensor(name, shape, dt))

    pe, act, dve, pool, sp = (Queue(nc, ctx, n) for n in ("pe", "act", "dve", "pool", "sp"))

    raw = sb("weight_raw", [P, RAW, CH * NC])
    whi = sb("weight_hi", [P, RING, 2 * NC], F32R)
    wlo = sb("weight_lo", [P, RING, 2 * NC], F32R)
    lhi = sb("lhs_hi", [P, LRING, 2, T], F32R)
    llo = sb("lhs_lo", [P, LRING, 2, T], F32R)
    xhi = sb("x_hi", [P, KD, T], F32R)
    xlo = sb("x_lo", [P, KD, T], F32R)
    arena = sb("arena", [P, 2 * KD * T + NBLK * BLK])
    cst = sb("constants", [P, 4 * P])
    cst2 = sb("phase_constants", [P, (LEVELS + 1) * P])
    wcol = sb("norm_columns", [P, 112])
    cwcol = sb("conv_columns", [P, 2 * 96])
    gt = sb("gate_work", [P, 10, 2, 48])
    sm = sb("stats", [P, 900])

    acts = arena[:, 0:2 * KD * T].rearrange("p (k t) -> p k t", t=T)
    acts_all = arena[:, 0:KF * T].rearrange("p (k t) -> p k t", t=T)
    blocks = [Place(arena[:, 2 * KD * T + i * BLK:2 * KD * T + (i + 1) * BLK]) for i in range(NBLK)]
    tail = blocks[:3]
    free_blocks = list(blocks)
    acts_free = []

    IDN, STR, INC, ONE = (cst[:, i * P:(i + 1) * P] for i in range(4))
    LVL = [cst2[:, i * P:(i + 1) * P] for i in range(LEVELS)]
    NEGM = cst2[:, LEVELS * P:(LEVELS + 1) * P]
    CUMF, CUMB, FLIP = (cst2[:, i * P:(i + 1) * P] for i in range(3))
    MASKF, MASKB = cst2[:, 3 * P:3 * P + GL_C], cst2[:, 3 * P + GL_C:4 * P]

    pairs = [Place([ctx.enter_context(nc.psum_tensor(f"gemm_{i}_{j}", [P, NC], F32)) for j in range(NT)])
             for i in range(2)]
    banks = [Place(ctx.enter_context(nc.psum_tensor(f"side_{i}", [P, NC], F32))) for i in range(4)]
    free_banks = list(banks)

    def take(but=()):
        while not any(b not in but for b in free_blocks):
            yield False
        b = next(b for b in free_blocks if b not in but)
        free_blocks.remove(b)
        return b

    def take_some(n):
        r = []
        for _ in range(n):
            r.append((yield from take()))
        return r

    def give(b, *readers):
        b.free = [readers]
        free_blocks.append(b)

    def bank():
        while not free_banks:
            yield False
        return free_banks.pop(0)

    def done_with(b, *readers):
        b.free = [readers]
        free_banks.append(b)

    stat = [0]

    def small(n):
        assert stat[0] + n <= 900, stat
        stat[0] += n
        return sm[:, stat[0] - n:stat[0]]

    def copy(q, stage, o, i, *after, scale=None):
        if q is act:
            return act.do(stage, lambda e: e.activation(o, i, ACT.Copy, scale=1.0 if scale is None else scale), *after)
        return q.do(stage, lambda e: e.tensor_copy(o, i), *after)

    def func(stage, f, o, i, *after, **kw):
        return act.do(stage, lambda e: e.activation(o, i, f, **kw), *after)

    def tt(q, stage, o, x, y, op, *after):
        return q.do(stage, lambda e: e.tensor_tensor(o, x, y, op), *after)

    def ts(stage, o, x, s1, op0, s2, op1, *after):
        if op1 is None:
            return dve.do(stage, lambda e: e.tensor_scalar(o, x, s1, None, op0), *after)
        return dve.do(stage, lambda e: e.tensor_scalar(o, x, s1, s2, op0, op1), *after)

    def stt(stage, o, x, s, y, op0, op1, *after):
        return dve.do(stage, lambda e: e.scalar_tensor_tensor(out=o, in0=x, scalar=s, in1=y, op0=op0, op1=op1), *after)

    def reduce(stage, o, i, op, *after):
        return dve.do(stage, lambda e: e.tensor_reduce(o, i, AX, op), *after)

    def mm(stage, o, l, r, *after, start=True, stop=True):
        return pe.do(stage, lambda e: e.matmul(o, l, r, start=start, stop=stop), *after)

    def turn(stage, o, i, *after):
        n = i.shape[0]
        return pe.do(stage, lambda e: e.transpose(o, i, IDN[0:n, 0:n]), *after)

    def rsqrt(stage, o, i, mul, *after):
        n = list(i.shape)
        half = over(minus_half[:, 0:1], 2, n[2])[:, 0:1, :].broadcast_to(n) if len(n) == 3 else minus_half[:, 0:1].broadcast_to(n)
        t = ts(stage + "_mean", i, i, mul, ALU.mult, EPS, ALU.add, *after)
        return tt(pool, stage, o, i, half, ALU.pow, t, t_half)

    def load(stage, o, i, *after, q=None):
        return (q or act).do(stage, lambda e: e.dma_start(o, i), *after, inc=16)

    xblk = [free_blocks.pop(0) for _ in range(D // NC)]
    t_x = []
    for n in range(D // NC):
        t_x.append(load(f"x{n}", xblk[n].t.rearrange("p (t n) -> p t n", t=NT),
                        a["x"][0, :, n * NC:(n + 1) * NC].rearrange("(t p) n -> p t n", p=P), q=sp))
    t_c = load("constants", cst[:, :], a["const_first"][:, 0:4 * P])
    rows = free_blocks.pop(0)
    vrows, crows = rows.t[:, 0:P], [rows.t[0:96, (1 + i) * P:(2 + i) * P] for i in range(2)]
    at = 0
    W_NORM, W_ATT, W_FFN, W_ML, W_DN, W_GLA, W_FIN = 0, 16, 32, 48, 64, 65, 73
    for name in ("norm_w", "attn_norm_w_2", "ffn_norm_w_2", "ml_norm_w", "dn_norm_w", "gla_norm_w_2"):
        n = a[name].shape[1] // P
        t_v = load("norm_rows", vrows[at:at + n, :], a[name].rearrange("a (r p) -> (a r) p", p=P))
        at += n
    t_v = load("norm_rows", vrows[at:at + KD, :], a["final_norm_w"].rearrange("(r p) -> r p", p=P))
    NV = W_BOTH = at + KD
    cw = a["dn_conv_w"].rearrange("a j (r p) -> (a j r) p", p=P)
    for i in range(2):
        t_v = load("norm_rows", crows[i], cw[i * 96:(i + 1) * 96, :])
    gb = sb("gate_bias", [P, 48])
    for lo, n, name in ((0, 8, "ml_i_bias"), (8, 8, "ml_f_bias"), (16, 16, "dn_a_log"), (32, 16, "dn_dt_bias")):
        t_b = load("gate_bias", gb[:, lo:lo + n], a[name].broadcast_to([P, n]))
    t_c2 = load("phase_constants", cst2[:, :], a["const_first"][:, 4 * P:])
    minus_half = sb("minus_half", [P, 1])
    t_half = dve.do("minus_half", lambda e: e.memset(minus_half[:, :], -0.5))

    pvec = free_banks.pop(0)
    turn("norm_columns", pvec.t[:, 0:NV], vrows[0:NV, :], t_c, t_v)
    for i in range(2):
        t = turn("norm_columns", pvec.t[:, P + i * 96:P + (i + 1) * 96], crows[i])
    t_w = [copy(dve, "norm_columns", wcol[:, 0:NV], pvec.t[:, 0:NV], t),
           copy(dve, "norm_columns", cwcol[:, :], pvec.t[:, P:P + 192], t)]
    t_w.append(tt(dve, "norm_columns", wcol[:, W_BOTH:W_BOTH + KD], wcol[:, W_ATT:W_ATT + KD], wcol[:, W_FIN:W_FIN + KD],
                  ALU.mult, t_w))
    done_with(pvec, t_w)
    give(rows, t)

    x_ready = {}
    scales = {}
    uses = {}

    def square_sums(n, b, acc, *after):
        scratch = yield from bank()
        for i in range(NT):
            s = func("square_sum", ACT.Square, scratch.t[:, :], b.t[:, i * NC:(i + 1) * NC], after, scratch.free,
                     accum_out=acc[:, i, n:n + 1])
            scratch.free = [s]
        done_with(scratch, s)
        return s

    def norm_scale(acc, *after):
        total, r = small(NT), small(NT)
        t = reduce("norm_total", total, acc, ALU.add, *after)
        return r, rsqrt("norm_rsqrt", r, total, 1.0 / D, t)

    def set_scale(key, r, t):
        hr = small(NT)
        scales[key] = (r, hr, [t, ts("norm_half", hr, r, 0.5, ALU.mult, None, None, t)])

    def turn_block(key, before, n, b, wc, *after):
        while before is not None and uses[before][0]:
            yield False
        free = uses[before][1] if before is not None else []
        for c in range(0, NC // P, 2):
            p = yield from bank()
            for cc in range(2):
                for i in range(NT):
                    t = turn("norm_turned", p.t[:, cc * T + i * P:cc * T + (i + 1) * P],
                             b.t[:, i * NC + (c + cc) * P:i * NC + (c + cc + 1) * P], after, p.free, t_c)
            k0 = n * (NC // P) + c
            part = [(k, p.t[:, (k - k0) * T:(k - k0 + 1) * T], wcol[:, wc + k:wc + k + 1]) for k in (k0, k0 + 1)]
            for k, src, w in part:
                hi = func("x_hi", ACT.Copy, xhi[:, k, :], src, t, t_w, free, scale=w)
            for k, src, w in part:
                lo = stt("x_lo", xlo[:, k, :], src, w, xhi[:, k, :].bitcast(F32), ALU.mult, ALU.subtract, t, hi, free)
            done_with(p, hi, lo)
            x_ready[key, k0] = [hi, lo]
            yield True
        return t

    state = {"pair": 0, "heavy": False}
    gens = []
    urgent = []

    def stage_turn():
        while state["heavy"]:
            yield False
        state["heavy"] = True

    def stage_over():
        state["heavy"] = False

    def step_all(limit=4):
        moved = False
        for lst, lim in ((urgent, 99), (gens, limit)):
            for g in list(lst[:lim]):
                try:
                    moved |= next(g) is not False
                except StopIteration:
                    lst.remove(g)
                    moved = True
        return moved

    def settle(until):
        idle = 0
        while not until():
            idle = 0 if step_all(4) else idle + 1
            assert idle < 8, ("nothing moves", len(free_blocks), len(free_banks), sorted(got))

    def run_jobs(jobs):
        halves = [(j, c, h) for j in jobs for c in range(len(j.chunks)) for h in range(2)]
        state_w = {}
        state_l = {}
        chunk_of = []
        for idx, (j, c, h) in enumerate(halves):
            chunk_of.append(idx // 2)
        loaded = {}

        def load_chunk(ci):
            j, c, _ = halves[2 * ci]
            slot = ci % RAW
            view = raw[:, slot, 0:CH * j.n].rearrange("p (k n) -> p k n", k=CH)
            prev = [state_w[2 * (ci - RAW) + h][0:2] for h in range(2)] if ci >= RAW else []
            for dst, src in j.load(view, j.chunks[c]):
                t = sp.do(f"weight{slot}", lambda e, dst=dst, src=src: e.dma_start(dst, src), prev, inc=16)
            loaded[ci] = t

        def split(idx):
            j, c, h = halves[idx]
            ci = idx // 2
            if ci not in loaded:
                load_chunk(ci)
            r = idx % RING
            src = raw[:, ci % RAW, h * 2 * j.n:(h + 1) * 2 * j.n]
            hi_t, lo_t = whi[:, r, 0:2 * j.n], wlo[:, r, 0:2 * j.n]
            used = state_w[idx - RING][2] if idx >= RING else []
            hi = copy(act, "weight_hi", hi_t, src, loaded[ci], used)
            lo = tt(dve, "weight_lo", lo_t, src, hi_t.bitcast(F32), ALU.subtract, hi, used)
            state_w[idx] = [hi, lo, None]
            if h == 1 and 2 * (ci + RAW) < len(halves):
                load_chunk(ci + RAW)

        def split_lhs(idx):
            j, c, h = halves[idx]
            k = j.chunks[c] * CH + 2 * h
            r = idx % LRING
            src = j.split(k)
            used = state_w[idx - LRING][2] if idx >= LRING else []
            hi = copy(act, "lhs_hi", lhi[:, r], src, j.ready(k), used)
            lo = tt(dve, "lhs_lo", llo[:, r], src, lhi[:, r].bitcast(F32), ALU.subtract, hi, used)
            state_l[idx] = [hi, lo]

        for ci in range(min(RAW, len(halves) // 2)):
            load_chunk(ci)
        for idx in range(min(AHEAD, len(halves))):
            split(idx)
        pair = None
        for idx, (j, c, h) in enumerate(halves):
            if idx + AHEAD < len(halves):
                split(idx + AHEAD)
            k0 = j.chunks[c] * CH + 2 * h
            if j.split is None:
                settle(lambda: j.ready(k0) is not None)
                parts, made = j.lhs, j.ready(k0)
            else:
                for look in range(idx, min(idx + LAHEAD + 1, len(halves))):
                    jj, cc, hh = halves[look]
                    if jj.split is None or look in state_l:
                        continue
                    kk = jj.chunks[cc] * CH + 2 * hh
                    if look == idx:
                        settle(lambda: jj.ready(kk) is not None)
                    if jj.ready(kk) is None:
                        break
                    split_lhs(look)
                r = idx % LRING
                parts = lambda k: (lhi[:, r, k - k0], llo[:, r, k - k0])
                made = state_l[idx]
            if c == 0 and h == 0:
                state["pair"] += 1
                pair = pairs[state["pair"] % 2]
                settle(lambda: pair.free is not None)
                opening = pair.free
                pair.free = None
            r4 = idx % RING
            last = c == len(j.chunks) - 1 and h == 1
            for kk in range(2):
                xh, xl = parts(k0 + kk)
                wh = whi[:, r4, kk * j.n:(kk + 1) * j.n]
                wl = wlo[:, r4, kk * j.n:(kk + 1) * j.n]
                for i in range(NT):
                    for n3, (l, w) in enumerate(((xh, wh), (xh, wl), (xl, wh))):
                        end = kk == 1 and i == NT - 1 and n3 == 2
                        t = mm("product" if end else None, pair.t[i][:, 0:j.n], l[:, i * P:(i + 1) * P], w,
                               state_w[idx][0:2], made, opening if c == 0 and h == 0 else None,
                               start=(c == 0 and h == 0 and kk == 0 and n3 == 0), stop=(last and kk == 1 and n3 == 2))
            state_w[idx][2] = t
            state["last"] = t
            if j.key:
                uses[j.key][1] = t
            if last:
                if j.key:
                    uses[j.key][0] -= 1
                urgent.append(j.done(pair, t))
            step_all()

    def columns(w, c0, n=NC):
        def f(view, c):
            return [(view, w[c * CH * P:(c + 1) * CH * P, c0:c0 + n].rearrange("(k p) n -> p k n", p=P))]
        return f

    def product(w, c0, done, key, n=NC, load=None):
        uses.setdefault(key, [0, None])[0] += 1
        return Job(load or columns(w, c0, n), list(range(KD // CH)), n, done,
                   lhs=lambda k: (xhi[:, k], xlo[:, k]), ready=lambda k: x_ready.get((key, k)), key=key)

    got = {}

    def scale_of(key):
        while key not in scales:
            yield False
        return scales[key]

    def keep(key, of, then=None):
        def done(pair, t):
            r, _, tr = yield from scale_of(of)
            b = yield from take()
            e = [func("kept", ACT.Copy, b.t[:, 0:NC], pair.t[0][:, :], t, tr, b.free, scale=r[:, 0:1]),
                 ts("kept", b.t[:, NC:2 * NC], pair.t[1][:, :], r[:, 1:2], ALU.mult, None, None, t, tr, b.free)]
            pair.free = e
            got[key] = (b, e)
            if then is not None:
                gens.append(then())
            yield True
        return done

    def keep_silu2(key, of, then=None):
        def done(pair, t):
            _, hr, tr = yield from scale_of(of)
            b = yield from take()
            for i in range(NT):
                e = func("half_tanh", ACT.Tanh, b.t[:, i * NC:(i + 1) * NC], pair.t[i][:, :], t, tr, b.free,
                         scale=hr[:, i:i + 1])
            yield True
            for i in range(NT):
                bb = b.t[:, i * NC:(i + 1) * NC]
                e2 = stt("silu2", bb, bb, 1.0, pair.t[i][:, :], ALU.add, ALU.mult, e)
            pair.free = [e2]
            got[key] = (b, [e2])
            if then is not None:
                gens.append(then())
            yield True
        return done

    def need(*keys):
        while not all(k in got for k in keys):
            yield False
        return [got.pop(k) for k in keys]

    def to_channels(b, t_b, scale=None):
        o = yield from take()
        view = o.t.rearrange("p (c t) -> p c t", t=T)
        ts_ = []
        for c in range(0, 4, 2):
            p = yield from bank()
            for cc in range(2):
                for i in range(NT):
                    t = turn("to_channels", p.t[:, cc * T + i * P:cc * T + (i + 1) * P],
                             b.t[:, i * NC + (c + cc) * P:i * NC + (c + cc + 1) * P], t_b, p.free)
            e = copy(act, "to_channels", view[:, c:c + 2, :], p.t[:, :].rearrange("p (c t) -> p c t", t=T), t, o.free, scale=scale)
            done_with(p, e)
            ts_.append(e)
            yield True
        give(b, t)
        return o, ts_

    w_in = a["w_in"][0]
    w_out = a["w_out"][0]

    def first_sums():
        acc = small(NT * (D // NC)).rearrange("p (t n) -> p t n", t=NT)
        for n in range(D // NC):
            s = yield from square_sums(n, xblk[n], acc, t_x[n])
        set_scale("u1", *norm_scale(acc, s))
        state["first_sums"] = s

    def first_turn():
        for n in range(D // NC):
            xblk[n].free = [(yield from turn_block("u1", None, n, xblk[n], W_NORM, t_x[n]))]
        while "first_sums" not in state:
            yield False
        for b in xblk:
            give(b, b.free, state["first_sums"])

    gens += [first_turn(), first_sums()]

    gates = {}

    def load_gates(view, c):
        rows_ = slice(c * CH * P, (c + 1) * CH * P)
        return [(view[:, :, 0:16], w_in[rows_, C_MI:C_MI + 16].rearrange("(k p) n -> p k n", p=P)),
                (view[:, :, 16:48], w_in[rows_, C_DB:C_DB + 32].rearrange("(k p) n -> p k n", p=P))]

    def gates_done(pair, t):
        r, _, tr = yield from scale_of("u1")
        g = [gt[:, i] for i in range(10)]
        v = g[0]
        for i in range(NT):
            e = ts("gate_raw", v[:, i, :], pair.t[i][:, 0:48], r[:, i:i + 1], ALU.mult, None, None, t, tr)
        pair.free = [e]
        th, arg, ex, u, ln, inv, z, res = g[1:9]
        b2 = lambda lo, n: over(gb[:, lo:lo + n], 1, NT)
        t1 = tt(dve, "gate_biased", th[:, :, 0:16], v[:, :, 0:16], b2(0, 16), ALU.add, e, t_b)
        t2 = tt(dve, "gate_z", z[:, :, 0:16], v[:, :, 32:48], b2(32, 16), ALU.add, e, t_b)
        t3 = func("gate_tanh", ACT.Tanh, th[:, :, 0:16], th[:, :, 0:16], t1, scale=1.0 / CAP)
        t4 = ts("gate_arg", arg[:, :, 0:8], th[:, :, 8:16], -CAP, ALU.mult, None, None, t3)
        t5 = ts("gate_arg", arg[:, :, 8:24], v[:, :, 16:32], -1.0, ALU.mult, None, None, e)
        t6 = stt("gate_arg", arg[:, :, 24:40], z[:, :, 0:16], -1.0, z[:, :, 0:16], ALU.mult, ALU.min, t2)
        t7 = func("gate_exp", ACT.Exp, ex[:, :, 0:40], arg[:, :, 0:40], t4, t5, t6)
        ta = func("gate_exp", ACT.Exp, gb[:, 16:32], gb[:, 16:32], t_b)
        t8 = ts("gate_u", u[:, :, 0:40], ex[:, :, 0:40], 1.0, ALU.add, None, None, t7)
        t9 = dve.do("gate_inv", lambda e: e.reciprocal(inv[:, :, 0:40], u[:, :, 0:40]), t8)
        func("gate_ln", ACT.Ln, ln[:, :, 0:8], u[:, :, 0:8], t8)
        tl = func("gate_ln", ACT.Ln, ln[:, :, 24:40], u[:, :, 24:40], t8)
        yield True
        for lo, n in ((0, 8), (24, 16)):
            s = (slice(None), slice(None), slice(lo, lo + n))
            x1 = ts("gate_log1p", arg[s], u[s], -1.0, ALU.add, None, None, t8)
            x2 = tt(dve, "gate_log1p", arg[s], ex[s], arg[s], ALU.subtract, x1)
            x3 = tt(dve, "gate_log1p", arg[s], arg[s], inv[s], ALU.mult, x2, t9)
            x4 = tt(dve, "gate_log1p", arg[s], arg[s], ln[s], ALU.add, x3, tl)
        r1 = ts("gate_i", res[:, :, 0:8], th[:, :, 0:8], CAP, ALU.mult, None, None, t3)
        r2 = ts("gate_f", res[:, :, 8:16], arg[:, :, 0:8], -1.0, ALU.mult, None, None, x4)
        y1 = stt("gate_g", res[:, :, 16:32], z[:, :, 0:16], 0.0, arg[:, :, 24:40], ALU.max, ALU.add, x4)
        y2 = stt("gate_g", res[:, :, 16:32], res[:, :, 16:32], -1.0, over(gb[:, 16:32], 1, NT), ALU.mult, ALU.mult, y1, ta)
        gates.update(i=res[:, :, 0:8], f=res[:, :, 8:16], g=res[:, :, 16:32], beta=inv[:, :, 8:24],
                     t=[r1, r2, y2, t9])
        yield True
        p = yield from bank()
        ft = g[9]
        mm("forget_sum", p.t[:, 0:8], INC, res[:, 0, 8:16], gates["t"], p.free)
        mm("forget_sum", p.t[:, 8:16], ONE, res[:, 0, 8:16], stop=False)
        m = mm("forget_sum", p.t[:, 8:16], INC, res[:, 1, 8:16], start=False)
        c = copy(dve, "forget_sum", ft[:, :, 0:8], p.t[:, 0:16].rearrange("p (t h) -> p t h", t=NT), m)
        done_with(p, c)
        gates.update(F=ft[:, :, 0:8], tF=[c])
        yield True

    def conv(key, ct):
        (b, tb), = yield from need(key)
        yield True
        y = yield from take()
        yv = y.t.rearrange("p (c t) -> p c t", t=T)
        fin = []
        for c in range(0, 4, 2):
            p = yield from bank()
            for cc in range(2):
                for i in range(NT):
                    t = turn("conv_turned", p.t[:, cc * T + i * P:cc * T + (i + 1) * P],
                             b.t[:, i * NC + (c + cc) * P:i * NC + (c + cc + 1) * P], tb, p.free)
            yield True
            w = lambda cc, j: cwcol[:, j * 48 + ct + c + cc:j * 48 + ct + c + cc + 1]
            for cc in range(2):
                s0 = func("conv_last_tap", ACT.Copy, yv[:, c + cc, :], p.t[:, cc * T:(cc + 1) * T], t, y.free, t_w,
                          scale=w(cc, CONV - 1))
            for cc in range(2):
                s = s0
                for j in range(1, CONV):
                    s = stt("conv_tap", yv[:, c + cc, j:T], p.t[:, cc * T:(cc + 1) * T - j], w(cc, CONV - 1 - j),
                            yv[:, c + cc, j:T], ALU.mult, ALU.add, s)
                fin.append(s)
            done_with(p, fin)
            yield True
        give(b, t)
        th = yield from take()
        e = func("conv_tanh", ACT.Tanh, th.t, y.t, fin, th.free, scale=0.5)
        e = stt("conv_silu2", y.t, th.t, 1.0, y.t, ALU.add, ALU.mult, e)
        give(th, e)
        got[key + "c"] = (y, [e])
        yield True

    HB = 4
    hb_ready = {}

    def delta(g):
        h0 = g * HB
        (yk, tk), (yq, tq) = yield from need(f"dk{g}c", f"dq{g}c")
        yield from stage_turn()
        beta, gg = gates["beta"], gates["g"]
        hs = slice(h0, h0 + HB)
        ss = small(4 * HB).rearrange("p (q t h) -> p q t h", q=2, t=NT)
        p = yield from bank()
        sq_free = []
        for n, (y, t_y) in enumerate(((yq, tq), (yk, tk))):
            sq = yield from take()
            e = func("delta_square", ACT.Square, sq.t, y.t, t_y, sq.free)
            for i in range(NT):
                for h in range(HB):
                    m = mm("delta_square_sum", p.t[:, (n * NT + i) * HB + h:(n * NT + i) * HB + h + 1],
                           sq.t[:, h * T + i * P:h * T + (i + 1) * P], ONE[:, 0:1], e, p.free)
            give(sq, m)
            yield True
        e = ts("delta_ss", ss.rearrange("p q t h -> p (q t h)"), p.t[:, 0:4 * HB], 0.25, ALU.mult, EPS, ALU.add, m)
        done_with(p, e)
        r = small(4 * HB).rearrange("p (q t h) -> p q t h", q=2, t=NT)
        e = tt(pool, "delta_rsqrt", r.rearrange("p q t h -> p (q t h)"), ss.rearrange("p q t h -> p (q t h)"),
               minus_half[:, 0:1].broadcast_to([P, 4 * HB]), ALU.pow, e, t_half)
        rq, rk, ck, hb_ = (small(NT * HB).rearrange("p (t h) -> p t h", t=NT) for _ in range(4))
        t_rq = ts("delta_factor", rq, r[:, 0], 0.5 * DN_D ** -0.5, ALU.mult, None, None, e)
        t_rk = ts("delta_factor", rk, r[:, 1], 0.5, ALU.mult, None, None, e)
        t_ck = tt(dve, "delta_factor", ck, rk, beta[:, :, hs], ALU.mult, t_rk, gates["t"])
        t_hb = ts("delta_factor", hb_, beta[:, :, hs], 0.5, ALU.mult, None, None, gates["t"])
        yield True
        kc = yield from take()
        for i in range(NT):
            p = yield from bank()
            for h in range(HB):
                m = turn("delta_k", p.t[:, h * P:(h + 1) * P], yk.t[:, h * T + i * P:h * T + (i + 1) * P], tk, p.free)
            e = tt(dve, "delta_k_scaled", kc.t[:, i * NC:(i + 1) * NC].rearrange("p (h d) -> p h d", h=HB),
                   p.t[:, :].rearrange("p (h d) -> p h d", h=HB), over(ck[:, i], 2, P), ALU.mult, m, t_ck, kc.free)
            done_with(p, e)
            yield True
        kt = yield from take()
        ktv = kt.t.rearrange("p (h t) -> p h t", h=HB)
        t_kc = []
        for i in range(NT):
            p = yield from bank()
            for h in range(HB):
                m = turn("delta_kc", p.t[:, h * P:(h + 1) * P], kc.t[:, i * NC + h * P:i * NC + (h + 1) * P], e, p.free)
            t_kc.append(copy(act, "delta_kc", ktv[:, :, i * P:(i + 1) * P],
                             p.t[:, :].rearrange("p (h d) -> p h d", h=HB), m, kt.free))
            done_with(p, t_kc)
            yield True
        give(kc, m)
        R0, R1 = (yield from take()), (yield from take())
        R0v, R1v = R0.t.rearrange("p (h t) -> p h t", h=HB), R1.t[:, 0:NC].rearrange("p (h t) -> p h t", h=HB)
        ra = tt(pool, "delta_decay_rhs", R0v[:, :, 0:P], over(INC, 1, HB), over(gg[:, 0, hs], 2, P), ALU.mult,
                R0.free, t_c, gates["t"])
        rb = tt(pool, "delta_decay_rhs", R0v[:, :, P:T], over(ONE, 1, HB), over(gg[:, 0, hs], 2, P), ALU.mult)
        rc = tt(pool, "delta_decay_rhs", R1v, over(INC, 1, HB), over(gg[:, 1, hs], 2, P), ALU.mult, R1.free)
        E0v, E1v = R0v, R1v
        es = []
        yield True
        for n in range(2):
            p = yield from bank()
            mm("delta_decay", p.t[:, :], STR, R0v[:, 2 * n:2 * n + 2, :], rb, p.free, stop=False)
            m = mm("delta_decay", p.t[:, :].rearrange("p (h t) -> p h t", h=2)[:, :, P:T], ONE,
                   R1v[:, 2 * n:2 * n + 2, :], rc, start=False)
            es.append(func("delta_decay", ACT.Exp, E0v[:, 2 * n:2 * n + 2, :],
                           p.t[:, :].rearrange("p (h t) -> p h t", h=2), m))
            done_with(p, es)
        p = yield from bank()
        m = mm("delta_decay", p.t[:, :], STR, R1v, rc, p.free)
        es.append(func("delta_decay", ACT.Exp, E1v, p.t[:, :].rearrange("p (h t) -> p h t", h=HB), m))
        done_with(p, es)
        yield True
        e = tt(pool, "delta_masked", E0v[:, :, 0:P], E0v[:, :, 0:P], over(INC, 1, HB), ALU.mult, es)
        e = tt(pool, "delta_masked", E1v, E1v, over(INC, 1, HB), ALU.mult, es)
        e = tt(pool, "delta_masked", E0v, E0v, over(rk[:, 0], 2, T), ALU.mult, e, t_rk)
        t_E = tt(pool, "delta_masked", E1v, E1v, over(rk[:, 1], 2, P), ALU.mult, e)
        P0, B0 = (yield from take()), (yield from take())
        PB1 = yield from take()
        P0v, B0v = (b.t.rearrange("p (h t) -> p h t", h=HB) for b in (P0, B0))
        P1v, B1v = (PB1.t[:, i * NC:(i + 1) * NC].rearrange("p (h t) -> p h t", h=HB) for i in range(2))
        t_P, t_B = [], []
        yield True
        for dst, y, lst in ((B0v, kt, t_B), (P0v, yq, t_P)):
            for n in range(2):
                p = yield from bank()
                for h in range(2 * n, 2 * n + 2):
                    m = mm("delta_scores", p.t[:, (h - 2 * n) * T:(h - 2 * n + 1) * T], yk.t[:, h * T:h * T + P],
                           y.t[:, h * T:(h + 1) * T], tk, tq, t_kc, p.free)
                lst.append(tt(dve, "delta_weights", dst[:, 2 * n:2 * n + 2, :],
                              p.t[:, :].rearrange("p (h t) -> p h t", h=2), E0v[:, 2 * n:2 * n + 2, :], ALU.mult,
                              m, t_E, P0.free, B0.free))
                done_with(p, lst)
                yield True
        for dst, y, lst in ((B1v, kt, t_B), (P1v, yq, t_P)):
            p = yield from bank()
            for h in range(HB):
                m = mm("delta_scores", p.t[:, h * P:(h + 1) * P], yk.t[:, h * T + P:(h + 1) * T],
                       y.t[:, h * T + P:(h + 1) * T], p.free)
            lst.append(tt(dve, "delta_weights", dst, p.t[:, :].rearrange("p (h t) -> p h t", h=HB), E1v, ALU.mult,
                          m, t_E, PB1.free))
            done_with(p, lst)
            yield True
        give(yk, m)
        give(yq, m)
        give(kt, m)
        give(R0, t_P, t_B)
        give(R1, t_P, t_B)
        U, Tt = (yield from take()), (yield from take())
        BM = yield from take()
        Xs = yield from take_some(2)
        units = lambda b: b.t.rearrange("p (g t) -> p g t", t=P)
        half = lambda b, i: b.t[:, i * NC:(i + 1) * NC]
        hv = lambda b, i: half(b, i).rearrange("p (h t) -> p h t", h=HB)
        sides = lambda ap, w, side: ap.rearrange("p (g s x) -> p g s x", s=2, x=w // 2)[:, :, side, :]

        def level(l, *after):
            tt(pool, "delta_level", units(BM)[:, 0:HB], B0v[:, :, 0:P], over(LVL[l], 1, HB), ALU.mult, t_B, BM.free, t_c2,
               after)
            return tt(pool, "delta_level", units(BM)[:, HB:2 * HB], B1v, over(LVL[l], 1, HB), ALU.mult)

        t_zero = [pool.do("delta_zero", lambda e, x=x: e.memset(x.t, 0.0), x.free) for x in Xs]
        e = level(0)
        t_U = tt(dve, "delta_U", units(U), over(IDN, 1, 2 * HB), units(BM), ALU.subtract, e, U.free)
        t_BM = level(1, t_U)
        yield True
        t_T = []
        for i in range(NT):
            p = yield from bank()
            for h in range(HB):
                m = turn("delta_T", p.t[:, h * P:(h + 1) * P], hv(U, i)[:, h, :], t_U, p.free)
            t_T.append(copy(act, "delta_T", half(Tt, i), p.t[:, :], m, Tt.free))
            done_with(p, t_T)
        yield True
        for l in range(1, LEVELS):
            w = 2 << l
            last = l == LEVELS - 1
            X, tz = Xs[l % 2], t_zero[l % 2]
            p = yield from bank()
            packed = lambda p, n: p.t[:, n * (P // 2):(n + 1) * (P // 2)].rearrange("p (g x) -> p g x", x=w // 2)
            for n in range(2 * HB):
                m = mm("delta_X", packed(p, n), units(BM)[:, n], sides(units(Tt)[:, n], w, 0), t_BM, t_T, p.free)
            t_X = copy(act, "delta_X", sides(X.t, w, 0), p.t[:, :].rearrange("p (g x) -> p g x", x=w // 2), m, tz)
            done_with(p, t_X)
            if not last:
                t_BM = level(l + 1, m)
            yield True
            p = yield from bank()
            p2 = (yield from bank()) if not last else None
            for n in range(2 * HB):
                m = mm("delta_Y", packed(p, n), units(X)[:, n], sides(units(U)[:, n], w, 1), t_X, t_U, p.free)
            if not last:
                for n in range(2 * HB):
                    m2 = mm("delta_YT", packed(p2, n), units(U)[:, n], sides(units(X)[:, n], w, 0), p2.free)
                t_zero[l % 2] = pool.do("delta_zero", lambda e, X=X: e.memset(X.t, 0.0), m2)
                tl = sides(Tt.t, w, 0)
                t_T = tt(dve, "delta_T", tl, tl, p2.t[:, :].rearrange("p (g x) -> p g x", x=w // 2), ALU.subtract, m2)
                done_with(p2, t_T)
                ur = m2
            else:
                ur = m
            ul = sides(U.t, w, 1)
            t_U = tt(dve, "delta_U", ul, ul, p.t[:, :].rearrange("p (g x) -> p g x", x=w // 2), ALU.subtract, ur)
            done_with(p, t_U)
            yield True
        give(Tt, m)
        give(BM, m)
        for x, tz in zip(Xs, t_zero):
            give(x, m, tz)
        stage_over()
        (yv, tv), = yield from need(f"dv{g}c")
        bv, u = (yield from take()), (yield from take())
        bvv = lambda i: bv.t[:, i * NC:(i + 1) * NC].rearrange("p (h d) -> p h d", h=HB)
        t_bv = []
        for i in range(NT):
            p = yield from bank()
            for h in range(HB):
                m = turn("delta_v", p.t[:, h * P:(h + 1) * P], yv.t[:, h * T + i * P:h * T + (i + 1) * P], tv, p.free)
            t_bv.append(tt(dve, "delta_bv", bvv(i), p.t[:, :].rearrange("p (h d) -> p h d", h=HB),
                           over(hb_[:, i], 2, P), ALU.mult, m, t_hb, bv.free))
            done_with(p, t_bv)
        give(yv, m)
        yield True
        p = yield from bank()
        for h in range(HB):
            m = mm("delta_u", p.t[:, h * P:(h + 1) * P], hv(U, 0)[:, h, :], bvv(0)[:, h, :], t_U, t_bv, p.free)
        t_u0 = copy(act, "delta_u", half(u, 0), p.t[:, :], m, u.free)
        done_with(p, t_u0)
        yield True
        p = yield from bank()
        for h in range(HB):
            m = mm("delta_bu", p.t[:, h * P:(h + 1) * P], B0v[:, h, P:T], hv(u, 0)[:, h, :], t_u0, p.free)
        e = tt(dve, "delta_bv", half(bv, 1), half(bv, 1), p.t[:, :], ALU.subtract, m)
        done_with(p, e)
        yield True
        p = yield from bank()
        for h in range(HB):
            m = mm("delta_u", p.t[:, h * P:(h + 1) * P], hv(U, 1)[:, h, :], bvv(1)[:, h, :], e, p.free)
        t_u1 = copy(act, "delta_u", half(u, 1), p.t[:, :], m)
        done_with(p, t_u1)
        give(bv, m)
        give(U, m)
        give(B0, m)
        o = yield from take()
        t_o = []
        yield True
        for i in range(NT):
            p = yield from bank()
            for h in range(HB):
                if i == 0:
                    m = mm("delta_o", p.t[:, h * P:(h + 1) * P], P0v[:, h, 0:P], hv(u, 0)[:, h, :], t_u0, t_P, p.free)
                else:
                    mm("delta_o", p.t[:, h * P:(h + 1) * P], P0v[:, h, P:T], hv(u, 0)[:, h, :], p.free, stop=False)
                    m = mm("delta_o", p.t[:, h * P:(h + 1) * P], P1v[:, h, :], hv(u, 1)[:, h, :], t_u1, start=False)
            t_o.append(tt(dve, "delta_o", hv(o, i), p.t[:, :].rearrange("p (h d) -> p h d", h=HB),
                          over(rq[:, i], 2, P), ALU.mult, m, t_rq, o.free))
            done_with(p, t_o)
            yield True
        give(P0, m)
        give(PB1, m)
        give(u, m)
        sq = yield from take()
        e = func("delta_o_square", ACT.Square, sq.t, o.t, t_o, sq.free)
        s2, ro = small(NT * HB), small(NT * HB)
        e = reduce("delta_o_sum", s2, sq.t.rearrange("p (g d) -> p g d", d=P), ALU.add, e)
        give(sq, e)
        e = rsqrt("delta_o_rsqrt", ro, s2, 1.0 / DN_D, e)
        rov = ro.rearrange("p (t h) -> p t h", t=NT)
        e = tt(dve, "delta_o_factor", rov, rov, over(scales["u1"][0], 2, HB), ALU.mult, e, scales["u1"][2])
        yield True
        (wz, tz), = yield from need(f"dz{g}")
        e = tt(pool, "delta_o_normed", o.t.rearrange("p (g d) -> p g d", d=P), o.t.rearrange("p (g d) -> p g d", d=P),
               over(ro, 2, P), ALU.mult, e)
        e = stt("delta_o_gated", o.t, wz.t, 0.5, o.t, ALU.mult, ALU.mult, e, tz)
        give(wz, e)
        yield True
        t_h = []
        for i in range(NT):
            p = yield from bank()
            for h in range(HB):
                m = turn("delta_out", p.t[:, h * P:(h + 1) * P], hv(o, i)[:, h, :], e, p.free)
            t_h.append(copy(act, "delta_out", acts[:, KD + h0:KD + h0 + HB, i * P:(i + 1) * P],
                            p.t[:, :].rearrange("p (h t) -> p h t", h=HB), m, acts_free, scale=wcol[:, W_DN:W_DN + 1]))
            done_with(p, t_h)
        give(o, m)
        hb_ready[g] = t_h
        yield True

    ml = {}

    def mlstm_scores(G):
        (qr, tq), = yield from need(f"mq{G}")
        (kr, tk), = yield from need(f"mk{G}")
        yield from stage_turn()
        qT, tq = yield from to_channels(qr, tq)
        kT, tk = yield from to_channels(kr, tk)
        hs = slice(G * HB, (G + 1) * HB)
        ig, fg, Fs = gates["i"], gates["f"], gates["F"]
        FS, II = (yield from take()), (yield from take())
        hv = lambda b, i: b.t[:, i * NC:(i + 1) * NC].rearrange("p (h t) -> p h t", h=HB)
        hf = lambda b, i: b.t[:, i * NC:(i + 1) * NC]
        for i in range(NT):
            tt(pool, "ml_decay_rhs", hv(FS, i), over(STR, 1, HB), over(fg[:, i, hs], 2, P), ALU.mult, FS.free, gates["t"])
            r = tt(pool, "ml_decay_rhs", hv(II, i), over(IDN, 1, HB), over(ig[:, i, hs], 2, P), ALU.mult, II.free)
        yield True
        Dd, Dx = (yield from take()), (yield from take())
        mx = small(3 * HB).rearrange("p (n h) -> p n h", h=HB)
        tm = []
        for n, (i, s) in enumerate(((0, 0), (1, 1), (1, 0))):
            p = yield from bank()
            pv = p.t[:, :].rearrange("p (h t) -> p h t", h=HB)
            mm("ml_decay", p.t[:, :], INC if i == s else ONE, hf(FS, s), r, p.free, stop=False)
            if i != s:
                mm("ml_decay", pv, INC, over(fg[:, 1, hs], 2, P), start=False, stop=False)
            m = mm("ml_decay", p.t[:, :], ONE, hf(II, s), start=False)
            if i == s:
                e = tt(dve, "ml_masked", hv(Dd, n), pv, over(NEGM, 1, HB), ALU.add, m, Dd.free, t_c2)
                tm.append(reduce("ml_max", mx[:, n], hv(Dd, n), ALU.max, e))
            else:
                e = copy(act, "ml_decay", hf(Dx, 0), p.t[:, :], m, Dx.free)
                tm.append(reduce("ml_max", mx[:, n], hv(Dx, 0), ALU.max, e))
            done_with(p, e)
            yield True
        give(FS, m)
        give(II, m)
        M, nM, em = (small(NT * HB).rearrange("p (t h) -> p t h", t=NT) for _ in range(3))
        e1 = tt(dve, "ml_m", M[:, 0], mx[:, 0], Fs[:, 0, hs], ALU.max, tm, gates["tF"])
        e2 = tt(dve, "ml_m", M[:, 1], mx[:, 1], mx[:, 2], ALU.max, tm)
        e2 = tt(dve, "ml_m", M[:, 1], M[:, 1], Fs[:, 1, hs], ALU.max, e2)
        e3 = ts("ml_m", nM, M, -1.0, ALU.mult, None, None, e1, e2)
        t_em = func("ml_em", ACT.Exp, em, nM, e3)
        tiles = ((0, 0, hv(Dd, 0), hf(Dd, 0)), (1, 1, hv(Dd, 1), hf(Dd, 1)), (1, 0, hv(Dx, 0), hf(Dx, 0)))
        es = []
        for n, (i, s, v, f) in enumerate(tiles):
            for h in range(HB):
                e = func("ml_exp", ACT.Exp, v[:, h], v[:, h], e3, bias=nM[:, i, h:h + 1])
            es.append(e)
            yield True
        dn = small(3 * HB).rearrange("p (n h) -> p n h", h=HB)
        WT = yield from take_some(2)
        wtv = [hv(WT[0], 0), hv(WT[0], 1), hv(WT[1], 0)]
        t_W, t_d = [], []
        for n, (i, s, v, f) in enumerate(tiles):
            p = yield from bank()
            for h in range(HB):
                m = mm("ml_scores", p.t[:, h * P:(h + 1) * P], qT.t[:, h * T + i * P:h * T + (i + 1) * P],
                       kT.t[:, h * T + s * P:h * T + (s + 1) * P], tq, tk, p.free)
            e = stt("ml_weights", f, p.t[:, :], ML_DK ** -0.5, f, ALU.mult, ALU.mult, m, es[n])
            t_d.append(reduce("ml_den", dn[:, n], v, ALU.add, e))
            done_with(p, e)
            yield True
            p = yield from bank()
            for h in range(HB):
                m2 = turn("ml_turned", p.t[:, h * P:(h + 1) * P], v[:, h], e, p.free)
            t_W.append(copy(act, "ml_turned", wtv[n], p.t[:, :].rearrange("p (h t) -> p h t", h=HB), m2, WT[n // 2].free))
            done_with(p, t_W)
            yield True
        give(qT, m)
        give(kT, m)
        give(Dd, m2, t_d)
        give(Dx, m2, t_d)
        den, inv = (small(NT * HB).rearrange("p (t h) -> p t h", t=NT) for _ in range(2))
        e = tt(dve, "ml_den2", dn[:, 1], dn[:, 1], dn[:, 2], ALU.add, t_d)
        e = stt("ml_den2", den, dn[:, 0:2], -1.0, dn[:, 0:2], ALU.mult, ALU.max, e)
        e = tt(dve, "ml_den2", den, den, em, ALU.max, e, t_em)
        e = dve.do("ml_inv", lambda q: q.reciprocal(inv, den), e)
        stage_over()
        ml[G] = dict(W=wtv, WT=WT, tW=t_W, inv=inv, tinv=e, users=[], left=2)
        yield True

    ha_ready = {}

    def mlstm_out(pr):
        G, h0 = pr // 2, 2 * (pr % 2)
        while G not in ml:
            yield False
        s = ml[G]
        (v, tv), = yield from need(f"mv{pr}")
        ssq, rr, fac = (small(NT * 2).rearrange("p (t h) -> p t h", t=NT) for _ in range(3))
        ps = []
        for i in range(NT):
            p = yield from bank()
            for hh in range(2):
                h = h0 + hh
                o = p.t[:, hh * ML_DV:(hh + 1) * ML_DV]
                vv = lambda k: v.t[:, k * NC + hh * ML_DV:k * NC + (hh + 1) * ML_DV]
                if i == 0:
                    m = mm("ml_num", o, s["W"][0][:, h], vv(0), s["tW"], tv, p.free)
                else:
                    mm("ml_num", o, s["W"][2][:, h], vv(0), p.free, stop=False)
                    m = mm("ml_num", o, s["W"][1][:, h], vv(1), start=False)
            ps.append(p)
        s["users"].append(m)
        s["left"] -= 1
        if s["left"] == 0:
            for b in s["WT"]:
                give(b, s["users"])
        give(v, m)
        yield True
        hA = yield from take()
        for i in range(NT):
            for hh in range(2):
                q = func("ml_square", ACT.Square, hA.t[:, 0:ML_DV], ps[i].t[:, hh * ML_DV:(hh + 1) * ML_DV], m,
                         s["tinv"], hA.free, scale=s["inv"][:, i, h0 + hh:h0 + hh + 1], accum_out=ssq[:, i, hh:hh + 1])
                hA.free = [q]
        e = rsqrt("ml_rsqrt", rr.rearrange("p t h -> p (t h)"), ssq.rearrange("p t h -> p (t h)"), 1.0 / ML_DV, q)
        e = stt("ml_factor", fac, rr, 0.25, s["inv"][:, :, h0:h0 + 2], ALU.mult, ALU.mult, e)
        e = tt(dve, "ml_factor", fac, fac, over(scales["u1"][0], 2, 2), ALU.mult, e, scales["u1"][2])
        yield True
        (g, tg), = yield from need(f"mg{pr}")
        for i in range(NT):
            for hh in range(2):
                sl = slice(i * NC + hh * ML_DV, i * NC + (hh + 1) * ML_DV)
                e2 = stt("ml_gated", hA.t[:, sl], ps[i].t[:, hh * ML_DV:(hh + 1) * ML_DV], fac[:, i, hh:hh + 1],
                         g.t[:, sl], ALU.mult, ALU.mult, e, tg, q)
            done_with(ps[i], e2)
        give(g, e2)
        yield True
        th = []
        for c in range(0, 4, 2):
            p = yield from bank()
            for cc in range(2):
                for i in range(NT):
                    m = turn("ml_out", p.t[:, cc * T + i * P:cc * T + (i + 1) * P],
                             hA.t[:, i * NC + (c + cc) * P:i * NC + (c + cc + 1) * P], e2, p.free)
            for cc in range(2):
                k = pr * 4 + c + cc
                th.append(copy(act, "ml_out", acts[:, k, :], p.t[:, cc * T:(cc + 1) * T], m, acts_free,
                               scale=wcol[:, W_ML + k:W_ML + k + 1]))
            done_with(p, th)
            yield True
        give(hA, m)
        ha_ready[pr] = th

    def keep_tanh(key):
        def done(pair, t):
            _, hr, tr = yield from scale_of("u1")
            b = yield from take()
            for i in range(NT):
                e = func("half_tanh", ACT.Tanh, b.t[:, i * NC:(i + 1) * NC], pair.t[i][:, :], t, tr, b.free,
                         scale=hr[:, i:i + 1])
            pair.free = [e]
            got[key] = (b, [e])
            yield True
        return done

    def mlstm_gate(pr):
        def done(pair, t):
            yield from keep_silu2(f"mzz{pr}", "u1")(pair, t)
            (z, tz), (o, to) = yield from need(f"mzz{pr}", f"mo{pr}")
            e = stt("ml_gate", z.t, o.t, 1.0, z.t, ALU.add, ALU.mult, tz, to)
            give(o, e)
            got[f"mg{pr}"] = (z, [e])
            gens.append(mlstm_out(pr))
            yield True
        return done

    jobs = []

    def j1(c0, done):
        jobs.append(product(w_in, c0, done, "u1"))

    def dn_jobs(g):
        if g == 0:
            jobs.append(product(w_in, 0, gates_done, "u1", 48, load_gates))
        j1(C_DK + g * NC, keep(f"dk{g}", "u1", then=lambda: conv(f"dk{g}", DN_W // P + 4 * g)))
        j1(C_DQ + g * NC, keep(f"dq{g}", "u1", then=lambda: conv(f"dq{g}", 4 * g)))
        j1(C_DV + g * NC, keep(f"dv{g}", "u1", then=lambda: conv(f"dv{g}", 2 * DN_W // P + 4 * g)))
        j1(C_DZ + g * NC, keep_silu2(f"dz{g}", "u1", then=lambda: delta(g)))

    def ml_qk(G):
        j1(C_MQ + G * NC, keep(f"mq{G}", "u1"))
        j1(C_MK + G * NC, keep(f"mk{G}", "u1", then=lambda: mlstm_scores(G)))

    def ml_pair(pr):
        j1(C_MV + pr * NC, keep(f"mv{pr}", "u1"))
        j1(C_MO + pr * NC, keep_tanh(f"mo{pr}"))
        j1(C_MZ + pr * NC, mlstm_gate(pr))

    dn_jobs(0)
    ml_qk(0)
    ml_pair(0)
    dn_jobs(1)
    ml_pair(1)
    dn_jobs(2)
    ml_qk(1)
    ml_pair(2)
    dn_jobs(3)
    ml_pair(3)

    resid = {}
    acc1 = small(NT * (D // NC)).rearrange("p (t n) -> p t n", t=NT)
    sums1 = []

    def gated(n, which):
        def done(pair, t):
            (g, tg), = yield from need(f"g{which}{n}")
            for i in range(NT):
                s = slice(i * NC, (i + 1) * NC)
                e = stt("out_gated", g.t[:, s], g.t[:, s], 1.0, pair.t[i][:, :], ALU.add, ALU.mult, tg, t)
            pair.free = [e]
            if which == "b":
                got[f"yb{n}"] = (g, [e])
                yield True
                return
            (b, tb), = yield from need(f"yb{n}")
            x = yield from take()
            tx = load(f"x{n}", x.t.rearrange("p (t n) -> p t n", t=NT),
                      a["x"][0, :, n * NC:(n + 1) * NC].rearrange("(t p) n -> p t n", p=P), x.free, q=act)
            e = tt(pool, "out_sum", b.t, b.t, g.t, ALU.add, e, tb)
            give(g, e)
            yield True
            e = stt("out_resid", x.t, b.t, 0.5, x.t, ALU.mult, ALU.add, e, tx)
            give(b, e)
            sums1.append((yield from square_sums(n, x, acc1, e)))
            yield True
            t = yield from turn_block("u2", "u1", n, x, W_BOTH, e)
            resid[n] = (x, [e, t])
            yield True
        return done

    def out_job(n, k0, ready, done):
        return Job(columns(w_out, n * NC), list(range(k0 // CH, (k0 + KD) // CH)), NC, done,
                   split=lambda k: acts[:, k:k + 2, :],
                   ready=ready)

    def gate_jobs(n):
        j1(C_GB + n * NC, keep_tanh(f"gb{n}"))
        j1(C_GA + n * NC, keep_tanh(f"ga{n}"))

    def y_jobs(n):
        jobs.append(out_job(n, KD, lambda k: hb_ready.get((k - KD) // 4), gated(n, "b")))
        jobs.append(out_job(n, 0, lambda k: ha_ready.get(k // 4), gated(n, "a")))

    for step, n in ((gate_jobs, 0), (gate_jobs, 1), (y_jobs, 0), (gate_jobs, 2), (y_jobs, 1), (gate_jobs, 3),
                    (y_jobs, 2), (y_jobs, 3)):
        step(n)

    w2 = a["w_in_2"][0]
    x2_dram = nc.dram_tensor("x2", (P, NT, D), F32, kind="Internal").ap()
    kept = {}

    def second_norm():
        while len(resid) < D // NC or len(sums1) < D // NC:
            yield False
        acts_free[:] = [state["last"]]
        r, t = norm_scale(acc1, sums1)
        acc = small(NT * (D // NC)).rearrange("p (t n) -> p t n", t=NT)
        ss = []
        for n in range(D // NC):
            b, tb = resid[n]
            for i in range(NT):
                s = slice(i * NC, (i + 1) * NC)
                e = stt("x2", b.t[:, s], b.t[:, s], r[:, i:i + 1],
                        final_w[n // 2].t[:, (n % 2) * NC:(n % 2 + 1) * NC], ALU.mult, ALU.mult, tb, t, t_final[n // 2])
            kept[n] = load(f"x2_store{n}", x2_dram[:, :, n * NC:(n + 1) * NC], b.t.rearrange("p (t n) -> p t n", t=NT), e, q=sp)
            ss.append((yield from square_sums(n, b, acc, e)))
            give(b, ss[-1], kept[n])
        for b in final_w:
            give(b, e)
        resid.clear()
        r2, t2 = norm_scale(acc, ss)
        both = small(NT)
        set_scale("u2", both, tt(dve, "norm_both", both, r, r2, ALU.mult, t, t2))
        x_ready["u2"] = True

    final_w, t_final = [], []

    def load_final_w(name, *after):
        for i in range(2):
            b = yield from take()
            final_w.append(b)
            t_final.append(load(f"{name}{i}", b.t, a[name][i * BLK:(i + 1) * BLK].unsqueeze(0).broadcast_to([P, BLK]),
                                b.free))

    H = acts[:, KD:2 * KD, :].rearrange("p k t -> p (k t)")
    line_dram = nc.dram_tensor("rel_line", (AT_H, 2 * T), F32, kind="Internal").ap()
    Hv = H[:, 0:8 * BAND].rearrange("p (h j) -> p h j", h=8)
    hband = {}

    def rel_line():
        b = yield from take()
        o = yield from take()
        tab, hot = b.t[0:33, 0:AT_H], o.t[0:33, 0:2 * T]
        t0 = dve.do("rel_ones", lambda e: e.memset(b.t[32:33, 0:AT_H], 1.0), b.free)
        t1 = load("rel_table", b.t[0:32, 0:AT_H], a["rel_bias_table_2"][:, :], b.free)
        t2 = load("rel_hot", hot, a["const_rel"][:, :], o.free)
        p = yield from bank()
        m = mm("rel_line", p.t[0:AT_H, :], tab, hot, t0, t1, t2, p.free)
        e = copy(dve, "rel_line", b.t[0:AT_H, NC:2 * NC], p.t[0:AT_H, :], m)
        done_with(p, e)
        give(o, m)
        e = load("rel_store", line_dram[:, :], b.t[0:AT_H, NC:2 * NC], e)
        give(b, e)
        hband["stored"] = e
        yield True

    def load_band(half, *after):
        src = bass.AP(tensor=line_dram.tensor, offset=half * 8 * 2 * T, ap=[[1, P], [2 * T, 8], [1, BAND]])
        hband[half] = load(f"rel_band{half}", Hv, src, hband["stored"], after)

    gens.append(rel_line())

    def second_constants():
        t = load("second_constants", cst2[:, 0:4 * P], a["const_second"][:, :], state["last_first"])
        hband["c2"] = t
        while "stored" not in hband:
            yield False
        load_band(0, acts_free)
        yield True

    at_ready = {}

    def attention(half):
        (qr, tq), (kr, tk), (v, tv) = yield from need(f"aq{half}", f"ak{half}", f"av{half}")
        qT, tq = yield from to_channels(qr, tq, scale=AT_D ** -0.5)
        kT, tk = yield from to_channels(kr, tk)
        while half not in hband:
            yield False
        o = yield from take()
        ov = o.t.rearrange("p (t h d) -> p t h d", t=NT, h=8)
        t_o = []
        po = None
        sums = small(NT * 8).rearrange("p (h t) -> p h t", t=NT)
        for h in range(8):
            c, base = h // 2, (h % 2) * AT_D
            rows_ = slice(base, base + AT_D)
            p = yield from bank()
            for i in range(NT):
                mm("at_logits", p.t[:, i * T:(i + 1) * T], qT.t[rows_, c * T + i * P:c * T + (i + 1) * P],
                   kT.t[rows_, c * T:(c + 1) * T], tq, tk, p.free, stop=False)
                m = mm("at_logits", p.t[:, i * T:(i + 1) * T], FLIP, Hv[:, h, P - i * P:P - i * P + T], hband[half],
                       hband["c2"], start=False)
            E = yield from take()
            mx, nm = small(NT), small(NT)
            e = reduce("at_max", mx, p.t[:, :].rearrange("p (i k) -> p i k", i=NT), ALU.max, m)
            e = ts("at_negmax", nm, mx, -1.0, ALU.mult, None, None, e)
            for i in range(NT):
                x = func("at_exp", ACT.Exp, E.t[:, i * T:(i + 1) * T], p.t[:, i * T:(i + 1) * T], e, E.free,
                         bias=nm[:, i:i + 1], accum_out=sums[:, h, i:i + 1])
            done_with(p, x)
            m_band = m
            yield True
            p = yield from bank()
            for kt_ in range(NT):
                for i in range(NT):
                    m = turn("at_turned", p.t[:, kt_ * T + i * P:kt_ * T + (i + 1) * P],
                             E.t[:, i * T + kt_ * P:i * T + (kt_ + 1) * P], x, p.free)
            e = copy(dve, "at_turned", E.t[:, NC:2 * NC], p.t[:, :], m)
            done_with(p, e)
            yield True
            if h % 4 == 0:
                po = yield from bank()
            for i in range(NT):
                for kt_ in range(NT):
                    m = mm("at_pv", po.t[:, ((h % 4) * NT + i) * AT_D:((h % 4) * NT + i + 1) * AT_D],
                           E.t[:, NC + kt_ * T + i * P:NC + kt_ * T + (i + 1) * P],
                           v.t[:, kt_ * NC + h * AT_D:kt_ * NC + (h + 1) * AT_D], e, tv, po.free,
                           start=kt_ == 0, stop=kt_ == 1)
            give(E, m)
            if h % 4 == 3:
                inv = small(NT * 4).rearrange("p (h t) -> p h t", t=NT)
                e = dve.do("at_inv", lambda q, inv=inv, s=sums[:, h - 3:h + 1]: q.reciprocal(inv, s), x)
                for i in range(NT):
                    pv = po.t[:, :].rearrange("p (h t d) -> p h t d", h=4, t=NT)[:, :, i]
                    t_o.append(tt(dve, "at_out", ov[:, i, h - 3:h + 1], pv, over(inv[:, :, i], 2, AT_D), ALU.mult,
                                  m, e, o.free))
                done_with(po, t_o)
            yield True
        give(qT, m)
        give(kT, m)
        give(v, m)
        if half == 0:
            load_band(1, m_band)
        th = []
        for c in range(0, 4, 2):
            p = yield from bank()
            for cc in range(2):
                for i in range(NT):
                    m = turn("at_out", p.t[:, cc * T + i * P:cc * T + (i + 1) * P],
                             o.t[:, i * NC + (c + cc) * P:i * NC + (c + cc + 1) * P], t_o, p.free)
            th.append(copy(act, "at_out", acts[:, 4 * half + c:4 * half + c + 2, :],
                           p.t[:, :].rearrange("p (c t) -> p c t", c=2), m, acts_free))
            done_with(p, th)
            yield True
        give(o, m)
        at_ready[half] = th

    gl = {}
    NCH = T // GL_C

    def gla_gates(pair, t):
        r, _, tr = yield from scale_of("u2")
        b = yield from take()
        bv = b.t[:, 0:64].rearrange("p (t n) -> p t n", t=NT)
        for i in range(NT):
            e = ts("gla_rank", bv[:, i], pair.t[i][:, 0:32], r[:, i:i + 1], ALU.mult, None, None, t, tr, b.free)
        pair.free = [e]
        w = yield from take()
        wv = w.t[0:GL_R, :].rearrange("p (d n) -> p d n", d=2)
        bi = yield from take()
        biv = bi.t[0:1, :].rearrange("p (d n) -> p d n", d=2)
        for d_, s in enumerate(("fwd", "bwd")):
            tl = (load("gla_gate_w", wv[:, d_], a[f"gla_gate_w_{s}_2"][0], w.free))
            tl = load("gla_gate_w", biv[:, d_], a[f"gla_gate_b_{s}_2"], bi.free)
        p = yield from bank()
        for d_ in range(2):
            for i in range(NT):
                m = turn("gla_rank", p.t[0:GL_R, d_ * T + i * P:d_ * T + (i + 1) * P],
                         bv[:, i, d_ * GL_R:(d_ + 1) * GL_R], e, p.free)
        lr = b.t[0:GL_R, NC:2 * NC]
        e = copy(dve, "gla_rank", lr, p.t[0:GL_R, :], m)
        done_with(p, e)
        yield True
        la = (yield from take_some(2))
        tla = []
        for d_ in range(2):
            for i in range(NT):
                p = yield from bank()
                mm("gla_gate", p.t[:, :], lr[:, d_ * T + i * P:d_ * T + (i + 1) * P], wv[:, d_], e, tl, p.free, stop=False)
                m = mm("gla_gate", p.t[:, :], ONE[0:1, :], biv[:, d_], start=False)
                o = la[d_].t[:, i * NC:(i + 1) * NC]
                x = func("gla_abs", ACT.Abs, o, p.t[:, :], m, la[d_].free)
                x = func("gla_exp", ACT.Exp, o, o, x, scale=-1.0)
                x = func("gla_ln", ACT.Ln, o, o, x, bias=1.0)
                x = stt("gla_log", o, p.t[:, :], 0.0, o, ALU.min, ALU.subtract, x)
                done_with(p, x)
                tla.append(x)
                yield True
        give(b, m)
        give(w, m)
        give(bi, m)
        gl["la"] = (la, tla)

    def gla(hp):
        if hp == 0:
            (qr, tq), (kr, tk) = yield from need("gq", "gk")
            qT, tq = yield from to_channels(qr, tq, scale=GL_DK ** -0.5)
            kT, tk = yield from to_channels(kr, tk)
            gl["qk"] = (qT, kT, tq, tk)
        while "qk" not in gl or "la" not in gl or "c2" not in hband:
            yield False
        qT, kT, tq, tk = gl["qk"]
        la, tla = gl["la"]
        (v, tv), = yield from need(f"gv{hp}")
        cols = slice(2 * hp * T, (2 * hp + 2) * T)
        q_in, k_in, kend = (yield from take()), (yield from take()), (yield from take())
        dec = small(2 * 2 * NCH).rearrange("p (d h c) -> p d h c", d=2, h=2)
        t_in, t_ke, t_dec = [], [], []
        for d_ in range(2):
            p = yield from bank()
            for hh in range(2):
                for i in range(NT):
                    h = 2 * hp + hh
                    m = mm("gla_sum", p.t[:, hh * T + i * P:hh * T + (i + 1) * P],
                           la[d_].t[:, i * NC + h * P:i * NC + (h + 1) * P], (CUMF, CUMB)[d_], tla, hband["c2"], p.free)
            pc = p.t[:, :].rearrange("p (h c t) -> p h c t", h=2, c=NCH)
            end = GL_C - 1 if d_ == 0 else 0
            gend = small(2 * NCH)
            e = copy(dve, "gla_end", gend, p.t[:, end::GL_C], m)
            t_dec.append(func("gla_dec", ACT.Exp, dec[:, d_].rearrange("p h c -> p (h c)"), gend, e, scale=1.0 / GL_TAU))
            s = slice(d_ * NC, (d_ + 1) * NC)
            x1 = func("gla_eq", ACT.Exp, q_in.t[:, s], p.t[:, :], e, q_in.free, scale=1.0 / GL_TAU)
            x2 = func("gla_eq", ACT.Exp, k_in.t[:, s], p.t[:, :], e, k_in.free, scale=-1.0 / GL_TAU)
            x3 = tt(dve, "gla_rest", kend.t[:, s].rearrange("p (g t) -> p g t", t=GL_C), over(gend, 2, GL_C),
                    p.t[:, :].rearrange("p (g t) -> p g t", t=GL_C), ALU.subtract, x2, kend.free)
            done_with(p, x1, x2, x3)
            x3 = func("gla_eq", ACT.Exp, kend.t[:, s], kend.t[:, s], x3, scale=1.0 / GL_TAU)
            t_in.append(tt(dve, "gla_q_in", q_in.t[:, s], q_in.t[:, s], qT.t[:, cols], ALU.mult, x1, tq))
            t_in.append(tt(dve, "gla_k_in", k_in.t[:, s], k_in.t[:, s], kT.t[:, cols], ALU.mult, x2, tk))
            t_ke.append(tt(dve, "gla_k_end", kend.t[:, s], kend.t[:, s], kT.t[:, cols], ALU.mult, x3, tk))
            yield True
        if hp == 1:
            give(qT, t_in, t_ke)
            give(kT, t_in, t_ke)
            for b in la:
                give(b, m)
        p = yield from bank()
        pa = p.t[:, :].rearrange("p (d h t c) -> p d h t c", d=2, h=2, t=NT)
        for d_ in range(2):
            for hh in range(2):
                for n in range(NCH):
                    b0 = (n % 2) * GL_C
                    at_ = slice(d_ * NC + hh * T + n * GL_C, d_ * NC + hh * T + (n + 1) * GL_C)
                    m = mm("gla_scores", pa[b0:b0 + GL_C, d_, hh, n // 2], k_in.t[:, at_], q_in.t[:, at_], t_in, p.free)
        give(k_in, m)
        S = yield from take_some(2)
        Sv = [b.t[:, 0:3 * GL_DV].rearrange("p (n v) -> p n v", n=3) for b in S]
        Av = [b.t[:, 3 * GL_DV:BLK].rearrange("p (g c) -> p g c", c=GL_C) for b in S]
        x = [tt(dve, "gla_masked", Av[d_], p.t[:, d_ * 256:(d_ + 1) * 256].rearrange("p (g c) -> p g c", c=GL_C),
                over((MASKF, MASKB)[d_], 1, 2 * NT), ALU.mult, m, S[d_].free) for d_ in range(2)]
        done_with(p, x)
        t_A = tt(dve, "gla_masked", Av[0], Av[0], Av[1], ALU.add, x)
        yield True
        ke = yield from take()
        kev = ke.t.rearrange("p (d h t k) -> p d h t k", d=2, h=2, t=NT)
        t_k = []
        for d_ in range(2):
            p = yield from bank()
            for hh in range(2):
                for i in range(NT):
                    m = turn("gla_k_end", p.t[:, (hh * NT + i) * P:(hh * NT + i + 1) * P],
                             kend.t[:, d_ * NC + hh * T + i * P:d_ * NC + hh * T + (i + 1) * P], t_ke, p.free)
            t_k.append(copy(act, "gla_k_end", ke.t[:, d_ * NC:(d_ + 1) * NC], p.t[:, :], m, ke.free))
            done_with(p, t_k)
            yield True
        give(kend, m)
        pos = []
        ssq = small(2 * NT).rearrange("p (h t) -> p h t", t=NT)
        go = yield from take()
        for i in range(NT):
            pos.append((yield from bank()))
        m_o = None
        for hh in range(2):
            t_S = [[None] * 3, [None] * 3]
            for d_ in range(2):
                order = range(3) if d_ == 0 else range(3, 0, -1)
                for z, n in enumerate(order):
                    b0 = (n % 2) * GL_C
                    p = yield from bank()
                    m = mm("gla_state", p.t[:, 0:GL_DV], kev[b0:b0 + GL_C, d_, hh, n // 2],
                           v.t[b0:b0 + GL_C, (n // 2) * NC + hh * GL_DV:(n // 2) * NC + (hh + 1) * GL_DV], t_k, tv, p.free)
                    if z == 0:
                        e = copy(dve, "gla_state", Sv[d_][:, 0], p.t[:, 0:GL_DV], m, S[d_].free)
                    else:
                        e = stt("gla_state", Sv[d_][:, z], Sv[d_][:, z - 1], dec[:, d_, hh, n:n + 1], p.t[:, 0:GL_DV],
                                ALU.mult, ALU.add, m, e, t_dec, S[d_].free)
                    done_with(p, e)
                    t_S[d_][z] = e
                    yield True
            for n in range(NCH):
                b0 = (n % 2) * GL_C
                o = pos[n // 2].t[b0:b0 + GL_C, hh * GL_DV:(hh + 1) * GL_DV]
                fr = pos[n // 2].free
                terms = [(Av[0][b0:b0 + GL_C, hh * NT + n // 2, :],
                          v.t[b0:b0 + GL_C, (n // 2) * NC + hh * GL_DV:(n // 2) * NC + (hh + 1) * GL_DV])]
                at_ = lambda d_: slice(d_ * NC + hh * T + n * GL_C, d_ * NC + hh * T + (n + 1) * GL_C)
                if n > 0:
                    terms.append((q_in.t[:, at_(0)], Sv[0][:, n - 1]))
                if n < NCH - 1:
                    terms.append((q_in.t[:, at_(1)], Sv[1][:, NCH - 2 - n]))
                for z, (l, r) in enumerate(terms):
                    m_o = mm("gla_o", o, l, r, t_A, t_S, fr, start=z == 0, stop=z == len(terms) - 1)
            S[0].free, S[1].free = [m_o], [m_o]
            yield True
        for b in (ke, q_in, v, *S):
            give(b, m_o)
        for i in range(NT):
            for hh in range(2):
                x = func("gla_square", ACT.Square, go.t[:, 0:GL_DV], pos[i].t[:, hh * GL_DV:(hh + 1) * GL_DV], m_o,
                         go.free, accum_out=ssq[:, hh, i:i + 1])
                go.free = [x]
        rr = small(2 * NT).rearrange("p (h t) -> p h t", t=NT)
        e = rsqrt("gla_rsqrt", rr.rearrange("p h t -> p (h t)"), ssq.rearrange("p h t -> p (h t)"), 1.0 / GL_DV, x)
        e = tt(dve, "gla_factor", rr, rr, over(scales["u2"][1], 1, 2), ALU.mult, e, scales["u2"][2])
        yield True
        (g, tg), = yield from need(f"gr{hp}")
        for i in range(NT):
            for hh in range(2):
                s = slice(i * NC + hh * GL_DV, i * NC + (hh + 1) * GL_DV)
                e2 = stt("gla_gated", go.t[:, s], pos[i].t[:, hh * GL_DV:(hh + 1) * GL_DV], rr[:, hh, i:i + 1],
                         g.t[:, s], ALU.mult, ALU.mult, e, tg, x)
            done_with(pos[i], e2)
        give(g, e2)
        yield True
        th = []
        for c in range(0, 4, 2):
            p = yield from bank()
            for cc in range(2):
                for i in range(NT):
                    m = turn("gla_out", p.t[:, cc * T + i * P:cc * T + (i + 1) * P],
                             go.t[:, i * NC + (c + cc) * P:i * NC + (c + cc + 1) * P], e2, p.free)
            for cc in range(2):
                k = hp * 4 + c + cc
                th.append(copy(act, "gla_out", acts[:, 8 + k, :], p.t[:, cc * T:(cc + 1) * T], m, acts_free,
                               scale=wcol[:, W_GLA + k:W_GLA + k + 1]))
            done_with(p, th)
            yield True
        give(go, m)
        at_ready[2 + hp] = th

    def j2(c0, done, n=NC):
        jobs.append(product(w2, c0, done, "u2", n))

    j2(C_GQ, keep("gq", "u2"))
    j2(C_GL, gla_gates, 2 * GL_R)
    j2(C_GK, keep("gk", "u2"))
    j2(C_GV, keep("gv0", "u2", then=lambda: gla(0)))
    j2(C_GR, keep_silu2("gr0", "u2"))
    j2(C_AQ, keep("aq0", "u2"))
    j2(C_AK, keep("ak0", "u2"))
    j2(C_AV, keep("av0", "u2", then=lambda: attention(0)))
    j2(C_AQ + NC, keep("aq1", "u2"))
    j2(C_AK + NC, keep("ak1", "u2"))
    j2(C_AV + NC, keep("av1", "u2", then=lambda: attention(1)))
    j2(C_GV + NC, keep("gv1", "u2", then=lambda: gla(1)))
    j2(C_GR + NC, keep_silu2("gr1", "u2"))

    acc3 = small(NT * (D // NC)).rearrange("p (t n) -> p t n", t=NT)
    acc4 = small(NT * (D // NC)).rearrange("p (t n) -> p t n", t=NT)
    sums3, sums4 = [], []

    def add_resid(n, acc, sums):
        def done(pair, t):
            if n not in resid:
                b = yield from take(but=tail)
                resid[n] = (b, [load(f"x2_load{n}", b.t.rearrange("p (t n) -> p t n", t=NT),
                                     x2_dram[:, :, n * NC:(n + 1) * NC], b.free, kept[n])])
            b, tb = resid[n]
            for i in range(NT):
                s = slice(i * NC, (i + 1) * NC)
                e = tt(dve, "resid", b.t[:, s], b.t[:, s], pair.t[i][:, :], ALU.add, t, tb)
            pair.free = [e]
            yield True
            sums.append((yield from square_sums(n, b, acc, e)))
            turned = (yield from turn_block("u3", "u2", n, b, W_FFN, e)) if sums is sums3 else None
            resid[n] = (b, [e, turned])
        return done

    for n in range(D // NC):
        jobs.append(Job(columns(a["w_out_2"][0], n * NC), [0, 2, 1, 3], NC, add_resid(n, acc3, sums3),
                        split=lambda k: acts[:, k:k + 2, :], ready=lambda k: at_ready.get(k // 4)))

    def third_norm():
        while len(sums3) < D // NC:
            yield False
        acts_free[:] = [state["last"]]
        r, t = norm_scale(acc3, sums3)
        set_scale("u3", r, t)
        sq = small(NT)
        scales["u3 act"] = (sq, ts("norm_square", sq, scales["u3"][1], 0.0, ALU.add, None, None, scales["u3"][2]))
        t = tt(dve, "norm_square", sq, sq, r, ALU.mult, scales["u3 act"][1])
        scales["u3 act"] = (sq, t)
        got_tail = []
        for b in tail:
            while b not in free_blocks:
                yield False
            free_blocks.remove(b)
            got_tail.append(b.free)
        acts_free.append(got_tail)
        state["tail"] = True

    ffn_ready = {}

    def ffn_up(n):
        def done(pair, t):
            while "u3 act" not in scales:
                yield False
            (g, tg), = yield from need(f"fg{n}")
            for i in range(NT):
                s = slice(i * NC, (i + 1) * NC)
                e = stt("ffn_act", g.t[:, s], g.t[:, s], scales["u3 act"][0][:, i:i + 1], pair.t[i][:, :], ALU.mult,
                        ALU.mult, t, tg, scales["u3 act"][1])
            pair.free = [e]
            yield True
            while "tail" not in state:
                yield False
            th = []
            for c in range(0, 4, 2):
                p = yield from bank()
                for cc in range(2):
                    for i in range(NT):
                        m = turn("ffn_act", p.t[:, cc * T + i * P:cc * T + (i + 1) * P],
                                 g.t[:, i * NC + (c + cc) * P:i * NC + (c + cc + 1) * P], e, p.free)
                k = 4 * n + c
                th.append(copy((act, dve)[c // 2], "ffn_act", acts_all[:, k:k + 2, :],
                               p.t[:, :].rearrange("p (c t) -> p c t", c=2), m, acts_free))
                done_with(p, th[-1])
                yield True
            give(g, m)
            ffn_ready[n] = th
        return done

    for n in range(FFN // NC):
        jobs.append(product(a["w_gate_2"][0], n * NC, keep_silu2(f"fg{n}", "u3"), "u3"))
        jobs.append(product(a["w_up_2"][0], n * NC, ffn_up(n), "u3"))
    for n in range(D // NC):
        jobs.append(Job(columns(a["w_down_2"][0], n * NC), list(range(KF // CH)), NC, add_resid(n, acc4, sums4),
                        split=lambda k: acts_all[:, k:k + 2, :], ready=lambda k: ffn_ready.get(k // 4)))

    def last_norm():
        while "tail" not in state:
            yield False
        final_w.clear()
        t_final.clear()
        yield from load_final_w("final_norm_w_2")
        wb, tw = final_w, t_final
        while len(sums4) < D // NC:
            yield False
        r, t = norm_scale(acc4, sums4)
        for n in range(D // NC):
            b, tb = resid[n]
            for i in range(NT):
                s = slice(i * NC, (i + 1) * NC)
                e = stt("final", b.t[:, s], b.t[:, s], r[:, i:i + 1], wb[n // 2].t[:, (n % 2) * NC:(n % 2 + 1) * NC],
                        ALU.mult, ALU.mult, tb, t, tw[n // 2])
            stored.append(load(f"store{n}", out[0, :, n * NC:(n + 1) * NC].rearrange("(t p) n -> p t n", p=P),
                               b.t.rearrange("p (t n) -> p t n", t=NT), e, q=sp))

    stored = []

    def background():
        while len(resid) < 1:
            yield False
        yield from load_final_w("final_norm_w")
        yield from second_norm()
        state["last_first"] = state["last"]
        yield from second_constants()
        yield from third_norm()
        yield from last_norm()

    def beside():
        g = background()
        while True:
            try:
                r = next(g)
            except StopIteration:
                return
            yield r

    urgent.append(beside())
    run_jobs(jobs)
    settle(lambda: len(stored) == D // NC and not gens)

    block = ctx.enter_context(nc.Block())

    @block.sync
    def _(e):
        sp.play(e)
        for t in stored:
            e.wait_ge(t.sem, t.value)

    @block.tensor
    def _(e):
        pe.play(e)

    @block.scalar
    def _(e):
        act.play(e)

    @block.vector
    def _(e):
        dve.play(e)

    @block.gpsimd
    def _(e):
        pool.play(e)


_INS = ["x", "norm_w", "w_in", "ml_i_bias", "ml_f_bias", "ml_norm_w", "dn_conv_w", "dn_a_log", "dn_dt_bias",
        "dn_norm_w", "w_out", "final_norm_w", "attn_norm_w_2", "w_in_2", "rel_bias_table_2", "gla_gate_w_fwd_2",
        "gla_gate_b_fwd_2", "gla_gate_w_bwd_2", "gla_gate_b_bwd_2", "gla_norm_w_2", "w_out_2", "ffn_norm_w_2",
        "w_gate_2", "w_up_2", "w_down_2", "final_norm_w_2"]


def kernel(**inputs):
    import numpy as _np
    import concourse.bacc as _bacc
    from concourse import mybir as _mybir
    from concourse.bass_utils import run_bass_kernel_spmd as _run

    nc = _bacc.Bacc("TRN2", target_bir_lowering=False, num_devices=1)
    given = {n: inputs[n] for n in _INS}
    given.update(host_constants())
    arrays, args = {}, {}
    for name, value in given.items():
        v = _np.ascontiguousarray(value)
        arrays[f"in_{name}_dram"] = v
        args[name] = nc.dram_tensor(f"in_{name}_dram", v.shape, _mybir.dt.from_np(v.dtype), kind="ExternalInput").ap()
    out = nc.dram_tensor("out_0_dram", (1, T, D), _mybir.dt.float32, kind="ExternalOutput").ap()
    build(nc, args, out)
    r = _run(nc, [arrays], core_ids=[0])
    return r.results[0]["out_0_dram"]
```

```python
from contextlib import ExitStack

import numpy as np
import concourse.bass as bass
from concourse import mybir

F32 = mybir.dt.float32
F32R = mybir.dt.float32r
ACT = mybir.ActivationFunctionType
ALU = mybir.AluOpType
AX = mybir.AxisListType.X

P = 128
T = 256
NT = T // P
D = 2048
KD = D // P
NC = 512
EPS = 1e-6

ML_H, ML_DK, ML_DV = 8, 128, 256
DN_H, DN_D = 16, 128
DN_W = DN_H * DN_D
CONV = 4
CAP = 15.0
C_MQ = 0
C_MK = C_MQ + ML_H * ML_DK
C_MV = C_MK + ML_H * ML_DK
C_MO = C_MV + ML_H * ML_DV
C_MZ = C_MO + ML_H * ML_DV
C_MI = C_MZ + ML_H * ML_DV
C_DQ = C_MI + 2 * ML_H
C_DK = C_DQ + DN_W
C_DV = C_DK + DN_W
C_DZ = C_DV + DN_W
C_DB = C_DZ + DN_W
C_GA = C_DB + 2 * DN_H
C_GB = C_GA + D

AT_H, AT_D = 16, 64
GL_H, GL_DK, GL_DV, GL_R, GL_C = 4, 128, 256, 16, 64
GL_TAU = 16.0
C_AQ = 0
C_AK = C_AQ + AT_H * AT_D
C_AV = C_AK + AT_H * AT_D
C_GQ = C_AV + AT_H * AT_D
C_GK = C_GQ + GL_H * GL_DK
C_GV = C_GK + GL_H * GL_DK
C_GR = C_GV + GL_H * GL_DV
C_GL = C_GR + GL_H * GL_DV
FFN = 5632
KF = FFN // P

CH = 4
RAW = 3
RING = 4
AHEAD = 3
LAHEAD = 2
LRING = LAHEAD + 1
NBLK = 15
BLK = 1024
NEG = -1e30
LEVELS = 7
BAND = 3 * P
BANDS = 10


def host_constants():
    r = np.arange(P)[:, None]
    c = np.arange(P)[None, :]
    f = np.float32
    base = [(r == c), (r > c), (r <= c), np.ones((P, P))]
    levels = []
    for l in range(LEVELS):
        w = 2 << l
        levels.append((r // w == c // w) & (r % w < w // 2) & (c % w >= w // 2))
    first = base + levels + [np.where(c > r, NEG, 0.0)]
    same = r // GL_C == c // GL_C
    h = np.arange(GL_C)[None, :]
    second = [same & (r <= c), same & (r >= c), r + c == P - 1,
              np.concatenate([r % GL_C <= h, r % GL_C >= h], axis=1)]
    rel = np.arange(2 * T) - (T - 1)
    half, exact, far = 16, 8, 1024
    n = np.abs(rel)
    large = exact + (np.log(np.maximum(n, 1) / exact) / np.log(far / exact) * (half - exact)).astype(np.int64)
    bucket = np.where(rel > 0, half, 0) + np.where(n < exact, n, np.minimum(large, half - 1))
    times = (n <= 64).astype(np.int64) + (n % 4 == 0) + (n % 16 == 0)
    hot = np.zeros((33, 2 * T), f)
    hot[bucket, np.arange(2 * T)] = 1.0
    hot[32] = np.where(times > 0, np.log(np.maximum(times, 1)), NEG)
    return {"const_first": np.concatenate([np.asarray(m, f) for m in first], axis=1),
            "const_second": np.concatenate([np.asarray(m, f) for m in second], axis=1),
            "const_rel": hot}


class Token:

    def __init__(self, sem, value):
        self.sem, self.value = sem, value


def flat(tokens):
    for t in tokens:
        if isinstance(t, (list, tuple)):
            yield from flat(t)
        elif t is not None:
            yield t


class Queue:

    def __init__(self, nc, ctx, name):
        self.nc, self.ctx, self.name = nc, ctx, name
        self.items, self.sems, self.seen = [], {}, {}

    def do(self, stage, fn, *after, inc=1):
        waits = []
        for t in flat(after):
            if self.seen.get(id(t.sem), 0) < t.value:
                self.seen[id(t.sem)] = t.value
                waits.append((t.sem, t.value))
        if stage is None:
            self.items.append((waits, fn, None, 0))
            return None
        if inc == 1:
            stage = stage.split("_")[0]
        if stage not in self.sems:
            self.sems[stage] = [self.ctx.enter_context(self.nc.semaphore(f"{self.name}_{stage}")), 0]
        s = self.sems[stage]
        s[1] += inc
        self.items.append((waits, fn, s[0], inc))
        return Token(s[0], s[1])

    def play(self, eng):
        for waits, fn, sem, inc in self.items:
            for s, v in waits:
                eng.wait_ge(s, v)
            ins = fn(eng)
            if sem is not None:
                ins.then_inc(sem, inc)


class Place:

    def __init__(self, t):
        self.t, self.free = t, []


def over(ap, axis, n):
    ap = ap.unsqueeze(axis)
    shape = list(ap.shape)
    shape[axis] = n
    return ap.broadcast_to(shape)


class Job:

    def __init__(self, load, chunks, n, done, lhs=None, split=None, ready=lambda k: [], key=None):
        self.load, self.chunks, self.n, self.done, self.key = load, chunks, n, done, key
        self.narrow = n < P
        self.half = KD // 2 if self.narrow else CH // 2
        self.lhs, self.split, self.ready = lhs, split, ready


def build(nc, a, out):
    with ExitStack() as ctx:
        _build(nc, ctx, a, out)


def _build(nc, ctx, a, out):
    def sb(name, shape, dt=F32):
        return ctx.enter_context(nc.sbuf_tensor(name, shape, dt))

    pe, act, dve, pool, sp = (Queue(nc, ctx, n) for n in ("pe", "act", "dve", "pool", "sp"))

    raw = sb("weight_raw", [P, RAW, CH * NC])
    whi = sb("weight_hi", [P, RING, 2 * NC], F32R)
    wlo = sb("weight_lo", [P, RING, 2 * NC], F32R)
    lhi = sb("lhs_hi", [P, LRING, 2, T], F32R)
    llo = sb("lhs_lo", [P, LRING, 2, T], F32R)
    xhi = sb("x_hi", [P, KD, T], F32R)
    xlo = sb("x_lo", [P, KD, T], F32R)
    arena = sb("arena", [P, 2 * KD * T + NBLK * BLK])
    cst = sb("constants", [P, 4 * P])
    cst2 = sb("phase_constants", [P, (LEVELS + 1) * P])
    wcol = sb("norm_columns", [P, 112])
    cwcol = sb("conv_columns", [P, 2 * 96])
    gt = sb("gate_work", [P, 10, 2, 48])
    sm = sb("stats", [P, 900])

    acts = arena[:, 0:2 * KD * T].rearrange("p (k t) -> p k t", t=T)
    acts_all = arena[:, 0:KF * T].rearrange("p (k t) -> p k t", t=T)
    blocks = [Place(arena[:, 2 * KD * T + i * BLK:2 * KD * T + (i + 1) * BLK]) for i in range(NBLK)]
    tail = blocks[:3]
    free_blocks = list(blocks)
    acts_free = []

    IDN, STR, INC, ONE = (cst[:, i * P:(i + 1) * P] for i in range(4))
    LVL = [cst2[:, i * P:(i + 1) * P] for i in range(LEVELS)]
    NEGM = cst2[:, LEVELS * P:(LEVELS + 1) * P]
    CUMF, CUMB, FLIP = (cst2[:, i * P:(i + 1) * P] for i in range(3))
    MASKF, MASKB = cst2[:, 3 * P:3 * P + GL_C], cst2[:, 3 * P + GL_C:4 * P]

    pairs = [Place([ctx.enter_context(nc.psum_tensor(f"gemm_{i}_{j}", [P, NC], F32)) for j in range(NT)])
             for i in range(2)]
    banks = [Place(ctx.enter_context(nc.psum_tensor(f"side_{i}", [P, NC], F32))) for i in range(4)]
    free_banks = list(banks)

    def take(but=()):
        while not any(b not in but for b in free_blocks):
            yield False
        b = next(b for b in free_blocks if b not in but)
        free_blocks.remove(b)
        return b

    def take_some(n):
        r = []
        for _ in range(n):
            r.append((yield from take()))
        return r

    def give(b, *readers):
        b.free = [readers]
        free_blocks.append(b)

    def bank():
        while not free_banks:
            yield False
        return free_banks.pop(0)

    def done_with(b, *readers):
        b.free = [readers]
        free_banks.append(b)

    stat = [0]

    def small(n):
        assert stat[0] + n <= 900, stat
        stat[0] += n
        return sm[:, stat[0] - n:stat[0]]

    def copy(q, stage, o, i, *after, scale=None):
        if q is act:
            return act.do(stage, lambda e: e.activation(o, i, ACT.Copy, scale=1.0 if scale is None else scale), *after)
        return q.do(stage, lambda e: e.tensor_copy(o, i), *after)

    def func(stage, f, o, i, *after, **kw):
        return act.do(stage, lambda e: e.activation(o, i, f, **kw), *after)

    def tt(q, stage, o, x, y, op, *after):
        return q.do(stage, lambda e: e.tensor_tensor(o, x, y, op), *after)

    def ts(stage, o, x, s1, op0, s2, op1, *after):
        if op1 is None:
            return dve.do(stage, lambda e: e.tensor_scalar(o, x, s1, None, op0), *after)
        return dve.do(stage, lambda e: e.tensor_scalar(o, x, s1, s2, op0, op1), *after)

    def stt(stage, o, x, s, y, op0, op1, *after):
        return dve.do(stage, lambda e: e.scalar_tensor_tensor(out=o, in0=x, scalar=s, in1=y, op0=op0, op1=op1), *after)

    def reduce(stage, o, i, op, *after):
        return dve.do(stage, lambda e: e.tensor_reduce(o, i, AX, op), *after)

    def mm(stage, o, l, r, *after, start=True, stop=True):
        return pe.do(stage, lambda e: e.matmul(o, l, r, start=start, stop=stop), *after)

    def turn(stage, o, i, *after):
        n = i.shape[0]
        return pe.do(stage, lambda e: e.transpose(o, i, IDN[0:n, 0:n]), *after)

    def turn_reversed(stage, o, i, *after):
        return mm(stage, o, i, FLIP, hband["c2"], *after)

    def rsqrt(stage, o, i, mul, *after):
        n = list(i.shape)
        half = over(minus_half[:, 0:1], 2, n[2])[:, 0:1, :].broadcast_to(n) if len(n) == 3 else minus_half[:, 0:1].broadcast_to(n)
        t = ts(stage + "_mean", i, i, mul, ALU.mult, EPS, ALU.add, *after)
        return tt(pool, stage, o, i, half, ALU.pow, t, t_half)

    def load(stage, o, i, *after, q=None):
        return (q or act).do(stage, lambda e: e.dma_start(o, i), *after, inc=16)

    xblk = [free_blocks.pop(0) for _ in range(D // NC)]
    t_x = []

    def load_x():
        n = len(t_x)
        if n < D // NC:
            t_x.append(load(f"x{n}", xblk[n].t.rearrange("p (t n) -> p t n", t=NT),
                            a["x"][0, :, n * NC:(n + 1) * NC].rearrange("(t p) n -> p t n", p=P), q=sp))

    load_x()
    rows = free_blocks.pop(0)
    first_rows, vrows, crows = rows.t[0:KD, 0:P], rows.t[:, P:2 * P], [rows.t[0:96, (2 + i) * P:(3 + i) * P] for i in range(2)]
    W_NORM, W_ATT, W_FFN, W_ML, W_DN, W_GLA, W_FIN = 0, 16, 32, 48, 64, 65, 73
    W_BOTH = W_FIN + KD
    NV = W_BOTH - KD
    t_v = load("first_rows", first_rows, a["norm_w"].rearrange("a (r p) -> (a r) p", p=P))
    t_c = load("constants", cst[:, :], a["const_first"][:, 0:4 * P])
    minus_half = sb("minus_half", [P, 1])
    t_half = dve.do("minus_half", lambda e: e.memset(minus_half[:, :], -0.5))
    pvec = free_banks.pop(0)
    t = turn("norm_columns", pvec.t[:, 0:KD], first_rows, t_c, t_v)
    t_w = [copy(dve, "norm_columns", wcol[:, 0:KD], pvec.t[:, 0:KD], t)]
    done_with(pvec, t_w[0])
    gb = sb("gate_bias", [P, 48])
    t_b, t_c2 = [], []

    def small_inputs():
        at = 0
        for name in ("attn_norm_w_2", "ffn_norm_w_2", "ml_norm_w", "dn_norm_w", "gla_norm_w_2"):
            n = a[name].shape[1] // P
            t_v = load("norm_rows", vrows[at:at + n, :], a[name].rearrange("a (r p) -> (a r) p", p=P))
            at += n
            yield True
        assert at == W_FIN - KD
        t_v = load("norm_rows", vrows[at:at + KD, :], a["final_norm_w"].rearrange("(r p) -> r p", p=P))
        cw = a["dn_conv_w"].rearrange("a j (r p) -> (a j r) p", p=P)
        for i in range(2):
            t_v = load("norm_rows", crows[i], cw[i * 96:(i + 1) * 96, :])
        yield True
        for lo, n, name in ((0, 8, "ml_i_bias"), (8, 8, "ml_f_bias"), (16, 16, "dn_a_log"), (32, 16, "dn_dt_bias")):
            t = load("gate_bias", gb[:, lo:lo + n], a[name].broadcast_to([P, n]))
        t_b.append(t)
        yield True
        p = yield from bank()
        turn("norm_columns", p.t[:, 0:NV], vrows[0:NV, :], t_v, p.free)
        for i in range(2):
            t = turn("norm_columns", p.t[:, P + i * 96:P + (i + 1) * 96], crows[i])
        e = [copy(dve, "norm_columns", wcol[:, KD:W_BOTH], p.t[:, 0:NV], t),
             copy(dve, "norm_columns", cwcol[:, :], p.t[:, P:P + 192], t)]
        done_with(p, e)
        e.append(tt(dve, "norm_columns", wcol[:, W_BOTH:W_BOTH + KD], wcol[:, W_ATT:W_ATT + KD],
                    wcol[:, W_FIN:W_FIN + KD], ALU.mult, e))
        t_w[:] = e
        give(rows, t)
        state["columns"] = True
        t_c2.append(load("phase_constants", cst2[:, :], a["const_first"][:, 4 * P:]))
        yield True

    x_ready = {}
    scales = {}
    uses = {}

    def square_sums(n, b, acc, *after, tiles=(None, None)):
        scratch = yield from bank()
        for i in range(NT):
            s = func("square_sum", ACT.Square, scratch.t[:, :], b.t[:, i * NC:(i + 1) * NC], after, tiles[i], scratch.free,
                     accum_out=acc[:, i, n:n + 1])
            scratch.free = [s]
        done_with(scratch, s)
        return s

    def norm_scale(acc, *after):
        total, r = small(NT), small(NT)
        t = reduce("norm_total", total, acc, ALU.add, *after)
        return r, rsqrt("norm_rsqrt", r, total, 1.0 / D, t)

    def set_scale(key, r, t):
        hr = small(NT)
        scales[key] = (r, hr, [t, ts("norm_half", hr, r, 0.5, ALU.mult, None, None, t)])

    def turn_block(key, before, n, b, wc, *after):
        while before is not None and uses[before][0]:
            yield False
        free = uses[before][1] if before is not None else []
        for c in range(0, NC // P, 2):
            p = yield from bank()
            for cc in range(2):
                for i in range(NT):
                    t = turn("norm_turned", p.t[:, cc * T + i * P:cc * T + (i + 1) * P],
                             b.t[:, i * NC + (c + cc) * P:i * NC + (c + cc + 1) * P], after, p.free, t_c)
            k0 = n * (NC // P) + c
            part = [(k, p.t[:, (k - k0) * T:(k - k0 + 1) * T], wcol[:, wc + k:wc + k + 1]) for k in (k0, k0 + 1)]
            for k, src, w in part:
                hi = func("x_hi", ACT.Copy, xhi[:, k, :], src, t, t_w, free, scale=w)
            for k, src, w in part:
                lo = stt("x_lo", xlo[:, k, :], src, w, xhi[:, k, :].bitcast(F32), ALU.mult, ALU.subtract, t, hi, free)
            done_with(p, hi, lo)
            x_ready[key, k0] = [hi, lo]
            yield True
        return t

    state = {"pair": 0, "heavy": False}
    gens = []
    urgent = []

    def stage_turn():
        while state["heavy"]:
            yield False
        state["heavy"] = True

    def stage_over():
        state["heavy"] = False

    def step_all(limit=4):
        moved = False
        for lst, lim in ((urgent, 99), (gens, limit)):
            for g in list(lst[:lim]):
                try:
                    moved |= next(g) is not False
                except StopIteration:
                    lst.remove(g)
                    moved = True
        return moved

    def settle(until):
        idle = 0
        while not until():
            idle = 0 if step_all(4) else idle + 1
            assert idle < 8, ("nothing moves", len(free_blocks), len(free_banks), sorted(got))

    def run_jobs(jobs):
        halves = [(j, c, h) for j in jobs for c in range(len(j.chunks)) for h in range(2)]
        state_w = {}
        state_l = {}
        chunk_of = []
        for idx, (j, c, h) in enumerate(halves):
            chunk_of.append(idx // 2)
        loaded = {}

        def load_chunk(ci):
            j, c, _ = halves[2 * ci]
            slot = ci % RAW
            view = raw[:, slot, 0:2 * j.half * j.n].rearrange("p (k n) -> p k n", k=2 * j.half)
            prev = [state_w[2 * (ci - RAW) + h][0:2] for h in range(2)] if ci >= RAW else []
            parts = j.load(view, j.chunks[c])
            if ci == 0:
                (dst, src), = parts
                m = j.half
                loaded[ci] = [load(f"weight_start{h}", dst[:, h * m:(h + 1) * m], src[:, h * m:(h + 1) * m], q=sp)
                              for h in range(2)]
                return
            for dst, src in parts:
                t = sp.do(f"weight{slot}", lambda e, dst=dst, src=src: e.dma_start(dst, src), prev, inc=16)
            loaded[ci] = [t, t]

        def split(idx):
            j, c, h = halves[idx]
            ci = idx // 2
            if ci not in loaded:
                load_chunk(ci)
            r = idx % RING
            m = j.half * j.n
            src = raw[:, ci % RAW, h * m:(h + 1) * m]
            hi_t, lo_t = whi[:, r, 0:m], wlo[:, r, 0:m]
            used = state_w[idx - RING][2] if idx >= RING else []
            hi = copy(act, "weight_hi", hi_t, src, loaded[ci][h], used)
            lo = tt(dve, "weight_lo", lo_t, src, hi_t.bitcast(F32), ALU.subtract, hi, used)
            state_w[idx] = [hi, lo, None]
            if h == 1 and 2 * (ci + RAW) < len(halves):
                load_chunk(ci + RAW)

        def split_lhs(idx):
            j, c, h = halves[idx]
            k = j.chunks[c] * CH + 2 * h
            r = idx % LRING
            src = j.split(k)
            used = state_w[idx - LRING][2] if idx >= LRING else []
            hi = copy(act, "lhs_hi", lhi[:, r], src, j.ready(k), used)
            lo = tt(dve, "lhs_lo", llo[:, r], src, lhi[:, r].bitcast(F32), ALU.subtract, hi, used)
            state_l[idx] = [hi, lo]

        for ci in range(min(RAW, len(halves) // 2)):
            load_chunk(ci)
            load_x()
        for idx in range(min(AHEAD, len(halves))):
            split(idx)
            step_all()
        pair = None
        for idx, (j, c, h) in enumerate(halves):
            if idx + AHEAD < len(halves):
                split(idx + AHEAD)
            k0 = (2 * j.chunks[c] + h) * j.half
            settle(lambda: all(j.ready(k) is not None for k in range(k0, k0 + j.half, 2)))
            for look in range(idx, min(idx + LAHEAD + 1, len(halves))):
                jj, cc, hh = halves[look]
                if jj.split is None or look in state_l:
                    continue
                if jj.ready(jj.chunks[cc] * CH + 2 * hh) is None:
                    break
                split_lhs(look)
            if j.split is None:
                parts, made = j.lhs, [j.ready(k) for k in range(k0, k0 + j.half, 2)]
            else:
                r = idx % LRING
                parts = lambda k: (lhi[:, r, k - k0], llo[:, r, k - k0])
                made = state_l[idx]
            if c == 0 and h == 0:
                state["pair"] += 1
                pair = pairs[state["pair"] % 2]
                settle(lambda: pair.free is not None)
                opening = pair.free
                pair.free = None
            r4 = idx % RING
            last = c == len(j.chunks) - 1 and h == 1
            for kk in range(j.half):
                xh, xl = parts(k0 + kk)
                wh = whi[:, r4, kk * j.n:(kk + 1) * j.n]
                wl = wlo[:, r4, kk * j.n:(kk + 1) * j.n]
                if j.narrow:
                    for n3, (l, w) in enumerate(((xh, wh), (xh, wl), (xl, wh))):
                        end = kk == j.half - 1 and n3 == 2
                        t = mm("product" if end else None, pair.t[0][0:j.n, 0:T], w, l, state_w[idx][0:2], made,
                               opening if c == 0 and h == 0 else None,
                               start=(c == 0 and h == 0 and kk == 0 and n3 == 0),
                               stop=(last and end))
                    continue
                for i in range(NT):
                    for n3, (l, w) in enumerate(((xh, wh), (xh, wl), (xl, wh))):
                        end = kk == 1 and i == NT - 1 and n3 == 2
                        t = mm("product" if end else None, pair.t[i][:, 0:j.n], l[:, i * P:(i + 1) * P], w,
                               state_w[idx][0:2], made, opening if c == 0 and h == 0 else None,
                               start=(c == 0 and h == 0 and kk == 0 and n3 == 0), stop=(last and kk == 1 and n3 == 2))
            state_w[idx][2] = t
            state["last"] = t
            if j.key:
                uses[j.key][1] = t
            if last:
                if j.key:
                    uses[j.key][0] -= 1
                urgent.append(j.done(pair, t))
            step_all()

    def columns(w, c0, n=NC):
        def f(view, c):
            rows = view.shape[1] * P
            return [(view, w[c * rows:(c + 1) * rows, c0:c0 + n].rearrange("(k p) n -> p k n", p=P))]
        return f

    def product(w, c0, done, key, n=NC, load=None):
        uses.setdefault(key, [0, None])[0] += 1
        return Job(load or columns(w, c0, n), [0] if n < P else list(range(KD // CH)), n, done,
                   lhs=lambda k: (xhi[:, k], xlo[:, k]), ready=lambda k: x_ready.get((key, k)), key=key)

    got = {}

    def scale_of(key):
        while key not in scales:
            yield False
        return scales[key]

    def keep(key, of, then=None):
        def done(pair, t):
            r, _, tr = yield from scale_of(of)
            b = yield from take()
            e = [func("kept", ACT.Copy, b.t[:, 0:NC], pair.t[0][:, :], t, tr, b.free, scale=r[:, 0:1]),
                 ts("kept", b.t[:, NC:2 * NC], pair.t[1][:, :], r[:, 1:2], ALU.mult, None, None, t, tr, b.free)]
            pair.free = e
            got[key] = (b, e)
            if then is not None:
                gens.append(then())
            yield True
        return done

    def keep_silu2(key, of, then=None):
        def done(pair, t):
            _, hr, tr = yield from scale_of(of)
            b = yield from take()
            for i in range(NT):
                e = func("half_tanh", ACT.Tanh, b.t[:, i * NC:(i + 1) * NC], pair.t[i][:, :], t, tr, b.free,
                         scale=hr[:, i:i + 1])
            yield True
            for i in range(NT):
                bb = b.t[:, i * NC:(i + 1) * NC]
                e2 = stt("silu2", bb, bb, 1.0, pair.t[i][:, :], ALU.add, ALU.mult, e)
            pair.free = [e2]
            got[key] = (b, [e2])
            if then is not None:
                gens.append(then())
            yield True
        return done

    def need(*keys):
        while not all(k in got for k in keys):
            yield False
        return [got.pop(k) for k in keys]

    def to_channels(b, t_b, scale=None, turn=turn):
        o = yield from take()
        view = o.t.rearrange("p (c t) -> p c t", t=T)
        ts_ = []
        for c in range(0, 4, 2):
            p = yield from bank()
            for cc in range(2):
                for i in range(NT):
                    t = turn("to_channels", p.t[:, cc * T + i * P:cc * T + (i + 1) * P],
                             b.t[:, i * NC + (c + cc) * P:i * NC + (c + cc + 1) * P], t_b, p.free)
            e = copy(act, "to_channels", view[:, c:c + 2, :], p.t[:, :].rearrange("p (c t) -> p c t", t=T), t, o.free, scale=scale)
            done_with(p, e)
            ts_.append(e)
            yield True
        give(b, t)
        return o, ts_

    w_in = a["w_in"][0]
    w_out = a["w_out"][0]

    def first_sums():
        acc = small(NT * (D // NC)).rearrange("p (t n) -> p t n", t=NT)
        for n in range(D // NC):
            while ("u1", n * (NC // P)) not in x_ready:
                yield False
            s = yield from square_sums(n, xblk[n], acc, t_x[n])
            yield True
        set_scale("u1", *norm_scale(acc, s))
        state["first_sums"] = s

    def first_turn():
        for n in range(D // NC):
            xblk[n].free = [(yield from turn_block("u1", None, n, xblk[n], W_NORM, t_x[n]))]
        while "first_sums" not in state:
            yield False
        for b in xblk:
            give(b, b.free, state["first_sums"])

    gens += [first_turn(), first_sums(), small_inputs()]

    gates = {}

    def load_gates(view, c):
        return [(view[:, :, 0:16], w_in[:, C_MI:C_MI + 16].rearrange("(k p) n -> p k n", p=P)),
                (view[:, :, 16:48], w_in[:, C_DB:C_DB + 32].rearrange("(k p) n -> p k n", p=P))]

    def narrow_turned(pair, t, n, dst, key, *after):
        r, _, tr = yield from scale_of(key)
        b = yield from take()
        e = copy(dve, "narrow", b.t[0:n, 0:T], pair.t[0][0:n, 0:T], t, b.free)
        pair.free = [e]
        yield True
        p = yield from bank()
        for i in range(NT):
            m = turn("narrow", p.t[:, i * n:(i + 1) * n], b.t[0:n, i * P:(i + 1) * P], e, p.free)
        give(b, m)
        for i in range(NT):
            e = ts("narrow", dst[:, i, :], p.t[:, i * n:(i + 1) * n], r[:, i:i + 1], ALU.mult, None, None, m, tr, after)
        done_with(p, e)
        return e

    def gates_done(pair, t):
        g = [gt[:, i] for i in range(10)]
        v = g[0]
        e = yield from narrow_turned(pair, t, 48, v, "u1")
        th, arg, ex, u, ln, inv, z, res = g[1:9]
        b2 = lambda lo, n: over(gb[:, lo:lo + n], 1, NT)
        t1 = tt(dve, "gate_biased", th[:, :, 0:16], v[:, :, 0:16], b2(0, 16), ALU.add, e, t_b)
        t2 = tt(dve, "gate_z", z[:, :, 0:16], v[:, :, 32:48], b2(32, 16), ALU.add, e, t_b)
        t3 = func("gate_tanh", ACT.Tanh, th[:, :, 0:16], th[:, :, 0:16], t1, scale=1.0 / CAP)
        t4 = ts("gate_arg", arg[:, :, 0:8], th[:, :, 8:16], -CAP, ALU.mult, None, None, t3)
        t5 = ts("gate_arg", arg[:, :, 8:24], v[:, :, 16:32], -1.0, ALU.mult, None, None, e)
        t6 = stt("gate_arg", arg[:, :, 24:40], z[:, :, 0:16], -1.0, z[:, :, 0:16], ALU.mult, ALU.min, t2)
        t7 = func("gate_exp", ACT.Exp, ex[:, :, 0:40], arg[:, :, 0:40], t4, t5, t6)
        ta = func("gate_exp", ACT.Exp, gb[:, 16:32], gb[:, 16:32], t_b)
        t8 = ts("gate_u", u[:, :, 0:40], ex[:, :, 0:40], 1.0, ALU.add, None, None, t7)
        t9 = dve.do("gate_inv", lambda e: e.reciprocal(inv[:, :, 0:40], u[:, :, 0:40]), t8)
        func("gate_ln", ACT.Ln, ln[:, :, 0:8], u[:, :, 0:8], t8)
        tl = func("gate_ln", ACT.Ln, ln[:, :, 24:40], u[:, :, 24:40], t8)
        yield True
        for lo, n in ((0, 8), (24, 16)):
            s = (slice(None), slice(None), slice(lo, lo + n))
            x1 = ts("gate_log1p", arg[s], u[s], -1.0, ALU.add, None, None, t8)
            x2 = tt(dve, "gate_log1p", arg[s], ex[s], arg[s], ALU.subtract, x1)
            x3 = tt(dve, "gate_log1p", arg[s], arg[s], inv[s], ALU.mult, x2, t9)
            x4 = tt(dve, "gate_log1p", arg[s], arg[s], ln[s], ALU.add, x3, tl)
        r1 = ts("gate_i", res[:, :, 0:8], th[:, :, 0:8], CAP, ALU.mult, None, None, t3)
        r2 = ts("gate_f", res[:, :, 8:16], arg[:, :, 0:8], -1.0, ALU.mult, None, None, x4)
        y1 = stt("gate_g", res[:, :, 16:32], z[:, :, 0:16], 0.0, arg[:, :, 24:40], ALU.max, ALU.add, x4)
        y2 = stt("gate_g", res[:, :, 16:32], res[:, :, 16:32], -1.0, over(gb[:, 16:32], 1, NT), ALU.mult, ALU.mult, y1, ta)
        gates.update(i=res[:, :, 0:8], f=res[:, :, 8:16], g=res[:, :, 16:32], beta=inv[:, :, 8:24],
                     t=[r1, r2, y2, t9])
        yield True
        yield True
        p = yield from bank()
        ft = g[9]
        mm("forget_sum", p.t[:, 0:8], INC, res[:, 0, 8:16], gates["t"], p.free)
        mm("forget_sum", p.t[:, 8:16], ONE, res[:, 0, 8:16], stop=False)
        m = mm("forget_sum", p.t[:, 8:16], INC, res[:, 1, 8:16], start=False)
        m = mm("forget_sum", p.t[:, 16:24], INC, res[:, 1, 8:16])
        c = copy(dve, "forget_sum", ft[:, :, 0:8], p.t[:, 0:16].rearrange("p (t h) -> p t h", t=NT), m)
        c = copy(dve, "forget_sum", ft[:, 0, 8:16], p.t[:, 16:24], m)
        done_with(p, c)
        gates.update(F=ft[:, :, 0:8], F1=ft[:, 0, 8:16], tF=[c])
        yield True

    def conv(key, ct):
        (b, tb), = yield from need(key)
        while "columns" not in state:
            yield False
        yield True
        y = yield from take()
        yv = y.t.rearrange("p (c t) -> p c t", t=T)
        fin = []
        for c in range(0, 4, 2):
            p = yield from bank()
            for cc in range(2):
                for i in range(NT):
                    t = turn("conv_turned", p.t[:, cc * T + i * P:cc * T + (i + 1) * P],
                             b.t[:, i * NC + (c + cc) * P:i * NC + (c + cc + 1) * P], tb, p.free)
            yield True
            w = lambda cc, j: cwcol[:, j * 48 + ct + c + cc:j * 48 + ct + c + cc + 1]
            for cc in range(2):
                s0 = func("conv_last_tap", ACT.Copy, yv[:, c + cc, :], p.t[:, cc * T:(cc + 1) * T], t, y.free, t_w,
                          scale=w(cc, CONV - 1))
            for cc in range(2):
                s = s0
                for j in range(1, CONV):
                    s = stt("conv_tap", yv[:, c + cc, j:T], p.t[:, cc * T:(cc + 1) * T - j], w(cc, CONV - 1 - j),
                            yv[:, c + cc, j:T], ALU.mult, ALU.add, s)
                fin.append(s)
            done_with(p, fin)
            yield True
        give(b, t)
        th = yield from take()
        e = func("conv_tanh", ACT.Tanh, th.t, y.t, fin, th.free, scale=0.5)
        e = stt("conv_silu2", y.t, th.t, 1.0, y.t, ALU.add, ALU.mult, e)
        give(th, e)
        got[key + "c"] = (y, [e])
        yield True

    HB = 4
    hb_ready = {}

    def delta(g):
        h0 = g * HB
        (yk, tk), (yq, tq) = yield from need(f"dk{g}c", f"dq{g}c")
        yield from stage_turn()
        beta, gg = gates["beta"], gates["g"]
        hs = slice(h0, h0 + HB)
        ss = small(4 * HB).rearrange("p (q t h) -> p q t h", q=2, t=NT)
        sk = small(NT * HB)
        sq = yield from take()
        e = func("delta_square", ACT.Square, sq.t, yq.t, tq, sq.free)
        kc = yield from take()
        pk = []
        for i in range(NT):
            p = yield from bank()
            for h in range(HB):
                m = turn("delta_k", p.t[:, h * P:(h + 1) * P], yk.t[:, h * T + i * P:h * T + (i + 1) * P], tk, p.free)
            for h in range(HB):
                t_sk = func("delta_square", ACT.Square, kc.t[:, i * NC + h * P:i * NC + (h + 1) * P],
                            p.t[:, h * P:(h + 1) * P], m, kc.free, accum_out=sk[:, i * HB + h:i * HB + h + 1])
            pk.append(p)
        yield True
        p = yield from bank()
        for i in range(NT):
            for h in range(HB):
                m = mm("delta_square_sum", p.t[:, i * HB + h:i * HB + h + 1],
                       sq.t[:, h * T + i * P:h * T + (i + 1) * P], ONE[:, 0:1], e, p.free)
        give(sq, m)
        flat_ = lambda v: v.rearrange("p t h -> p (t h)")
        e = ts("delta_ss", flat_(ss[:, 1]), sk, 0.25, ALU.mult, EPS, ALU.add, t_sk)
        e = ts("delta_ss", flat_(ss[:, 0]), p.t[:, 0:NT * HB], 0.25, ALU.mult, EPS, ALU.add, m)
        done_with(p, e)
        r = small(4 * HB).rearrange("p (q t h) -> p q t h", q=2, t=NT)
        e = tt(pool, "delta_rsqrt", r.rearrange("p q t h -> p (q t h)"), ss.rearrange("p q t h -> p (q t h)"),
               minus_half[:, 0:1].broadcast_to([P, 4 * HB]), ALU.pow, e, t_half)
        rq, rk, ck, hb_ = (small(NT * HB).rearrange("p (t h) -> p t h", t=NT) for _ in range(4))
        t_rq = ts("delta_factor", rq, r[:, 0], 0.5 * DN_D ** -0.5, ALU.mult, None, None, e)
        t_rk = ts("delta_factor", rk, r[:, 1], 0.5, ALU.mult, None, None, e)
        t_ck = tt(dve, "delta_factor", ck, rk, beta[:, :, hs], ALU.mult, t_rk, gates["t"])
        t_hb = ts("delta_factor", hb_, beta[:, :, hs], 0.5, ALU.mult, None, None, gates["t"])
        yield True
        for i, p in enumerate(pk):
            e = tt(dve, "delta_k_scaled", kc.t[:, i * NC:(i + 1) * NC].rearrange("p (h d) -> p h d", h=HB),
                   p.t[:, :].rearrange("p (h d) -> p h d", h=HB), over(ck[:, i], 2, P), ALU.mult, t_ck, t_sk)
            done_with(p, e)
        yield True
        kt = yield from take()
        ktv = kt.t.rearrange("p (h t) -> p h t", h=HB)
        t_kc = []
        for i in range(NT):
            p = yield from bank()
            for h in range(HB):
                m = turn("delta_kc", p.t[:, h * P:(h + 1) * P], kc.t[:, i * NC + h * P:i * NC + (h + 1) * P], e, p.free)
            t_kc.append(copy(act, "delta_kc", ktv[:, :, i * P:(i + 1) * P],
                             p.t[:, :].rearrange("p (h d) -> p h d", h=HB), m, kt.free))
            done_with(p, t_kc)
            yield True
        give(kc, m)
        R0, R1 = (yield from take()), (yield from take())
        R0v, R1v = R0.t.rearrange("p (h t) -> p h t", h=HB), R1.t[:, 0:NC].rearrange("p (h t) -> p h t", h=HB)
        tt(pool, "delta_decay_rhs", R0v[:, :, 0:P], over(INC, 1, HB), over(gg[:, 0, hs], 2, P), ALU.mult,
           R0.free, t_c, gates["t"])
        rc = tt(pool, "delta_decay_rhs", R1v, over(INC, 1, HB), over(gg[:, 1, hs], 2, P), ALU.mult, R1.free)
        E0v, E1v = R0v, R1v
        es = []
        yield True
        rest = small(HB)
        p, p2 = (yield from bank()), (yield from bank())
        m = mm("delta_decay", p2.t[:, 0:HB], STR, gg[:, 0, hs], rc, p2.free)
        e = copy(dve, "delta_rest", rest, p2.t[:, 0:HB], m)
        m0 = mm("delta_decay", p.t[:, :], STR, R0v[:, :, 0:P], p.free)
        m = mm("delta_decay", p2.t[:, :], ONE, R1v, e)
        es.append(func("delta_decay", ACT.Exp, E0v[:, :, 0:P], p.t[:, :].rearrange("p (h t) -> p h t", h=HB), m0))
        done_with(p, es)
        for h in range(HB):
            es.append(func("delta_decay", ACT.Exp, E0v[:, h, P:T], p2.t[:, h * P:(h + 1) * P], m, e,
                           bias=rest[:, h:h + 1]))
        done_with(p2, es)
        p = yield from bank()
        m = mm("delta_decay", p.t[:, :], STR, R1v, rc, p.free)
        es.append(func("delta_decay", ACT.Exp, E1v, p.t[:, :].rearrange("p (h t) -> p h t", h=HB), m))
        done_with(p, es)
        yield True
        e = tt(pool, "delta_masked", E0v[:, :, 0:P], E0v[:, :, 0:P], over(INC, 1, HB), ALU.mult, es)
        e = tt(pool, "delta_masked", E1v, E1v, over(INC, 1, HB), ALU.mult, es)
        e = tt(pool, "delta_masked", E0v, E0v, over(rk[:, 0], 2, T), ALU.mult, e, t_rk)
        t_E = tt(pool, "delta_masked", E1v, E1v, over(rk[:, 1], 2, P), ALU.mult, e)
        P0, B0 = (yield from take()), (yield from take())
        PB1 = yield from take()
        P0v, B0v = (b.t.rearrange("p (h t) -> p h t", h=HB) for b in (P0, B0))
        P1v, B1v = (PB1.t[:, i * NC:(i + 1) * NC].rearrange("p (h t) -> p h t", h=HB) for i in range(2))
        t_P, t_B = [], []
        yield True
        for dst, y, lst in ((B0v, kt, t_B), (P0v, yq, t_P)):
            for n in range(2):
                p = yield from bank()
                for h in range(2 * n, 2 * n + 2):
                    m = mm("delta_scores", p.t[:, (h - 2 * n) * T:(h - 2 * n + 1) * T], yk.t[:, h * T:h * T + P],
                           y.t[:, h * T:(h + 1) * T], tk, tq, t_kc, p.free)
                lst.append(tt(dve, "delta_weights", dst[:, 2 * n:2 * n + 2, :],
                              p.t[:, :].rearrange("p (h t) -> p h t", h=2), E0v[:, 2 * n:2 * n + 2, :], ALU.mult,
                              m, t_E, P0.free, B0.free))
                done_with(p, lst)
                yield True
        for dst, y, lst in ((B1v, kt, t_B), (P1v, yq, t_P)):
            p = yield from bank()
            for h in range(HB):
                m = mm("delta_scores", p.t[:, h * P:(h + 1) * P], yk.t[:, h * T + P:(h + 1) * T],
                       y.t[:, h * T + P:(h + 1) * T], p.free)
            lst.append(tt(dve, "delta_weights", dst, p.t[:, :].rearrange("p (h t) -> p h t", h=HB), E1v, ALU.mult,
                          m, t_E, PB1.free))
            done_with(p, lst)
            yield True
        give(yk, m)
        give(yq, m)
        give(kt, m)
        give(R0, t_P, t_B)
        give(R1, t_P, t_B)
        U, Tt = (yield from take()), (yield from take())
        BM = yield from take()
        Xs = yield from take_some(2)
        units = lambda b: b.t.rearrange("p (g t) -> p g t", t=P)
        half = lambda b, i: b.t[:, i * NC:(i + 1) * NC]
        hv = lambda b, i: half(b, i).rearrange("p (h t) -> p h t", h=HB)
        sides = lambda ap, w, side: ap.rearrange("p (g s x) -> p g s x", s=2, x=w // 2)[:, :, side, :]

        def level(l, *after):
            tt(pool, "delta_level", units(BM)[:, 0:HB], B0v[:, :, 0:P], over(LVL[l], 1, HB), ALU.mult, t_B, BM.free, t_c2,
               after)
            return tt(pool, "delta_level", units(BM)[:, HB:2 * HB], B1v, over(LVL[l], 1, HB), ALU.mult)

        e = level(0)
        t_U = tt(dve, "delta_U", units(U), over(IDN, 1, 2 * HB), units(BM), ALU.subtract, e, U.free)
        t_BM = level(1, t_U)
        t_zero = [pool.do("delta_zero", lambda e, x=x: e.memset(x.t, 0.0), x.free) for x in Xs]
        yield True
        yield True
        t_T = []
        for i in range(NT):
            p = yield from bank()
            for h in range(HB):
                m = turn("delta_T", p.t[:, h * P:(h + 1) * P], hv(U, i)[:, h, :], t_U, p.free)
            t_T.append(copy(act, "delta_T", half(Tt, i), p.t[:, :], m, Tt.free))
            done_with(p, t_T)
        yield True
        for l in range(1, LEVELS):
            w = 2 << l
            last = l == LEVELS - 1
            X, tz = Xs[l % 2], t_zero[l % 2]
            p = yield from bank()
            packed = lambda p, n: p.t[:, n * (P // 2):(n + 1) * (P // 2)].rearrange("p (g x) -> p g x", x=w // 2)
            for n in range(2 * HB):
                m = mm("delta_X", packed(p, n), units(BM)[:, n], sides(units(Tt)[:, n], w, 0), t_BM, t_T, p.free)
            t_X = copy(act, "delta_X", sides(X.t, w, 0), p.t[:, :].rearrange("p (g x) -> p g x", x=w // 2), m, tz)
            done_with(p, t_X)
            if not last:
                t_BM = level(l + 1, m)
            yield True
            p = yield from bank()
            p2 = (yield from bank()) if not last else None
            for n in range(2 * HB):
                m = mm("delta_Y", packed(p, n), units(X)[:, n], sides(units(U)[:, n], w, 1), t_X, t_U, p.free)
            if not last:
                for n in range(2 * HB):
                    m2 = mm("delta_YT", packed(p2, n), units(U)[:, n], sides(units(X)[:, n], w, 0), p2.free)
                t_zero[l % 2] = pool.do("delta_zero", lambda e, X=X: e.memset(X.t, 0.0), m2)
                tl = sides(Tt.t, w, 0)
                t_T = tt(dve, "delta_T", tl, tl, p2.t[:, :].rearrange("p (g x) -> p g x", x=w // 2), ALU.subtract, m2)
                done_with(p2, t_T)
                ur = m2
            else:
                ur = m
            ul = sides(U.t, w, 1)
            t_U = tt(dve, "delta_U", ul, ul, p.t[:, :].rearrange("p (g x) -> p g x", x=w // 2), ALU.subtract, ur)
            done_with(p, t_U)
            yield True
        give(Tt, m)
        give(BM, m)
        for x, tz in zip(Xs, t_zero):
            give(x, m, tz)
        stage_over()
        (yv, tv), = yield from need(f"dv{g}c")
        bv, u = (yield from take()), (yield from take())
        bvv = lambda i: bv.t[:, i * NC:(i + 1) * NC].rearrange("p (h d) -> p h d", h=HB)
        t_bv = []
        for i in range(NT):
            p = yield from bank()
            for h in range(HB):
                m = turn("delta_v", p.t[:, h * P:(h + 1) * P], yv.t[:, h * T + i * P:h * T + (i + 1) * P], tv, p.free)
            t_bv.append(tt(dve, "delta_bv", bvv(i), p.t[:, :].rearrange("p (h d) -> p h d", h=HB),
                           over(hb_[:, i], 2, P), ALU.mult, m, t_hb, bv.free))
            done_with(p, t_bv)
        give(yv, m)
        yield True
        p = yield from bank()
        for h in range(HB):
            m = mm("delta_u", p.t[:, h * P:(h + 1) * P], hv(U, 0)[:, h, :], bvv(0)[:, h, :], t_U, t_bv, p.free)
        t_u0 = copy(act, "delta_u", half(u, 0), p.t[:, :], m, u.free)
        done_with(p, t_u0)
        yield True
        p = yield from bank()
        for h in range(HB):
            m = mm("delta_bu", p.t[:, h * P:(h + 1) * P], B0v[:, h, P:T], hv(u, 0)[:, h, :], t_u0, p.free)
        e = tt(dve, "delta_bv", half(bv, 1), half(bv, 1), p.t[:, :], ALU.subtract, m)
        done_with(p, e)
        yield True
        p = yield from bank()
        for h in range(HB):
            m = mm("delta_u", p.t[:, h * P:(h + 1) * P], hv(U, 1)[:, h, :], bvv(1)[:, h, :], e, p.free)
        t_u1 = copy(act, "delta_u", half(u, 1), p.t[:, :], m)
        done_with(p, t_u1)
        give(bv, m)
        give(U, m)
        give(B0, m)
        o = yield from take()
        t_o = []
        yield True
        for i in range(NT):
            p = yield from bank()
            for h in range(HB):
                if i == 0:
                    m = mm("delta_o", p.t[:, h * P:(h + 1) * P], P0v[:, h, 0:P], hv(u, 0)[:, h, :], t_u0, t_P, p.free)
                else:
                    mm("delta_o", p.t[:, h * P:(h + 1) * P], P0v[:, h, P:T], hv(u, 0)[:, h, :], p.free, stop=False)
                    m = mm("delta_o", p.t[:, h * P:(h + 1) * P], P1v[:, h, :], hv(u, 1)[:, h, :], t_u1, start=False)
            t_o.append(tt(dve, "delta_o", hv(o, i), p.t[:, :].rearrange("p (h d) -> p h d", h=HB),
                          over(rq[:, i], 2, P), ALU.mult, m, t_rq, o.free))
            done_with(p, t_o)
            yield True
        give(P0, m)
        give(PB1, m)
        give(u, m)
        sq = yield from take()
        e = func("delta_o_square", ACT.Square, sq.t, o.t, t_o, sq.free)
        s2, ro = small(NT * HB), small(NT * HB)
        e = reduce("delta_o_sum", s2, sq.t.rearrange("p (g d) -> p g d", d=P), ALU.add, e)
        give(sq, e)
        e = rsqrt("delta_o_rsqrt", ro, s2, 1.0 / DN_D, e)
        rov = ro.rearrange("p (t h) -> p t h", t=NT)
        e = tt(dve, "delta_o_factor", rov, rov, over(scales["u1"][0], 2, HB), ALU.mult, e, scales["u1"][2])
        yield True
        (wz, tz), = yield from need(f"dz{g}")
        e = tt(pool, "delta_o_normed", o.t.rearrange("p (g d) -> p g d", d=P), o.t.rearrange("p (g d) -> p g d", d=P),
               over(ro, 2, P), ALU.mult, e)
        e = stt("delta_o_gated", o.t, wz.t, 0.5, o.t, ALU.mult, ALU.mult, e, tz)
        give(wz, e)
        yield True
        yield True
        t_h = []
        for i in range(NT):
            p = yield from bank()
            for h in range(HB):
                m = turn("delta_out", p.t[:, h * P:(h + 1) * P], hv(o, i)[:, h, :], e, p.free)
            t_h.append(copy(act, "delta_out", acts[:, KD + h0:KD + h0 + HB, i * P:(i + 1) * P],
                            p.t[:, :].rearrange("p (h t) -> p h t", h=HB), m, acts_free, scale=wcol[:, W_DN:W_DN + 1]))
            done_with(p, t_h)
        give(o, m)
        hb_ready[g] = t_h
        yield True

    ml = {}

    def mlstm_scores(G):
        (qr, tq), = yield from need(f"mq{G}")
        (kr, tk), = yield from need(f"mk{G}")
        yield from stage_turn()
        qT, tq = yield from to_channels(qr, tq)
        kT, tk = yield from to_channels(kr, tk)
        hs = slice(G * HB, (G + 1) * HB)
        ig, fg, Fs = gates["i"], gates["f"], gates["F"]
        FI, II = (yield from take()), (yield from take())
        hv = lambda b, i: b.t[:, i * NC:(i + 1) * NC].rearrange("p (h t) -> p h t", h=HB)
        hf = lambda b, i: b.t[:, i * NC:(i + 1) * NC]
        for i in range(NT):
            r1 = tt(pool, "ml_decay_rhs", hv(FI, i), over(STR, 1, HB), over(fg[:, i, hs], 2, P), ALU.mult, FI.free,
                    gates["t"])
            r2 = tt(pool, "ml_decay_rhs", hv(II, i), over(IDN, 1, HB), over(ig[:, i, hs], 2, P), ALU.mult, II.free)
            r = tt(pool, "ml_decay_rhs", hf(FI, i), hf(FI, i), hf(II, i), ALU.add, r1, r2)
        give(II, r)
        yield True
        yield True
        Dd, Dx = (yield from take()), (yield from take())
        mx = small(3 * HB).rearrange("p (n h) -> p n h", h=HB)
        tm = []
        for n, (i, s) in enumerate(((0, 0), (1, 1), (1, 0))):
            p = yield from bank()
            pv = p.t[:, :].rearrange("p (h t) -> p h t", h=HB)
            m = mm("ml_decay", p.t[:, :], INC if i == s else ONE, hf(FI, s), r, p.free)
            if i == s:
                e = tt(dve, "ml_masked", hv(Dd, n), pv, over(NEGM, 1, HB), ALU.add, m, Dd.free, t_c2)
                tm.append(reduce("ml_max", mx[:, n], hv(Dd, n), ALU.max, e))
            else:
                e = tt(dve, "ml_decay", hv(Dx, 0), pv, over(gates["F1"][:, hs], 2, P), ALU.add, m, Dx.free, gates["tF"])
                tm.append(reduce("ml_max", mx[:, n], hv(Dx, 0), ALU.max, e))
            done_with(p, e)
            yield True
        give(FI, m)
        M, nM, em = (small(NT * HB).rearrange("p (t h) -> p t h", t=NT) for _ in range(3))
        e1 = tt(dve, "ml_m", M[:, 0], mx[:, 0], Fs[:, 0, hs], ALU.max, tm, gates["tF"])
        e2 = tt(dve, "ml_m", M[:, 1], mx[:, 1], mx[:, 2], ALU.max, tm)
        e2 = tt(dve, "ml_m", M[:, 1], M[:, 1], Fs[:, 1, hs], ALU.max, e2)
        e3 = ts("ml_m", nM, M, -1.0, ALU.mult, None, None, e1, e2)
        t_em = func("ml_em", ACT.Exp, em, nM, e3)
        tiles = ((0, 0, hv(Dd, 0), hf(Dd, 0)), (1, 1, hv(Dd, 1), hf(Dd, 1)), (1, 0, hv(Dx, 0), hf(Dx, 0)))
        es = []
        for n, (i, s, v, f) in enumerate(tiles):
            for h in range(HB):
                e = func("ml_exp", ACT.Exp, v[:, h], v[:, h], e3, bias=nM[:, i, h:h + 1])
            es.append(e)
            yield True
        dn = small(3 * HB).rearrange("p (n h) -> p n h", h=HB)
        WT = yield from take_some(2)
        wtv = [hv(WT[0], 0), hv(WT[0], 1), hv(WT[1], 0)]
        t_W, t_d = [], []
        for n, (i, s, v, f) in enumerate(tiles):
            p = yield from bank()
            for h in range(HB):
                m = mm("ml_scores", p.t[:, h * P:(h + 1) * P], qT.t[:, h * T + i * P:h * T + (i + 1) * P],
                       kT.t[:, h * T + s * P:h * T + (s + 1) * P], tq, tk, p.free)
            e = stt("ml_weights", f, p.t[:, :], ML_DK ** -0.5, f, ALU.mult, ALU.mult, m, es[n])
            t_d.append(reduce("ml_den", dn[:, n], v, ALU.add, e))
            done_with(p, e)
            yield True
            p = yield from bank()
            for h in range(HB):
                m2 = turn("ml_turned", p.t[:, h * P:(h + 1) * P], v[:, h], e, p.free)
            t_W.append(copy(act, "ml_turned", wtv[n], p.t[:, :].rearrange("p (h t) -> p h t", h=HB), m2, WT[n // 2].free))
            done_with(p, t_W)
            yield True
        give(qT, m)
        give(kT, m)
        give(Dd, m2, t_d)
        give(Dx, m2, t_d)
        den, inv = (small(NT * HB).rearrange("p (t h) -> p t h", t=NT) for _ in range(2))
        e = tt(dve, "ml_den2", dn[:, 1], dn[:, 1], dn[:, 2], ALU.add, t_d)
        e = stt("ml_den2", den, dn[:, 0:2], -1.0, dn[:, 0:2], ALU.mult, ALU.max, e)
        e = tt(dve, "ml_den2", den, den, em, ALU.max, e, t_em)
        e = dve.do("ml_inv", lambda q: q.reciprocal(inv, den), e)
        stage_over()
        ml[G] = dict(W=wtv, WT=WT, tW=t_W, inv=inv, tinv=e, users=[], left=2)
        yield True

    ha_ready = {}

    def mlstm_out(pr):
        G, h0 = pr // 2, 2 * (pr % 2)
        while G not in ml:
            yield False
        s = ml[G]
        (v, tv), = yield from need(f"mv{pr}")
        ssq, rr, fac = (small(NT * 2).rearrange("p (t h) -> p t h", t=NT) for _ in range(3))
        ps = []
        for i in range(NT):
            p = yield from bank()
            for hh in range(2):
                h = h0 + hh
                o = p.t[:, hh * ML_DV:(hh + 1) * ML_DV]
                vv = lambda k: v.t[:, k * NC + hh * ML_DV:k * NC + (hh + 1) * ML_DV]
                if i == 0:
                    m = mm("ml_num", o, s["W"][0][:, h], vv(0), s["tW"], tv, p.free)
                else:
                    mm("ml_num", o, s["W"][2][:, h], vv(0), p.free, stop=False)
                    m = mm("ml_num", o, s["W"][1][:, h], vv(1), start=False)
            ps.append(p)
        s["users"].append(m)
        s["left"] -= 1
        if s["left"] == 0:
            for b in s["WT"]:
                give(b, s["users"])
        give(v, m)
        yield True
        hA = yield from take()
        for i in range(NT):
            for hh in range(2):
                q = func("ml_square", ACT.Square, hA.t[:, 0:ML_DV], ps[i].t[:, hh * ML_DV:(hh + 1) * ML_DV], m,
                         s["tinv"], hA.free, scale=s["inv"][:, i, h0 + hh:h0 + hh + 1], accum_out=ssq[:, i, hh:hh + 1])
                hA.free = [q]
        e = rsqrt("ml_rsqrt", rr.rearrange("p t h -> p (t h)"), ssq.rearrange("p t h -> p (t h)"), 1.0 / ML_DV, q)
        e = stt("ml_factor", fac, rr, 0.25, s["inv"][:, :, h0:h0 + 2], ALU.mult, ALU.mult, e)
        e = tt(dve, "ml_factor", fac, fac, over(scales["u1"][0], 2, 2), ALU.mult, e, scales["u1"][2])
        yield True
        (g, tg), = yield from need(f"mg{pr}")
        for i in range(NT):
            for hh in range(2):
                sl = slice(i * NC + hh * ML_DV, i * NC + (hh + 1) * ML_DV)
                e2 = stt("ml_gated", hA.t[:, sl], ps[i].t[:, hh * ML_DV:(hh + 1) * ML_DV], fac[:, i, hh:hh + 1],
                         g.t[:, sl], ALU.mult, ALU.mult, e, tg, q)
            done_with(ps[i], e2)
        give(g, e2)
        yield True
        th = []
        for c in range(0, 4, 2):
            p = yield from bank()
            for cc in range(2):
                for i in range(NT):
                    m = turn("ml_out", p.t[:, cc * T + i * P:cc * T + (i + 1) * P],
                             hA.t[:, i * NC + (c + cc) * P:i * NC + (c + cc + 1) * P], e2, p.free)
            for cc in range(2):
                k = pr * 4 + c + cc
                th.append(copy(act, "ml_out", acts[:, k, :], p.t[:, cc * T:(cc + 1) * T], m, acts_free,
                               scale=wcol[:, W_ML + k:W_ML + k + 1]))
            done_with(p, th)
            yield True
        give(hA, m)
        ha_ready[pr] = th

    def keep_tanh(key):
        def done(pair, t):
            _, hr, tr = yield from scale_of("u1")
            b = yield from take()
            for i in range(NT):
                e = func("half_tanh", ACT.Tanh, b.t[:, i * NC:(i + 1) * NC], pair.t[i][:, :], t, tr, b.free,
                         scale=hr[:, i:i + 1])
            pair.free = [e]
            got[key] = (b, [e])
            yield True
        return done

    def mlstm_gate(pr):
        def done(pair, t):
            yield from keep_silu2(f"mzz{pr}", "u1")(pair, t)
            (z, tz), (o, to) = yield from need(f"mzz{pr}", f"mo{pr}")
            e = stt("ml_gate", z.t, o.t, 1.0, z.t, ALU.add, ALU.mult, tz, to)
            give(o, e)
            got[f"mg{pr}"] = (z, [e])
            gens.append(mlstm_out(pr))
            yield True
        return done

    jobs = []

    def j1(c0, done):
        jobs.append(product(w_in, c0, done, "u1"))

    def dn_jobs(g):
        j1(C_DK + g * NC, keep(f"dk{g}", "u1", then=lambda: conv(f"dk{g}", DN_W // P + 4 * g)))
        if g == 0:
            jobs.append(product(w_in, 0, gates_done, "u1", 48, load_gates))
        j1(C_DQ + g * NC, keep(f"dq{g}", "u1", then=lambda: conv(f"dq{g}", 4 * g)))
        j1(C_DV + g * NC, keep(f"dv{g}", "u1", then=lambda: conv(f"dv{g}", 2 * DN_W // P + 4 * g)))
        j1(C_DZ + g * NC, keep_silu2(f"dz{g}", "u1", then=lambda: delta(g)))

    def ml_qk(G):
        j1(C_MQ + G * NC, keep(f"mq{G}", "u1"))
        j1(C_MK + G * NC, keep(f"mk{G}", "u1", then=lambda: mlstm_scores(G)))

    def ml_pair(pr):
        j1(C_MV + pr * NC, keep(f"mv{pr}", "u1"))
        j1(C_MO + pr * NC, keep_tanh(f"mo{pr}"))
        j1(C_MZ + pr * NC, mlstm_gate(pr))

    dn_jobs(0)
    ml_qk(0)
    ml_pair(0)
    dn_jobs(1)
    ml_pair(1)
    dn_jobs(2)
    ml_qk(1)
    ml_pair(2)
    dn_jobs(3)
    ml_pair(3)

    resid = {}
    acc1 = small(NT * (D // NC)).rearrange("p (t n) -> p t n", t=NT)
    sums1 = []

    def gated(n, which):
        def done(pair, t):
            (g, tg), = yield from need(f"g{which}{n}")
            for i in range(NT):
                s = slice(i * NC, (i + 1) * NC)
                e = stt("out_gated", g.t[:, s], g.t[:, s], 1.0, pair.t[i][:, :], ALU.add, ALU.mult, tg, t)
            pair.free = [e]
            if which == "b":
                got[f"yb{n}"] = (g, [e])
                yield True
                return
            (b, tb), = yield from need(f"yb{n}")
            x = yield from take()
            tx = load(f"x{n}", x.t.rearrange("p (t n) -> p t n", t=NT),
                      a["x"][0, :, n * NC:(n + 1) * NC].rearrange("(t p) n -> p t n", p=P), x.free, q=act)
            e = tt(pool, "out_sum", b.t, b.t, g.t, ALU.add, e, tb)
            give(g, e)
            yield True
            e = stt("out_resid", x.t, b.t, 0.5, x.t, ALU.mult, ALU.add, e, tx)
            give(b, e)
            sums1.append((yield from square_sums(n, x, acc1, e)))
            yield True
            t = yield from turn_block("u2", "u1", n, x, W_BOTH, e)
            resid[n] = (x, [e, t])
            yield True
        return done

    def out_job(n, k0, ready, done):
        return Job(columns(w_out, n * NC), list(range(k0 // CH, (k0 + KD) // CH)), NC, done,
                   split=lambda k: acts[:, k:k + 2, :],
                   ready=ready)

    def gate_jobs(n):
        j1(C_GB + n * NC, keep_tanh(f"gb{n}"))
        j1(C_GA + n * NC, keep_tanh(f"ga{n}"))

    def y_jobs(n):
        jobs.append(out_job(n, KD, lambda k: hb_ready.get((k - KD) // 4), gated(n, "b")))
        jobs.append(out_job(n, 0, lambda k: ha_ready.get(k // 4), gated(n, "a")))

    for step, n in ((gate_jobs, 0), (gate_jobs, 1), (y_jobs, 0), (gate_jobs, 2), (y_jobs, 1), (gate_jobs, 3),
                    (y_jobs, 2), (y_jobs, 3)):
        step(n)

    w2 = a["w_in_2"][0]
    x2_dram = nc.dram_tensor("x2", (P, NT, D), F32, kind="Internal").ap()
    kept = {}

    def second_norm():
        while len(resid) < D // NC or len(sums1) < D // NC:
            yield False
        acts_free[:] = [state["last"]]
        r, t = norm_scale(acc1, sums1)
        acc = small(NT * (D // NC)).rearrange("p (t n) -> p t n", t=NT)
        ss, xs = [], []
        for n in range(D // NC):
            b, tb = resid[n]
            for i in range(NT):
                s = slice(i * NC, (i + 1) * NC)
                e = stt("x2", b.t[:, s], b.t[:, s], r[:, i:i + 1],
                        final_w[n // 2].t[:, (n % 2) * NC:(n % 2 + 1) * NC], ALU.mult, ALU.mult, tb, t, t_final[n // 2])
            ss.append((yield from square_sums(n, b, acc, e)))
            xs.append((b, e))
        for b in final_w:
            give(b, e)
        resid.clear()
        r2, t2 = norm_scale(acc, ss)
        both = small(NT)
        set_scale("u2", both, tt(dve, "norm_both", both, r, r2, ALU.mult, t, t2))
        for n, (b, e) in enumerate(xs):
            yield True
            kept[n] = load(f"x2_store{n}", x2_dram[:, :, n * NC:(n + 1) * NC], b.t.rearrange("p (t n) -> p t n", t=NT), e)
            give(b, ss[-1], kept[n])

    final_w, t_final = [], []

    def load_final_w(name, *after):
        for i in range(2):
            b = yield from take()
            final_w.append(b)
            t_final.append(load(f"{name}{i}", b.t, a[name][i * BLK:(i + 1) * BLK].unsqueeze(0).broadcast_to([P, BLK]),
                                b.free))

    H = acts[:, KD:2 * KD, :].rearrange("p k t -> p (k t)")
    line_dram = nc.dram_tensor("rel_line", (AT_H, 2 * T), F32, kind="Internal").ap()
    Hv = H[:, 0:BANDS * BAND].rearrange("p (h j) -> p h j", h=BANDS)
    hband = {}

    def rel_line():
        while "F" not in gates:
            yield False
        b = yield from take()
        o = yield from take()
        tab, hot = b.t[0:33, 0:AT_H], o.t[0:33, 0:2 * T]
        t0 = dve.do("rel_ones", lambda e: e.memset(b.t[32:33, 0:AT_H], 1.0), b.free)
        t1 = load("rel_table", b.t[0:32, 0:AT_H], a["rel_bias_table_2"][:, :], b.free)
        t2 = load("rel_hot", hot, a["const_rel"][:, :], o.free)
        yield True
        yield True
        yield True
        p = yield from bank()
        m = mm("rel_line", p.t[0:AT_H, :], tab, hot, t0, t1, t2, p.free)
        e = copy(dve, "rel_line", b.t[0:AT_H, NC:2 * NC], p.t[0:AT_H, :], m)
        done_with(p, e)
        give(o, m)
        e = load("rel_store", line_dram[:, :], b.t[0:AT_H, NC:2 * NC], e)
        give(b, e)
        hband["stored"] = e
        yield True

    def load_band(h0, n, *after):
        src = bass.AP(tensor=line_dram.tensor, offset=h0 * 2 * T, ap=[[1, P], [2 * T, n], [1, BAND]])
        t = load(f"rel_band{h0}", Hv[:, h0 % BANDS:h0 % BANDS + n, :], src, hband["stored"], after)
        for h in range(h0, h0 + n):
            hband[h] = t

    gens.append(rel_line())

    def second_constants():
        t = load("second_constants", cst2[:, 0:4 * P], a["const_second"][:, :], state["last_first"])
        hband["c2"] = t
        while "stored" not in hband:
            yield False
        for h in range(0, BANDS, 2):
            yield True
            load_band(h, 2, acts_free)

    at_ready = {}

    def attention(half):
        (qr, tq), (kr, tk), (v, tv) = yield from need(f"aq{half}", f"ak{half}", f"av{half}")
        while 8 * half + 1 not in hband:
            yield False
        qT, tq = yield from to_channels(qr, tq, scale=AT_D ** -0.5, turn=turn_reversed)
        kT, tk = yield from to_channels(kr, tk)
        o = yield from take()
        ov = o.t.rearrange("p (t h d) -> p t h d", t=NT, h=8)
        t_o = []
        sums = small(NT * 8).rearrange("p (h t) -> p h t", t=NT)
        Es, t_exp, t_turned, po = {}, {}, {}, {}

        def logits(h):
            c, base = h // 2, (h % 2) * AT_D
            rows_ = slice(base, base + AT_D)
            p = yield from bank()
            for i in range(NT):
                m = mm("at_logits", p.t[:, i * T:(i + 1) * T], qT.t[rows_, c * T + i * P:c * T + (i + 1) * P],
                       kT.t[rows_, c * T:(c + 1) * T], tq, tk, p.free)
            E = Es[h] = yield from take()
            mx, nm = small(NT), small(NT)
            head = 8 * half + h
            for i in range(NT):
                e = tt(dve, "at_biased", E.t[:, i * T:(i + 1) * T], p.t[:, i * T:(i + 1) * T],
                       Hv[:, head % BANDS, P - i * P:P - i * P + T], ALU.add, m, E.free, hband[head])
            done_with(p, e)
            if h % 2 == 1 and head + BANDS - 1 < AT_H:
                load_band(head + BANDS - 1, 2, e)
            e = reduce("at_max", mx, E.t[:, 0:NC].rearrange("p (i k) -> p i k", i=NT), ALU.max, e)
            e = ts("at_negmax", nm, mx, -1.0, ALU.mult, None, None, e)
            for i in range(NT):
                t_exp[h] = func("at_exp", ACT.Exp, E.t[:, i * T:(i + 1) * T], E.t[:, i * T:(i + 1) * T], e,
                                bias=nm[:, i:i + 1], accum_out=sums[:, h, i:i + 1])
            return m

        def turned(h):
            E = Es[h]
            p = yield from bank()
            for kt_ in range(NT):
                for i in range(NT):
                    m = turn("at_turned", p.t[:, kt_ * T + i * P:kt_ * T + (i + 1) * P],
                             E.t[:, i * T + kt_ * P:i * T + (kt_ + 1) * P], t_exp[h], p.free)
            t_turned[h] = copy(act, "at_turned", E.t[:, NC:2 * NC], p.t[:, :], m)
            done_with(p, t_turned[h])

        def weighted(h):
            E = Es.pop(h)
            if h % 4 == 0:
                po[0] = yield from bank()
            p = po[0]
            for i in range(NT):
                for kt_ in range(NT):
                    m = mm("at_pv", p.t[:, ((h % 4) * NT + i) * AT_D:((h % 4) * NT + i + 1) * AT_D],
                           E.t[:, NC + kt_ * T + i * P:NC + kt_ * T + (i + 1) * P],
                           v.t[:, kt_ * NC + h * AT_D:kt_ * NC + (h + 1) * AT_D], t_turned[h], tv, p.free,
                           start=kt_ == 0, stop=kt_ == 1)
            give(E, m)
            if h % 4 == 3:
                inv = small(NT * 4).rearrange("p (h t) -> p h t", t=NT)
                e = dve.do("at_inv", lambda q, inv=inv, s=sums[:, h - 3:h + 1]: q.reciprocal(inv, s), t_exp[h])
                for i in range(NT):
                    pv = p.t[:, :].rearrange("p (h t d) -> p h t d", h=4, t=NT)[:, :, i]
                    t_o.append(tt(dve, "at_out", ov[:, i, h - 3:h + 1], pv, over(inv[:, :, i], 2, AT_D), ALU.mult,
                                  m, e, o.free))
                done_with(p, t_o)
            return m

        for s in range(8 + 2):
            if 1 <= s <= 8:
                yield from turned(s - 1)
            if s < 8:
                yield from logits(s)
            if s >= 2:
                m = yield from weighted(s - 2)
            yield True
        give(qT, m)
        give(kT, m)
        give(v, m)
        th = []
        for c in range(0, 4, 2):
            p = yield from bank()
            for cc in range(2):
                for i in range(NT):
                    m = turn_reversed("at_out", p.t[:, cc * T + i * P:cc * T + (i + 1) * P],
                             o.t[:, i * NC + (c + cc) * P:i * NC + (c + cc + 1) * P], t_o, p.free)
            th.append(copy(act, "at_out", acts[:, 4 * half + c:4 * half + c + 2, :],
                           p.t[:, :].rearrange("p (c t) -> p c t", c=2), m, acts_free))
            done_with(p, th)
            yield True
        give(o, m)
        at_ready[half] = th

    gl = {}
    NCH = T // GL_C

    def gla_gates(pair, t):
        b = yield from take()
        bv = b.t[:, 0:64].rearrange("p (t n) -> p t n", t=NT)
        e = yield from narrow_turned(pair, t, 2 * GL_R, bv, "u2", b.free)
        w = yield from take()
        wv = w.t[0:GL_R, :].rearrange("p (d n) -> p d n", d=2)
        bi = yield from take()
        biv = bi.t[0:1, :].rearrange("p (d n) -> p d n", d=2)
        for d_, s in enumerate(("fwd", "bwd")):
            tl = (load("gla_gate_w", wv[:, d_], a[f"gla_gate_w_{s}_2"][0], w.free))
            tl = load("gla_gate_w", biv[:, d_], a[f"gla_gate_b_{s}_2"], bi.free)
        p = yield from bank()
        for d_ in range(2):
            for i in range(NT):
                m = turn("gla_rank", p.t[0:GL_R, d_ * T + i * P:d_ * T + (i + 1) * P],
                         bv[:, i, d_ * GL_R:(d_ + 1) * GL_R], e, p.free)
        lr = b.t[0:GL_R, NC:2 * NC]
        e = copy(dve, "gla_rank", lr, p.t[0:GL_R, :], m)
        done_with(p, e)
        yield True
        yield True
        la = (yield from take_some(2))
        tla = []
        for d_ in range(2):
            for i in range(NT):
                p = yield from bank()
                mm("gla_gate", p.t[:, :], lr[:, d_ * T + i * P:d_ * T + (i + 1) * P], wv[:, d_], e, tl, p.free, stop=False)
                m = mm("gla_gate", p.t[:, :], ONE[0:1, :], biv[:, d_], start=False)
                o = la[d_].t[:, i * NC:(i + 1) * NC]
                x = func("gla_abs", ACT.Abs, o, p.t[:, :], m, la[d_].free)
                x = func("gla_exp", ACT.Exp, o, o, x, scale=-1.0)
                x = func("gla_ln", ACT.Ln, o, o, x, bias=1.0)
                x = stt("gla_log", o, p.t[:, :], 0.0, o, ALU.min, ALU.subtract, x)
                done_with(p, x)
                tla.append(x)
                yield True
        give(b, m)
        give(w, m)
        give(bi, m)
        gl["la"] = (la, tla)

    def gla(hp):
        if hp == 0:
            (qr, tq), (kr, tk) = yield from need("gq", "gk")
            qT, tq = yield from to_channels(qr, tq, scale=GL_DK ** -0.5)
            kT, tk = yield from to_channels(kr, tk)
            gl["qk"] = (qT, kT, tq, tk)
        while "qk" not in gl or "la" not in gl or "c2" not in hband:
            yield False
        qT, kT, tq, tk = gl["qk"]
        la, tla = gl["la"]
        (v, tv), = yield from need(f"gv{hp}")
        cols = slice(2 * hp * T, (2 * hp + 2) * T)
        q_in, k_in, kend = (yield from take()), (yield from take()), (yield from take())
        dec = small(2 * 2 * NCH).rearrange("p (d h c) -> p d h c", d=2, h=2)
        t_in, t_ke, t_dec = [], [], []
        for d_ in range(2):
            p = yield from bank()
            for hh in range(2):
                for i in range(NT):
                    h = 2 * hp + hh
                    m = mm("gla_sum", p.t[:, hh * T + i * P:hh * T + (i + 1) * P],
                           la[d_].t[:, i * NC + h * P:i * NC + (h + 1) * P], (CUMF, CUMB)[d_], tla, hband["c2"], p.free)
            pc = p.t[:, :].rearrange("p (h c t) -> p h c t", h=2, c=NCH)
            end = GL_C - 1 if d_ == 0 else 0
            gend = small(2 * NCH)
            e = copy(dve, "gla_end", gend, p.t[:, end::GL_C], m)
            t_dec.append(func("gla_dec", ACT.Exp, dec[:, d_].rearrange("p h c -> p (h c)"), gend, e, scale=1.0 / GL_TAU))
            s = slice(d_ * NC, (d_ + 1) * NC)
            x1 = func("gla_eq", ACT.Exp, q_in.t[:, s], p.t[:, :], e, q_in.free, scale=1.0 / GL_TAU)
            x2 = func("gla_eq", ACT.Exp, k_in.t[:, s], p.t[:, :], e, k_in.free, scale=-1.0 / GL_TAU)
            x3 = tt(dve, "gla_rest", kend.t[:, s].rearrange("p (g t) -> p g t", t=GL_C), over(gend, 2, GL_C),
                    p.t[:, :].rearrange("p (g t) -> p g t", t=GL_C), ALU.subtract, x2, kend.free)
            done_with(p, x1, x2, x3)
            x3 = func("gla_eq", ACT.Exp, kend.t[:, s], kend.t[:, s], x3, scale=1.0 / GL_TAU)
            t_in.append(tt(dve, "gla_q_in", q_in.t[:, s], q_in.t[:, s], qT.t[:, cols], ALU.mult, x1, tq))
            t_in.append(tt(dve, "gla_k_in", k_in.t[:, s], k_in.t[:, s], kT.t[:, cols], ALU.mult, x2, tk))
            t_ke.append(tt(dve, "gla_k_end", kend.t[:, s], kend.t[:, s], kT.t[:, cols], ALU.mult, x3, tk))
            yield True
        if hp == 1:
            give(qT, t_in, t_ke)
            give(kT, t_in, t_ke)
            for b in la:
                give(b, m)
        yield True
        p = yield from bank()
        pa = p.t[:, :].rearrange("p (d h t c) -> p d h t c", d=2, h=2, t=NT)
        for d_ in range(2):
            for hh in range(2):
                for n in range(NCH):
                    b0 = (n % 2) * GL_C
                    at_ = slice(d_ * NC + hh * T + n * GL_C, d_ * NC + hh * T + (n + 1) * GL_C)
                    m = mm("gla_scores", pa[b0:b0 + GL_C, d_, hh, n // 2], k_in.t[:, at_], q_in.t[:, at_], t_in, p.free)
        give(k_in, m)
        S = yield from take_some(2)
        Sv = [b.t[:, 0:3 * GL_DV].rearrange("p (n v) -> p n v", n=3) for b in S]
        Av = [b.t[:, 3 * GL_DV:BLK].rearrange("p (g c) -> p g c", c=GL_C) for b in S]
        x = [tt(dve, "gla_masked", Av[d_], p.t[:, d_ * 256:(d_ + 1) * 256].rearrange("p (g c) -> p g c", c=GL_C),
                over((MASKF, MASKB)[d_], 1, 2 * NT), ALU.mult, m, S[d_].free) for d_ in range(2)]
        done_with(p, x)
        t_A = tt(dve, "gla_masked", Av[0], Av[0], Av[1], ALU.add, x)
        yield True
        ke = yield from take()
        kev = ke.t.rearrange("p (d h t k) -> p d h t k", d=2, h=2, t=NT)
        t_k = []
        for d_ in range(2):
            p = yield from bank()
            for hh in range(2):
                for i in range(NT):
                    m = turn("gla_k_end", p.t[:, (hh * NT + i) * P:(hh * NT + i + 1) * P],
                             kend.t[:, d_ * NC + hh * T + i * P:d_ * NC + hh * T + (i + 1) * P], t_ke, p.free)
            t_k.append(copy(act, "gla_k_end", ke.t[:, d_ * NC:(d_ + 1) * NC], p.t[:, :], m, ke.free))
            done_with(p, t_k)
            yield True
        give(kend, m)
        pos = []
        ssq = small(2 * NT).rearrange("p (h t) -> p h t", t=NT)
        go = yield from take()
        for i in range(NT):
            pos.append((yield from bank()))
        m_o = None
        for hh in range(2):
            t_S = [[None] * 3, [None] * 3]
            for z in range(3):
                for d_, n in ((0, z), (1, NCH - 1 - z)):
                    b0 = (n % 2) * GL_C
                    p = yield from bank()
                    m = mm("gla_state", p.t[:, 0:GL_DV], kev[b0:b0 + GL_C, d_, hh, n // 2],
                           v.t[b0:b0 + GL_C, (n // 2) * NC + hh * GL_DV:(n // 2) * NC + (hh + 1) * GL_DV], t_k, tv, p.free)
                    if z == 0:
                        e = copy(dve, "gla_state", Sv[d_][:, 0], p.t[:, 0:GL_DV], m, S[d_].free)
                    else:
                        e = stt("gla_state", Sv[d_][:, z], Sv[d_][:, z - 1], dec[:, d_, hh, n:n + 1], p.t[:, 0:GL_DV],
                                ALU.mult, ALU.add, m, t_S[d_][z - 1], t_dec, S[d_].free)
                    done_with(p, e)
                    t_S[d_][z] = e
                yield True
            for n in range(NCH):
                b0 = (n % 2) * GL_C
                o = pos[n // 2].t[b0:b0 + GL_C, hh * GL_DV:(hh + 1) * GL_DV]
                fr = pos[n // 2].free
                terms = [(Av[0][b0:b0 + GL_C, hh * NT + n // 2, :],
                          v.t[b0:b0 + GL_C, (n // 2) * NC + hh * GL_DV:(n // 2) * NC + (hh + 1) * GL_DV])]
                at_ = lambda d_: slice(d_ * NC + hh * T + n * GL_C, d_ * NC + hh * T + (n + 1) * GL_C)
                if n > 0:
                    terms.append((q_in.t[:, at_(0)], Sv[0][:, n - 1]))
                if n < NCH - 1:
                    terms.append((q_in.t[:, at_(1)], Sv[1][:, NCH - 2 - n]))
                for z, (l, r) in enumerate(terms):
                    m_o = mm("gla_o", o, l, r, t_A, t_S, fr, start=z == 0, stop=z == len(terms) - 1)
            S[0].free, S[1].free = [m_o], [m_o]
            yield True
        for b in (ke, q_in, v, *S):
            give(b, m_o)
        for i in range(NT):
            for hh in range(2):
                x = func("gla_square", ACT.Square, go.t[:, 0:GL_DV], pos[i].t[:, hh * GL_DV:(hh + 1) * GL_DV], m_o,
                         go.free, accum_out=ssq[:, hh, i:i + 1])
                go.free = [x]
        rr = small(2 * NT).rearrange("p (h t) -> p h t", t=NT)
        e = rsqrt("gla_rsqrt", rr.rearrange("p h t -> p (h t)"), ssq.rearrange("p h t -> p (h t)"), 1.0 / GL_DV, x)
        e = tt(dve, "gla_factor", rr, rr, over(scales["u2"][1], 1, 2), ALU.mult, e, scales["u2"][2])
        yield True
        (g, tg), = yield from need(f"gr{hp}")
        for i in range(NT):
            for hh in range(2):
                s = slice(i * NC + hh * GL_DV, i * NC + (hh + 1) * GL_DV)
                e2 = stt("gla_gated", go.t[:, s], pos[i].t[:, hh * GL_DV:(hh + 1) * GL_DV], rr[:, hh, i:i + 1],
                         g.t[:, s], ALU.mult, ALU.mult, e, tg, x)
            done_with(pos[i], e2)
        give(g, e2)
        yield True
        th = []
        for c in range(0, 4, 2):
            p = yield from bank()
            for cc in range(2):
                for i in range(NT):
                    m = turn("gla_out", p.t[:, cc * T + i * P:cc * T + (i + 1) * P],
                             go.t[:, i * NC + (c + cc) * P:i * NC + (c + cc + 1) * P], e2, p.free)
            for cc in range(2):
                k = hp * 4 + c + cc
                th.append(copy(act, "gla_out", acts[:, 8 + k, :], p.t[:, cc * T:(cc + 1) * T], m, acts_free,
                               scale=wcol[:, W_GLA + k:W_GLA + k + 1]))
            done_with(p, th)
            yield True
        give(go, m)
        at_ready[2 + hp] = th

    def j2(c0, done, n=NC):
        jobs.append(product(w2, c0, done, "u2", n))

    j2(C_GQ, keep("gq", "u2"))
    j2(C_GL, gla_gates, 2 * GL_R)
    j2(C_GK, keep("gk", "u2"))
    j2(C_GV, keep("gv0", "u2", then=lambda: gla(0)))
    j2(C_GR, keep_silu2("gr0", "u2"))
    j2(C_AQ, keep("aq0", "u2"))
    j2(C_AK, keep("ak0", "u2"))
    j2(C_AV, keep("av0", "u2", then=lambda: attention(0)))
    j2(C_AQ + NC, keep("aq1", "u2"))
    j2(C_AK + NC, keep("ak1", "u2"))
    j2(C_AV + NC, keep("av1", "u2", then=lambda: attention(1)))
    j2(C_GV + NC, keep("gv1", "u2", then=lambda: gla(1)))
    j2(C_GR + NC, keep_silu2("gr1", "u2"))

    acc3 = small(NT * (D // NC)).rearrange("p (t n) -> p t n", t=NT)
    acc4 = small(NT * (D // NC)).rearrange("p (t n) -> p t n", t=NT)
    sums3, sums4, resid_done = [], [], {}

    def add_resid(n, acc, sums):
        def done(pair, t):
            if n not in resid:
                b = yield from take(but=tail)
                resid[n] = (b, [load(f"x2_load{n}", b.t.rearrange("p (t n) -> p t n", t=NT),
                                     x2_dram[:, :, n * NC:(n + 1) * NC], b.free, kept[n])])
            b, tb = resid[n]
            es = []
            for i in range(NT):
                s = slice(i * NC, (i + 1) * NC)
                es.append(tt(dve, "resid", b.t[:, s], b.t[:, s], pair.t[i][:, :], ALU.add, t, tb))
            e = es[-1]
            pair.free = [e]
            if sums is sums4:
                resid_done[n] = (b, es)
                sums.append((yield from square_sums(n, b, acc, tiles=es)))
                return
            yield True
            sums.append((yield from square_sums(n, b, acc, tiles=es)))
            yield True
            turned = (yield from turn_block("u3", "u2", n, b, W_FFN, e)) if sums is sums3 else None
            resid[n] = (b, [e, turned])
        return done

    for n in range(D // NC):
        jobs.append(Job(columns(a["w_out_2"][0], n * NC), [0, 2, 1, 3], NC, add_resid(n, acc3, sums3),
                        split=lambda k: acts[:, k:k + 2, :], ready=lambda k: at_ready.get(k // 4)))

    def third_norm():
        while len(sums3) < D // NC:
            yield False
        acts_free[:] = [state["last"]]
        r, t = norm_scale(acc3, sums3)
        set_scale("u3", r, t)
        sq = small(NT)
        scales["u3 act"] = (sq, ts("norm_square", sq, scales["u3"][1], 0.0, ALU.add, None, None, scales["u3"][2]))
        t = tt(dve, "norm_square", sq, sq, r, ALU.mult, scales["u3 act"][1])
        scales["u3 act"] = (sq, t)
        got_tail = []
        for b in tail:
            while b not in free_blocks:
                yield False
            free_blocks.remove(b)
            got_tail.append(b.free)
        acts_free.append(got_tail)
        state["tail"] = True

    ffn_ready = {}

    def ffn_up(n):
        def done(pair, t):
            while "u3 act" not in scales:
                yield False
            (g, tg), = yield from need(f"fg{n}")
            for i in range(NT):
                s = slice(i * NC, (i + 1) * NC)
                e = stt("ffn_act", g.t[:, s], g.t[:, s], scales["u3 act"][0][:, i:i + 1], pair.t[i][:, :], ALU.mult,
                        ALU.mult, t, tg, scales["u3 act"][1])
            pair.free = [e]
            yield True
            while "tail" not in state:
                yield False
            th = []
            for c in range(0, 4, 2):
                p = yield from bank()
                for cc in range(2):
                    for i in range(NT):
                        m = turn("ffn_act", p.t[:, cc * T + i * P:cc * T + (i + 1) * P],
                                 g.t[:, i * NC + (c + cc) * P:i * NC + (c + cc + 1) * P], e, p.free)
                k = 4 * n + c
                th.append(copy((act, dve)[c // 2], "ffn_act", acts_all[:, k:k + 2, :],
                               p.t[:, :].rearrange("p (c t) -> p c t", c=2), m, acts_free))
                done_with(p, th[-1])
                yield True
            give(g, m)
            ffn_ready[n] = th
        return done

    for n in range(FFN // NC):
        jobs.append(product(a["w_gate_2"][0], n * NC, keep_silu2(f"fg{n}", "u3"), "u3"))
        jobs.append(product(a["w_up_2"][0], n * NC, ffn_up(n), "u3"))
    for n in range(D // NC):
        jobs.append(Job(columns(a["w_down_2"][0], n * NC), list(range(KF // CH)), NC, add_resid(n, acc4, sums4),
                        split=lambda k: acts_all[:, k:k + 2, :], ready=lambda k: ffn_ready.get(k // 4)))

    def last_norm():
        while "tail" not in state:
            yield False
        final_w.clear()
        t_final.clear()
        yield from load_final_w("final_norm_w_2")
        wb, tw = final_w, t_final
        weighted = []
        ahead = D // NC - 1
        for n in range(ahead):
            while len(sums4) <= n:
                yield False
            b, tb = resid_done[n]
            e = tt(dve, "final_weight", b.t.rearrange("p (t n) -> p t n", t=NT), b.t.rearrange("p (t n) -> p t n", t=NT),
                   over(wb[n // 2].t[:, (n % 2) * NC:(n % 2 + 1) * NC], 1, NT), ALU.mult, tb, sums4[n], tw[n // 2])
            weighted.append(e)
        while len(sums4) <= ahead:
            yield False
        r, t = norm_scale(acc4, sums4)
        for n in range(D // NC):
            b, tb = resid_done[n]
            if n < ahead:
                e = [func("final", ACT.Copy, b.t[:, 0:NC], b.t[:, 0:NC], t, weighted[n], scale=r[:, 0:1]),
                     ts("final", b.t[:, NC:2 * NC], b.t[:, NC:2 * NC], r[:, 1:2], ALU.mult, None, None, t, weighted[n])]
            else:
                for i in range(NT):
                    s = slice(i * NC, (i + 1) * NC)
                    e = stt("final", b.t[:, s], b.t[:, s], r[:, i:i + 1], wb[n // 2].t[:, (n % 2) * NC:(n % 2 + 1) * NC],
                            ALU.mult, ALU.mult, tb, t, tw[n // 2])
            stored.append(load(f"store{n}", out[0, :, n * NC:(n + 1) * NC].rearrange("(t p) n -> p t n", p=P),
                               b.t.rearrange("p (t n) -> p t n", t=NT), e, q=sp))

    stored = []

    def background():
        while len(resid) < 1:
            yield False
        yield from load_final_w("final_norm_w")
        yield from second_norm()
        state["last_first"] = state["last"]
        yield from second_constants()
        yield from third_norm()
        yield from last_norm()

    def beside():
        g = background()
        while True:
            try:
                r = next(g)
            except StopIteration:
                return
            yield r

    urgent.append(beside())
    run_jobs(jobs)
    settle(lambda: len(stored) == D // NC and not gens)

    block = ctx.enter_context(nc.Block())

    @block.sync
    def _(e):
        sp.play(e)
        for t in stored:
            e.wait_ge(t.sem, t.value)

    @block.tensor
    def _(e):
        pe.play(e)

    @block.scalar
    def _(e):
        act.play(e)

    @block.vector
    def _(e):
        dve.play(e)

    @block.gpsimd
    def _(e):
        pool.play(e)


_INS = ["x", "norm_w", "w_in", "ml_i_bias", "ml_f_bias", "ml_norm_w", "dn_conv_w", "dn_a_log", "dn_dt_bias",
        "dn_norm_w", "w_out", "final_norm_w", "attn_norm_w_2", "w_in_2", "rel_bias_table_2", "gla_gate_w_fwd_2",
        "gla_gate_b_fwd_2", "gla_gate_w_bwd_2", "gla_gate_b_bwd_2", "gla_norm_w_2", "w_out_2", "ffn_norm_w_2",
        "w_gate_2", "w_up_2", "w_down_2", "final_norm_w_2"]


def kernel(**inputs):
    import numpy as _np
    import concourse.bacc as _bacc
    from concourse import mybir as _mybir
    from concourse.bass_utils import run_bass_kernel_spmd as _run

    nc = _bacc.Bacc("TRN2", target_bir_lowering=False, num_devices=1)
    given = {n: inputs[n] for n in _INS}
    given.update(host_constants())
    arrays, args = {}, {}
    for name, value in given.items():
        v = _np.ascontiguousarray(value)
        arrays[f"in_{name}_dram"] = v
        args[name] = nc.dram_tensor(f"in_{name}_dram", v.shape, _mybir.dt.from_np(v.dtype), kind="ExternalInput").ap()
    out = nc.dram_tensor("out_0_dram", (1, T, D), _mybir.dt.float32, kind="ExternalOutput").ap()
    build(nc, args, out)
    r = _run(nc, [arrays], core_ids=[0])
    return r.results[0]["out_0_dram"]
```
